# Optimizing a Trainium2 kernel written in Bass

```python
import jax, jax.numpy as jnp
from jax import lax
import numpy as np

D_MODEL = 1024
BATCH = 1
SEQ = 1024
DEPTH = 2
DEC_BATCH = 8
DEC_SEQ = 16
PAST_LEN = 512

CHUNK = 64
META = 16
N_A_LAYERS = DEPTH // 2
N_B_LAYERS = DEPTH - N_A_LAYERS
A_HEADS = 4
A_DQK = D_MODEL // (2 * A_HEADS)
A_DV = D_MODEL // A_HEADS
A_QK = A_HEADS * A_DQK
A_V = A_HEADS * A_DV
A_IN = 2 * A_QK + 2 * A_V + 2 * A_HEADS
B_HEAD_DIM = 64
B_Q_HEADS = D_MODEL // B_HEAD_DIM
B_KV_HEADS = 4
B_GROUP = B_Q_HEADS // B_KV_HEADS
WINDOW = 128
WINDOW_CHUNKS = WINDOW // CHUNK
ROPE_THETA = 10000.0
D_FF = -(-8 * D_MODEL // (3 * 256)) * 256
EPS = 1e-6
F_BIAS_LO = 3.0
F_BIAS_HI = 6.0

kernel_name = 'yoco_mlstm_swa_sink_stream_step'

def rmsnorm(x, g):
    xf = x.astype(jnp.float32)
    y = xf * lax.rsqrt(jnp.mean(xf * xf, axis=-1, keepdims=True) + EPS)
    return (y * g.astype(jnp.float32)).astype(x.dtype)

def rope(x, pos):
    half = x.shape[-1] // 2
    inv = ROPE_THETA ** (-jnp.arange(half, dtype=jnp.float32) / half)
    ang = pos.astype(jnp.float32)[:, None] * inv[None, :]
    cos = jnp.cos(ang)[:, None, :]
    sin = jnp.sin(ang)[:, None, :]
    xf = x.astype(jnp.float32)
    x1, x2 = xf[..., :half], xf[..., half:]
    return jnp.concatenate([x1 * cos - x2 * sin, x2 * cos + x1 * sin], axis=-1).astype(x.dtype)

def swiglu(x, w_gu, w_dn):
    g, u = jnp.split(x @ w_gu, 2, axis=-1)
    return (jax.nn.silu(g) * u) @ w_dn

def mlstm_project(xn, w_in, b_gate):
    B, S, _ = xn.shape
    p = xn @ w_in
    q, k, v, o, gates = jnp.split(p, [A_QK, 2 * A_QK, 2 * A_QK + A_V, 2 * A_QK + 2 * A_V], axis=-1)
    heads = lambda a, d: a.reshape(B, S, A_HEADS, d).transpose(0, 2, 1, 3)
    gates = (gates.astype(jnp.float32) + b_gate.astype(jnp.float32)).transpose(0, 2, 1)
    logi = gates[:, :A_HEADS]
    logf = jax.nn.log_sigmoid(gates[:, A_HEADS:])
    return heads(q, A_DQK), heads(k, A_DQK), heads(v, A_DV), o, logi, logf

def mlstm_chunk(state, q, k, v, logi, logf):
    c, n, m = state
    L = q.shape[2]
    qf = q.astype(jnp.float32) * (A_DQK ** -0.5)
    kf = k.astype(jnp.float32)
    vf = v.astype(jnp.float32)
    b = jnp.cumsum(logf, axis=-1)
    causal = jnp.tril(jnp.ones((L, L), dtype=bool))
    dmat = jnp.where(causal, b[..., :, None] - b[..., None, :] + logi[..., None, :], -jnp.inf)
    m_inter = b + m[..., None]
    m_t = jnp.maximum(m_inter, jnp.max(dmat, axis=-1))
    w = jnp.exp(dmat - m_t[..., None])
    s_in = jnp.exp(m_inter - m_t)
    qk = jnp.einsum('bhtd,bhsd->bhts', qf, kf) * w
    num = jnp.einsum('bhts,bhse->bhte', qk, vf) + s_in[..., None] * jnp.einsum('bhtd,bhde->bhte', qf, c)
    den = jnp.sum(qk, axis=-1) + s_in * jnp.einsum('bhtd,bhd->bht', qf, n)
    h = num / jnp.maximum(jnp.abs(den), jnp.exp(-m_t))[..., None]
    m_new = m_t[..., -1]
    wl = jnp.exp(b[..., -1:] - b + logi - m_new[..., None])
    decay = jnp.exp(b[..., -1] + m - m_new)
    c_new = decay[..., None, None] * c + jnp.einsum('bhs,bhsd,bhse->bhde', wl, kf, vf)
    n_new = decay[..., None] * n + jnp.einsum('bhs,bhsd->bhd', wl, kf)
    return (c_new, n_new, m_new), h

def mlstm_scan_chunks(state, q, k, v, logi, logf):
    B, H, S = q.shape[:3]
    nc = S // CHUNK
    def to_chunks(a):
        return jnp.moveaxis(a.reshape((B, H, nc, CHUNK) + a.shape[3:]), 2, 0)
    xs = tuple(to_chunks(a) for a in (q, k, v, logi, logf))
    state, hs = lax.scan(lambda st, inp: mlstm_chunk(st, *inp), state, xs)
    return state, jnp.moveaxis(hs, 0, 2).reshape(B, H, S, A_DV)

def mlstm_out(h, o, g_head, w_out):
    B, H, S, _ = h.shape
    hn = h * lax.rsqrt(jnp.mean(h * h, axis=-1, keepdims=True) + EPS)
    hn = hn.transpose(0, 2, 1, 3).reshape(B, S, A_V) * g_head.astype(jnp.float32)
    return (jax.nn.sigmoid(o.astype(jnp.float32)) * hn).astype(o.dtype) @ w_out

def mlstm_layer_prompt(xn, w_in, b_gate, g_head, w_out):
    B = xn.shape[0]
    q, k, v, o, logi, logf = mlstm_project(xn, w_in, b_gate)
    st = (jnp.zeros((B, A_HEADS, A_DQK, A_DV), jnp.float32),
          jnp.zeros((B, A_HEADS, A_DQK), jnp.float32),
          jnp.zeros((B, A_HEADS), jnp.float32))
    st, h_meta = mlstm_chunk(st, *(a[:, :, :META] for a in (q, k, v, logi, logf)))
    st, h_real = mlstm_scan_chunks(st, *(a[:, :, META:] for a in (q, k, v, logi, logf)))
    return mlstm_out(jnp.concatenate([h_meta, h_real], axis=2), o, g_head, w_out), st

def mlstm_layer_sample(xn, st, w_in, b_gate, g_head, w_out):
    q, k, v, o, logi, logf = mlstm_project(xn, w_in, b_gate)
    st, h = mlstm_chunk(st, q, k, v, logi, logf)
    return mlstm_out(h, o, g_head, w_out), st

def shared_kv(h, g_kv, w_kv, pos):
    B, S, _ = h.shape
    kv = (rmsnorm(h, g_kv) @ w_kv).reshape(B, S, 2, B_KV_HEADS, B_HEAD_DIM)
    return rope(kv[:, :, 0], pos), kv[:, :, 1]

def sink_softmax(s_meta, s_loc, mask, sinks_r):
    s_loc = jnp.where(mask, s_loc, -jnp.inf)
    sink = jnp.broadcast_to(sinks_r, s_meta.shape[:-1] + (1,))
    p = jax.nn.softmax(jnp.concatenate([s_meta, s_loc, sink], axis=-1), axis=-1)
    return p[..., :META], p[..., META:-1]

def swa_prompt(xn, w_q, sinks, w_o, k_meta, v_meta, k_real, v_real):
    B, S, _ = xn.shape
    nc = S // CHUNK
    q = rope((xn @ w_q).reshape(B, S, B_Q_HEADS, B_HEAD_DIM), META + jnp.arange(S))
    q = q.reshape(B, nc, CHUNK, B_KV_HEADS, B_GROUP, B_HEAD_DIM)
    pad = ((0, 0), ((WINDOW_CHUNKS - 1) * CHUNK, 0), (0, 0), (0, 0))
    def band(a):
        a = jnp.pad(a, pad).reshape(B, nc + WINDOW_CHUNKS - 1, CHUNK, B_KV_HEADS, B_HEAD_DIM)
        return jnp.concatenate([a[:, i:i + nc] for i in range(WINDOW_CHUNKS)], axis=2)
    kb, vb = band(k_real), band(v_real)
    slot_chunk = jnp.arange(nc)[:, None] - (WINDOW_CHUNKS - 1) + jnp.arange(WINDOW)[None, :] // CHUNK
    mask = (slot_chunk >= 0)[:, None, :]
    scale = B_HEAD_DIM ** -0.5
    s_meta = jnp.einsum('bnqkgd,bjkd->bkgnqj', q, k_meta).astype(jnp.float32) * scale
    s_loc = jnp.einsum('bnqkgd,bnjkd->bkgnqj', q, kb).astype(jnp.float32) * scale
    sinks_r = sinks.astype(jnp.float32).reshape(1, B_KV_HEADS, B_GROUP, 1, 1, 1)
    p_meta, p_loc = sink_softmax(s_meta, s_loc, mask, sinks_r)
    out = (jnp.einsum('bkgnqj,bjkd->bnqkgd', p_meta, v_meta.astype(jnp.float32))
           + jnp.einsum('bkgnqj,bnjkd->bnqkgd', p_loc, vb.astype(jnp.float32)))
    return out.reshape(B, S, B_Q_HEADS * B_HEAD_DIM).astype(xn.dtype) @ w_o

def swa_sample(xn, w_q, sinks, w_o, k_meta, v_meta, k_loc, v_loc):
    B, T, _ = xn.shape
    q = rope((xn @ w_q).reshape(B, T, B_Q_HEADS, B_HEAD_DIM), META + PAST_LEN + jnp.arange(T))
    q = q.reshape(B, T, B_KV_HEADS, B_GROUP, B_HEAD_DIM)
    kpos = PAST_LEN - WINDOW + jnp.arange(WINDOW + T)
    qpos = PAST_LEN + jnp.arange(T)
    kc = kpos // CHUNK
    qc = qpos // CHUNK
    mask = (kpos[None, :] >= 0) & (kc[None, :] <= qc[:, None]) & (kc[None, :] > qc[:, None] - WINDOW_CHUNKS)
    scale = B_HEAD_DIM ** -0.5
    s_meta = jnp.einsum('btkgd,bjkd->bkgtj', q, k_meta).astype(jnp.float32) * scale
    s_loc = jnp.einsum('btkgd,bjkd->bkgtj', q, k_loc).astype(jnp.float32) * scale
    sinks_r = sinks.astype(jnp.float32).reshape(1, B_KV_HEADS, B_GROUP, 1, 1)
    p_meta, p_loc = sink_softmax(s_meta, s_loc, mask, sinks_r)
    out = (jnp.einsum('bkgtj,bjkd->btkgd', p_meta, v_meta.astype(jnp.float32))
           + jnp.einsum('bkgtj,bjkd->btkgd', p_loc, v_loc.astype(jnp.float32)))
    return out.reshape(B, T, B_Q_HEADS * B_HEAD_DIM).astype(xn.dtype) @ w_o

def prompt_path(x, meta_tokens, norm_mix, norm_ffn, w_gate_up, w_down, a_w_in, a_b_gate, a_g_head,
                a_w_out, g_kv, w_kv, b_w_q, b_sinks, b_w_o, g_final):
    B, S, _ = x.shape
    h = jnp.concatenate([jnp.broadcast_to(meta_tokens.astype(x.dtype)[None], (B, META, D_MODEL)), x], axis=1)
    states = []
    for l in range(DEPTH):
        if l < N_A_LAYERS:
            y, st = mlstm_layer_prompt(rmsnorm(h, norm_mix[l]), a_w_in[l], a_b_gate[l], a_g_head[l], a_w_out[l])
            states.append(st)
            h = h + y
        else:
            j = l - N_A_LAYERS
            h = h + swa_prompt(rmsnorm(h, norm_mix[l]), b_w_q[j], b_sinks[j], b_w_o[j],
                               k_meta, v_meta, k_real, v_real)
        h = h + swiglu(rmsnorm(h, norm_ffn[l]), w_gate_up[l], w_down[l])
        if l == N_A_LAYERS - 1:
            k_all, v_all = shared_kv(h, g_kv, w_kv, jnp.arange(META + S))
            k_meta, v_meta = k_all[:, :META], v_all[:, :META]
            k_real, v_real = k_all[:, META:], v_all[:, META:]
            h = h[:, META:]
    y = rmsnorm(h, g_final)
    c = jnp.stack([s[0] for s in states], axis=1)
    n = jnp.stack([s[1] for s in states], axis=1)
    m = jnp.stack([s[2] for s in states], axis=1)
    return y, c, n, m, k_meta, v_meta, k_real[:, -WINDOW:], v_real[:, -WINDOW:]

def sample_path(x, state_c, state_n, state_m, cache_meta_k, cache_meta_v, cache_win_k, cache_win_v,
                norm_mix, norm_ffn, w_gate_up, w_down, a_w_in, a_b_gate, a_g_head, a_w_out,
                g_kv, w_kv, b_w_q, b_sinks, b_w_o, g_final):
    B, T, _ = x.shape
    h = x
    states = []
    for l in range(DEPTH):
        if l < N_A_LAYERS:
            st = (state_c[:, l].astype(jnp.float32), state_n[:, l].astype(jnp.float32),
                  state_m[:, l].astype(jnp.float32))
            y, st = mlstm_layer_sample(rmsnorm(h, norm_mix[l]), st, a_w_in[l], a_b_gate[l], a_g_head[l], a_w_out[l])
            states.append(st)
            h = h + y
        else:
            j = l - N_A_LAYERS
            h = h + swa_sample(rmsnorm(h, norm_mix[l]), b_w_q[j], b_sinks[j], b_w_o[j],
                               cache_meta_k, cache_meta_v, k_loc, v_loc)
        h = h + swiglu(rmsnorm(h, norm_ffn[l]), w_gate_up[l], w_down[l])
        if l == N_A_LAYERS - 1:
            k_new, v_new = shared_kv(h, g_kv, w_kv, META + PAST_LEN + jnp.arange(T))
            k_loc = jnp.concatenate([cache_win_k.astype(k_new.dtype), k_new], axis=1)
            v_loc = jnp.concatenate([cache_win_v.astype(v_new.dtype), v_new], axis=1)
    y = rmsnorm(h, g_final)
    c = jnp.stack([s[0] for s in states], axis=1)
    n = jnp.stack([s[1] for s in states], axis=1)
    m = jnp.stack([s[2] for s in states], axis=1)
    return y, c, n, m, k_loc[:, -WINDOW:], v_loc[:, -WINDOW:]

def setup_inputs(seed: int = 0) -> dict:
    key = jax.random.key(seed)
    ks = jax.random.split(key, 32)
    nrm = lambda k, shape, s: jax.random.normal(k, shape, jnp.float32) * s
    gain = lambda k, shape: 1.0 + 0.02 * jax.random.normal(k, shape, jnp.float32)
    f_bias = jnp.linspace(F_BIAS_LO, F_BIAS_HI, A_HEADS, dtype=jnp.float32)[None, :]
    a_b_gate = jnp.concatenate([nrm(ks[20], (N_A_LAYERS, A_HEADS), 0.1),
                                f_bias + nrm(ks[21], (N_A_LAYERS, A_HEADS), 0.1)], axis=-1)
    return {
        'x_prompt': nrm(ks[0], (BATCH, SEQ, D_MODEL), 1.0),
        'x_sample': nrm(ks[1], (DEC_BATCH, DEC_SEQ, D_MODEL), 1.0),
        'state_c': nrm(ks[2], (DEC_BATCH, N_A_LAYERS, A_HEADS, A_DQK, A_DV), 0.1),
        'state_n': nrm(ks[3], (DEC_BATCH, N_A_LAYERS, A_HEADS, A_DQK), 0.5),
        'state_m': nrm(ks[4], (DEC_BATCH, N_A_LAYERS, A_HEADS), 0.5),
        'cache_meta_k': nrm(ks[5], (DEC_BATCH, META, B_KV_HEADS, B_HEAD_DIM), 1.0),
        'cache_meta_v': nrm(ks[6], (DEC_BATCH, META, B_KV_HEADS, B_HEAD_DIM), 1.0),
        'cache_win_k': nrm(ks[7], (DEC_BATCH, WINDOW, B_KV_HEADS, B_HEAD_DIM), 1.0),
        'cache_win_v': nrm(ks[8], (DEC_BATCH, WINDOW, B_KV_HEADS, B_HEAD_DIM), 1.0),
        'meta_tokens': nrm(ks[9], (META, D_MODEL), 1.0),
        'norm_mix': gain(ks[10], (DEPTH, D_MODEL)),
        'norm_ffn': gain(ks[11], (DEPTH, D_MODEL)),
        'w_gate_up': nrm(ks[12], (DEPTH, D_MODEL, 2 * D_FF), D_MODEL ** -0.5),
        'w_down': nrm(ks[13], (DEPTH, D_FF, D_MODEL), D_FF ** -0.5),
        'a_w_in': nrm(ks[14], (N_A_LAYERS, D_MODEL, A_IN), D_MODEL ** -0.5),
        'a_b_gate': a_b_gate,
        'a_g_head': gain(ks[15], (N_A_LAYERS, A_V)),
        'a_w_out': nrm(ks[16], (N_A_LAYERS, A_V, D_MODEL), A_V ** -0.5),
        'g_kv': gain(ks[17], (D_MODEL,)),
        'w_kv': nrm(ks[18], (D_MODEL, 2 * B_KV_HEADS * B_HEAD_DIM), D_MODEL ** -0.5),
        'b_w_q': nrm(ks[19], (N_B_LAYERS, D_MODEL, B_Q_HEADS * B_HEAD_DIM), D_MODEL ** -0.5),
        'b_sinks': nrm(ks[22], (N_B_LAYERS, B_Q_HEADS), 0.5),
        'b_w_o': nrm(ks[23], (N_B_LAYERS, B_Q_HEADS * B_HEAD_DIM, D_MODEL), (B_Q_HEADS * B_HEAD_DIM) ** -0.5),
        'g_final': gain(ks[24], (D_MODEL,)),
    }

def reference(x_prompt, x_sample, state_c, state_n, state_m, cache_meta_k, cache_meta_v, cache_win_k,
              cache_win_v, meta_tokens, norm_mix, norm_ffn, w_gate_up, w_down, a_w_in, a_b_gate, a_g_head,
              a_w_out, g_kv, w_kv, b_w_q, b_sinks, b_w_o, g_final):
    y_p, c_p, n_p, m_p, mk_p, mv_p, wk_p, wv_p = prompt_path(
        x_prompt, meta_tokens, norm_mix, norm_ffn, w_gate_up, w_down, a_w_in, a_b_gate, a_g_head,
        a_w_out, g_kv, w_kv, b_w_q, b_sinks, b_w_o, g_final)
    y_s, c_s, n_s, m_s, wk_s, wv_s = sample_path(
        x_sample, state_c, state_n, state_m, cache_meta_k, cache_meta_v, cache_win_k, cache_win_v,
        norm_mix, norm_ffn, w_gate_up, w_down, a_w_in, a_b_gate, a_g_head, a_w_out,
        g_kv, w_kv, b_w_q, b_sinks, b_w_o, g_final)
    return (y_p, y_s, c_p, n_p, m_p, mk_p, mv_p, wk_p, wv_p, c_s, n_s, m_s, wk_s, wv_s)


_drawn_inputs = setup_inputs


def setup_inputs(seed=0):
    import zlib

    import numpy as np

    out = dict(_drawn_inputs(seed))
    spreads = {}
    factors = {'norm_ffn': 3.058,
     'a_g_head': 4.907,
     'g_kv': 8.095,
     'b_sinks': 25.877,
     'g_final': 8.077,
     'cache_meta_k': 8.0,
     'cache_meta_v': 8.0}
    for name, (base, spread) in spreads.items():
        noise = np.random.default_rng([zlib.crc32(name.encode()), seed]).standard_normal(out[name].shape)
        drawn = base * np.exp(spread * noise) if base else spread * noise
        out[name] = __import__('jax').numpy.asarray(drawn.astype(out[name].dtype))
    for name, factor in factors.items():
        out[name] = (out[name] * factor).astype(out[name].dtype)
    return out
```

```python
from contextlib import ExitStack

import numpy as np

import concourse.bass as bass
from concourse import mybir
from concourse.alu_op_type import AluOpType as ALU

F32 = mybir.dt.float32
F32R = mybir.dt.float32r
ACT = mybir.ActivationFunctionType
AX_X = mybir.AxisListType.X
ds = bass.ds

P = 128
D = 1024
KD = D // P
META, SEQ, NB, TS = 16, 1024, 8, 16
NS = NB * TS
T = META + SEQ + NS
T_S = META + SEQ
TOK = [(0, 400), (400, 384), (784, 384)]
HA, DQK, DV = 4, 128, 256
QSCALE = DQK ** -0.5
DFF = 2816
HD, KVH = 64, 4
CHUNK, WINDOW, PAST = 64, 128, 512
EPS = 1e-6
SCORE_SCALE = HD ** -0.5
MCH = 128
NMC = SEQ // MCH


class Group:

    def __init__(self, n0, pairs, weight, gain, kind):
        self.n0, self.pairs, self.weight, self.gain, self.kind = n0, pairs, weight, gain, kind


def over(eng, groups, body):
    for g in groups:
        if g.pairs == 1:
            for u in range(2):
                body(g, u, g.n0 + u, u, g.n0 // 2)
        else:
            with eng.Fori(0, g.pairs) as i:
                for u in range(2):
                    body(g, 2 * i + u, g.n0 + 2 * i + u, u, i + g.n0 // 2)


def build(nc, a, upto=99):
    ctx = ExitStack()
    with ctx:
        _build(nc, a, ctx, upto)


def _build(nc, a, ctx, upto):
    base = [(nc.sbuf_base + 31) // 32 * 32]
    limit = nc.sbuf_usable_end

    def at(name, shape, dt=F32, offset=0):
        n = int(np.prod(shape[1:])) * 4
        assert offset + n <= limit, (name, offset + n, limit)
        return nc.alloc_sbuf_tensor_at(name, shape, dt, offset=offset), offset + (n + 31) // 32 * 32

    def sb(name, shape, dt=F32):
        t, base[0] = at(name, shape, dt, base[0])
        return t

    phase = [None]

    def sem(name):
        phase[0].append(nc.alloc_semaphore(name))
        return phase[0][-1]

    def run(step, *args, **kw):
        phase[0] = []
        step(*args, **kw)
        nc.clear_and_free_semaphores(phase[0])
        nc.all_engine_barrier()

    def dram(name, shape):
        return nc.dram_tensor(name, shape, F32, kind="Internal").ap()

    h = sb("h", [P, KD, T])
    rstd = sb("rstd", [P, T])
    ident = sb("ident", [P, P])
    ones = sb("ones", [P, P])
    gains = sb("gains", [P, 6, KD])
    epsc = sb("epsc", [P, 1])
    fixed_end = base[0]

    xh = sb("xh", [P, KD, T], F32R)
    xl = sb("xl", [P, KD, T], F32R)
    x_end = base[0]
    raw = sb("raw", [P, 2, D])
    wh = sb("wh", [P, 3, D], F32R)
    wl = sb("wl", [P, 3, D], F32R)
    sq_at = base[0]
    sq = sb("sq", [P, 2, T])
    acc = sb("acc", [P, T])
    dense_end = base[0]
    tmp, e1 = at("tmp", [P, 2, T], F32, dense_end)
    swp, e2 = at("swp", [P, T], F32, e1)
    hidh, e1b = at("hidh", [P, 2, T], F32R, dense_end)
    hidl, e2b = at("hidl", [P, 2, T], F32R, e1b)
    cosr, e3 = at("cosr", [P, T], F32, e2)
    sinr, e4 = at("sinr", [P, T], F32, e3)
    gate, up_at = at("gate", [P, T], F32, sq_at)
    up, _ = at("up", [P, T], F32, up_at)

    qkvo = dram("qkvo", (24, P, T))
    gates_d = dram("gates_d", (2, 4, T))
    og_d = dram("og_d", (KD, P, T))
    k2_d = dram("k2_d", (KVH, P, T))
    vt_d = dram("vt_d", (2, P, T))
    qr_d = dram("qr_d", (KD, P, T))

    psum = ctx.enter_context(nc.psum_tensor("psum", [P, 8, 512], F32))

    unit = ones[:, 0:1].to_broadcast([P, D])

    def wcols(w, col0=0):
        v = w.rearrange("(k p) n -> p k n", p=P)
        return lambda j: v[:, :, ds(j * P + col0, P)]

    def weight_tile(b):
        return b.rearrange("p (k n) -> p k n", k=KD)

    def setup():
        xin, e = at("xin", [P, 10, D], F32, x_end)
        identw = sem("su_ident")
        const = sem("su_const")
        loads = [sem(f"su_x{i}") for i in range(2)]
        gl = sem("su_gains")
        copies = sem("su_cache_copies")
        turned = sem("su_turned")
        placed = sem("su_placed")
        with nc.Block() as block:
            @block.sync
            def _(sp):
                for i in range(8):
                    sp.dma_start(xin[:, i, :], a["x_prompt"][0, i * P:(i + 1) * P, :]).then_inc(loads[0], 16)
                sp.dma_start(xin[:, 8, :], a["x_sample"].rearrange("b t d -> (b t) d")).then_inc(loads[0], 16)
                sp.dma_start(xin[0:META, 9, :], a["meta_tokens"]).then_inc(loads[0], 16)
                for w, c in (("win_k_s", "cache_win_k"), ("win_v_s", "cache_win_v")):
                    sp.dma_start(a[w][:, 0:WINDOW - TS], a[c][:, TS:WINDOW]).then_inc(copies, 16)
                sp.wait_ge(copies, 32)

            @block.scalar
            def _(act):
                for n, g in enumerate((a["norm_mix"][0], a["a_g_head"][0], a["norm_ffn"][0], a["g_kv"],
                                       a["norm_mix"][1], a["norm_ffn"][1])):
                    with nc.allow_non_contiguous_dma("gain columns"):
                        act.dma_start(gains[:, n, :], g.rearrange("(k p) -> p k", p=P)).then_inc(gl, 16)
                act.wait_ge(gl, 96)

            @block.gpsimd
            def _(pool):
                pool.memset(ident[:], 0.0).then_inc(identw, 1)
                pool.wait_ge(identw, 1)
                pool.affine_select(out=ident[:], in_=ident[:], compare_op=ALU.not_equal, fill=1.0, base=0,
                                   pattern=[[-1, P]], channel_multiplier=1).then_inc(const, 1)
                pool.memset(ones[:], 1.0).then_inc(const, 1)
                pool.memset(epsc[:], EPS).then_inc(const, 1)

            @block.tensor
            def _(pe):
                pe.wait_ge(const, 3)
                pe.wait_ge(loads[0], 160)
                for i in range(10):
                    n = META if i == 9 else P
                    for half in range(2):
                        u = 2 * i + half
                        if u >= 8:
                            pe.wait_ge(placed, u - 7)
                        for k in range(4):
                            t = pe.transpose(psum[:, u % 8, k * P:k * P + n],
                                             xin[0:n, i, (4 * half + k) * P:(4 * half + k + 1) * P], ident[0:n, 0:n])
                        t.then_inc(turned, 1)

            @block.vector
            def _(dve):
                for i in range(10):
                    n = META if i == 9 else P
                    col = 0 if i == 9 else META + i * P
                    for half in range(2):
                        u = 2 * i + half
                        dve.wait_ge(turned, u + 1)
                        dve.tensor_copy(h[:, 4 * half:4 * half + 4, col:col + n],
                                        psum[:, u % 8, :].rearrange("p (k t) -> p k t", k=4)[:, :, 0:n])\
                            .then_inc(placed, 1)

    class Prep:

        def __init__(self, name):
            self.hi, self.lo = sem(name + "_x_hi"), sem(name + "_x_lo")
            self.sq, self.summed = sem(name + "_squared"), sem(name + "_summed")
            self.total, self.root, self.rstd = sem(name + "_total"), sem(name + "_root"), sem(name + "_rstd")

        def act_split(self, act):
            for k in range(KD):
                act.activation(xh[:, k, :], h[:, k, :], ACT.Copy).then_inc(self.hi, 1)
                if k >= 2:
                    act.wait_ge(self.summed, k - 1)
                act.activation(sq[:, k % 2, :], h[:, k, :], ACT.Square).then_inc(self.sq, 1)

        def act_root(self, act):
            for c, (t0, n) in enumerate(TOK):
                act.wait_ge(self.total, c + 1)
                act.activation(rstd[:, t0:t0 + n], psum[:, 6 + c % 2, 0:n], ACT.Sqrt, scale=1.0 / D,
                               bias=epsc[:, 0:1]).then_inc(self.root, 1)

        def dve_split(self, dve):
            for k in range(KD):
                dve.wait_ge(self.hi, k + 1)
                dve.tensor_tensor(xl[:, k, :], h[:, k, :], xh[:, k, :].bitcast(F32), ALU.subtract)\
                    .then_inc(self.lo, 1)
                dve.wait_ge(self.sq, k + 1)
                if k == 0:
                    dve.tensor_copy(acc[:], sq[:, 0, :]).then_inc(self.summed, 1)
                else:
                    dve.wait_ge(self.summed, k)
                    dve.tensor_tensor(acc[:], acc[:], sq[:, k % 2, :], ALU.add).then_inc(self.summed, 1)

        def dve_rstd(self, dve):
            for c, (t0, n) in enumerate(TOK):
                dve.wait_ge(self.root, c + 1)
                dve.reciprocal(rstd[:, t0:t0 + n], rstd[:, t0:t0 + n]).then_inc(self.rstd, 1)

        def pe_total(self, pe):
            pe.wait_ge(self.summed, KD)
            for c, (t0, n) in enumerate(TOK):
                if c == 2:
                    pe.wait_ge(self.root, 1)
                pe.matmul(psum[:, 6 + c % 2, 0:n], ones[:], acc[:, t0:t0 + n], start=True, stop=True)\
                    .then_inc(self.total, 1)

    def product(pe, bank, hi, lo, nk, bh, bl, ready=None):
        for k in range(nk):
            if ready is not None:
                pe.wait_ge(ready, k + 1)
            for n, (w, x) in enumerate(((hi, bh), (hi, bl), (lo, bh))):
                for c, (t0, nt) in enumerate(TOK):
                    mm = pe.matmul(psum[:, bank + c, 0:nt], w(k), x[:, k, t0:t0 + nt],
                                   start=(k == 0 and n == 0), stop=(k == nk - 1 and n == 2))
        return mm

    def dense(name, groups, prep=None, gates=None, load_x=None, tables=None):
        njobs = sum(2 * g.pairs for g in groups) + (1 if gates is not None else 0)
        loaded = [sem(f"{name}_w_loaded{u}") for u in range(2)]
        stored = [sem(f"{name}_stored{u}") for u in range(2)]
        scaled, hi_s, split = (sem(f"{name}_w_{x}") for x in ("scaled", "hi", "split"))
        job_done, evac, sig = (sem(f"{name}_{x}") for x in ("job_done", "evac", "activated"))
        swapped, part, xr, gm = (sem(f"{name}_{x}") for x in ("swapped", "part", "x_ready", "gate_memset"))
        xload = [sem(f"{name}_x_loaded{u}") for u in range(2)]
        tab = sem(f"{name}_tables")
        trot = sem(f"{name}_tables_scaled")
        gst = sem(f"{name}_gates_stored")
        gainful = any(g.gain is not None for g in groups)
        storing = groups[0].kind != "residual"
        pr = Prep(name) if prep else None
        nst = [0]
        G = njobs - 1
        hi_x = sem(f"{name}_x_hi2")

        def stored_before(r):
            return r * 16 + (48 if groups[0].kind == "rope_k" else 0)

        with nc.Block() as block:
            @block.sync
            def _(sp):
                if tables is not None:
                    sp.dma_start(cosr[:], a["rope_cos"]).then_inc(tab, 16)
                    sp.dma_start(sinr[:], a["rope_sin"]).then_inc(tab, 16)

                def load(g, j, n, u, r):
                    if not (isinstance(n, int) and n < 2):
                        sp.wait_ge(split, n - 1)
                    sp.dma_start(weight_tile(raw[:, u, :]), g.weight(j)).then_inc(loaded[u], 16)

                over(sp, groups, load)
                if gates is not None:
                    sp.wait_ge(gm, 1)
                    for half in range(2):
                        sp.dma_start(weight_tile(raw[:, 0, :])[:, :, 32 * half:32 * half + HA],
                                     gates[:, :, HA * half:HA * half + HA]).then_inc(loaded[0], 16)

            @block.gpsimd
            def _(pool):
                def split_w(g, j, n, u, r, gate_tile=False):
                    pool.wait_ge(loaded[u], r * 16 + (32 if gate_tile else 16))
                    if g.gain is not None:
                        pool.tensor_tensor(weight_tile(raw[:, u, :]), weight_tile(raw[:, u, :]),
                                           gains[:, g.gain, :].unsqueeze(2).to_broadcast([P, KD, P]),
                                           ALU.mult).then_inc(scaled, 1)
                        pool.wait_ge(scaled, n + 1)
                    if not (isinstance(n, int) and n < 2):
                        pool.wait_ge(job_done, n - 1)
                    pool.tensor_tensor(wh[:, u, :], raw[:, u, :], unit, ALU.mult).then_inc(hi_s, 1)
                    pool.wait_ge(hi_s, n + 1)
                    pool.tensor_tensor(wl[:, u, :], raw[:, u, :], wh[:, u, :].bitcast(F32), ALU.subtract)\
                        .then_inc(split, 1)

                over(pool, groups, split_w)
                if gates is not None:
                    pool.memset(raw[:, 0, :], 0.0).then_inc(gm, 1)
                    split_w(groups[0], None, G, 0, G // 2, gate_tile=True)

            @block.tensor
            def _(pe):
                def job(g, j, n, u, r, ready=None):
                    pe.wait_ge(split, n + 1)
                    if not (isinstance(n, int) and n < 2):
                        pe.wait_ge(evac, n - 1)
                    hi, lo = weight_tile(wh[:, u, :]), weight_tile(wl[:, u, :])
                    if ready is None and isinstance(n, int) and n == 0:
                        ready = pr.lo if pr else (xr if load_x is not None else None)
                    product(pe, 3 * u, lambda k: hi[:, k, :], lambda k: lo[:, k, :], KD, xh, xl, ready)\
                        .then_inc(job_done, 1)
                    if isinstance(n, int) and n == 0 and pr:
                        pr.pe_total(pe)

                over(pe, groups, job)
                if gates is not None:
                    job(None, None, G, 0, G // 2)

            @block.scalar
            def _(act):
                if load_x is not None:
                    for k in range(KD + 1):
                        if k < KD:
                            if k >= 2:
                                act.wait_ge(xr, k - 1)
                            act.dma_start(sq[:, k % 2, :], load_x[k]).then_inc(xload[k % 2], 16)
                        if k >= 1:
                            act.wait_ge(xload[(k - 1) % 2], 16 * ((k - 1) // 2 + 1))
                            act.activation(xh[:, k - 1, :], sq[:, (k - 1) % 2, :], ACT.Copy).then_inc(hi_x, 1)
                if pr:
                    pr.act_split(act)
                    pr.act_root(act)

                def finish(g, j, n, u, r):
                    if g.kind == "sigmoid":
                        act.wait_ge(part, n - g.n0 + 1)
                        act.activation(tmp[:, u, :], tmp[:, u, :], ACT.Sigmoid).then_inc(sig, 1)
                        act.wait_ge(sig, n - g.n0 + 1)
                        act.dma_start(qkvo[ds(j + g.n0, 1)].rearrange("a p t -> (a p) t"), tmp[:, u, :])\
                            .then_inc(stored[u], 16)
                    elif g.kind == "store":
                        act.wait_ge(evac, n + 1)
                        act.dma_start(qkvo[ds(j + g.n0, 1)].rearrange("a p t -> (a p) t"), tmp[:, u, :])\
                            .then_inc(stored[u], 16)
                    elif g.kind in ("rope_k", "rope_q"):
                        act.wait_ge(part, n + 1 if g.n0 == 0 else n - 1)
                        if not (isinstance(n, int) and n == 0):
                            act.wait_ge(evac, n)
                        for q in range(4):
                            o, i = 32 * q, 32 * (q ^ 1)
                            for c, (t0, nt) in enumerate(TOK):
                                x = act.activation(swp[o:o + 32, t0:t0 + nt], psum[i:i + 32, 3 * u + c, 0:nt],
                                                   ACT.Copy)
                        x.then_inc(swapped, 1)
                        act.wait_ge(evac, n + 1)
                        if g.kind == "rope_k":
                            for hh in range(2):
                                for dup in range(2):
                                    act.dma_start(k2_d[2 * j + hh, HD * dup:HD * dup + HD, :],
                                                  tmp[HD * hh:HD * hh + HD, u, :]).then_inc(stored[u], 16)
                        else:
                            act.dma_start(qr_d[ds(j, 1)].rearrange("a p t -> (a p) t"), tmp[:, u, :])\
                                .then_inc(stored[u], 16)
                    elif g.kind == "plain_v":
                        act.wait_ge(evac, n + 1)
                        act.dma_start(vt_d[j], tmp[:, u, :]).then_inc(stored[u], 16)

                over(act, groups, finish)
                if gates is not None:
                    act.wait_ge(evac, G + 1)
                    for half in range(2):
                        act.dma_start(gates_d[half], tmp[0:4, half, :]).then_inc(gst, 16)
                    act.wait_ge(gst, 32)
                if storing:
                    for u in range(2):
                        act.wait_ge(stored[u], stored_before(njobs // 2))

            @block.vector
            def _(dve):
                if load_x is not None:
                    for k in range(KD):
                        dve.wait_ge(hi_x, k + 1)
                        dve.tensor_tensor(xl[:, k, :], sq[:, k % 2, :], xh[:, k, :].bitcast(F32), ALU.subtract)\
                            .then_inc(xr, 1)
                if pr:
                    pr.dve_split(dve)
                    pr.dve_rstd(dve)
                    dve.wait_ge(pr.rstd, 3)
                if tables is not None:
                    dve.wait_ge(tab, 32)
                    dve.tensor_tensor(cosr[:], cosr[:], rstd[:], ALU.mult).then_inc(trot, 1)
                    dve.tensor_tensor(sinr[:], sinr[:], rstd[:], ALU.mult).then_inc(trot, 1)
                    dve.wait_ge(trot, 2)

                def leave(g, j, n, u, r):
                    dve.wait_ge(job_done, n + 1)
                    if g.kind == "residual":
                        for c, (t0, nt) in enumerate(TOK):
                            x = dve.tensor_tensor(hcol(j + g.n0, t0, nt), hcol(j + g.n0, t0, nt), psum[:, 3 * u + c, 0:nt], ALU.add)
                        x.then_inc(evac, 1)
                        return
                    if not (isinstance(n, int) and n < 2):
                        dve.wait_ge(stored[u], stored_before(r))
                    if g.kind in ("rope_k", "rope_q"):
                        for c, (t0, nt) in enumerate(TOK):
                            x = dve.tensor_tensor(tmp[:, u, t0:t0 + nt], psum[:, 3 * u + c, 0:nt],
                                                  cosr[:, t0:t0 + nt], ALU.mult)
                        x.then_inc(part, 1)
                        rc = rope_count(g, n)
                        dve.wait_ge(swapped, rc + 1)
                        dve.tensor_tensor(swp[:], swp[:], sinr[:], ALU.mult).then_inc(sig, 1)
                        dve.wait_ge(sig, rc + 1)
                        dve.wait_ge(part, rc + 1)
                        dve.tensor_tensor(tmp[:, u, :], tmp[:, u, :], swp[:], ALU.add).then_inc(evac, 1)
                    elif g.kind == "sigmoid":
                        for c, (t0, nt) in enumerate(TOK):
                            x = dve.tensor_tensor(tmp[:, u, t0:t0 + nt], psum[:, 3 * u + c, 0:nt],
                                                  rstd[:, t0:t0 + nt], ALU.mult)
                        x.then_inc(part, 1)
                        dve.wait_ge(part, n - g.n0 + 1)
                        dve.sem_inc(evac, 1)
                    else:
                        for c, (t0, nt) in enumerate(TOK):
                            x = dve.tensor_tensor(tmp[:, u, t0:t0 + nt], psum[:, 3 * u + c, 0:nt],
                                                  rstd[:, t0:t0 + nt], ALU.mult)
                        x.then_inc(evac, 1)

                def rope_count(g, n):
                    return n if g.n0 == 0 else n - 2

                def hcol(j, t0, nt):
                    if isinstance(j, int):
                        return h[:, j, t0:t0 + nt]
                    return h[:, ds(j, 1), t0:t0 + nt].rearrange("p a t -> p (a t)")

                over(dve, groups, leave)
                if gates is not None:
                    dve.wait_ge(job_done, G + 1)
                    for u in range(2):
                        dve.wait_ge(stored[u], stored_before(G // 2))
                    for half in range(2):
                        for c, (t0, nt) in enumerate(TOK):
                            x = dve.tensor_tensor(tmp[0:4, half, t0:t0 + nt],
                                                  psum[32 * half:32 * half + 4, c, 0:nt],
                                                  rstd[0:4, t0:t0 + nt], ALU.mult)
                    x.then_inc(evac, 1)

    def ffn(name, w_gu, w_dn, gain):
        NG = DFF // P // 2
        loaded = [sem(f"{name}_w_loaded{u}") for u in range(2)]
        scaled, hi_s, split, used = (sem(f"{name}_w_{x}") for x in ("scaled", "hi", "split", "used"))
        gu_done, gu_evac, silu, hid = (sem(f"{name}_{x}") for x in ("gate_up_done", "gate_up_evac", "silu", "hidden"))
        hhi, hlo, dn_done, dn_evac = (sem(f"{name}_{x}") for x in ("hid_hi", "hid_lo", "down_done", "down_evac"))
        pr = Prep(name)
        gu = w_gu.rearrange("(k p) n -> p k n", p=P)

        def source(kind, g, s):
            if kind == "d":
                return w_dn[ds((g * 2 + s) * P, P), :]
            return gu[:, :, ds((g * 2 + s) * P + (DFF if kind == "u" else 0), P)]

        FIRST = [("g", 0), ("u", 0), ("g", 1), ("u", 1)]
        BODY = [("g", 0), ("d", 0), ("d", 1), ("u", 0), ("g", 1), ("u", 1)]

        def stream(eng, body):
            for n, (kind, s) in enumerate(FIRST):
                body(kind, 0, s, n, n, n // 2)
            with eng.Fori(0, NG - 1) as i:
                for q, (kind, s) in enumerate(BODY):
                    body(kind, i if kind == "d" else i + 1, s, i * 6 + 4 + q, 4 + q, i * 3 + (4 + q) // 2)
            for s in range(2):
                n = 4 + 6 * (NG - 1) + s
                body("d", NG - 1, s, n, n, n // 2)

        with nc.Block() as block:
            @block.sync
            def _(sp):
                def load(kind, g, s, n, pos, r):
                    if pos >= 2:
                        sp.wait_ge(split, n - 1)
                    dst = raw[:, pos % 2, :] if kind == "d" else weight_tile(raw[:, pos % 2, :])
                    sp.dma_start(dst, source(kind, g, s)).then_inc(loaded[pos % 2], 16)

                stream(sp, load)

            @block.gpsimd
            def _(pool):
                def split_w(kind, g, s, n, pos, rnd):
                    r, b = pos % 2, pos % 3
                    pool.wait_ge(loaded[r], rnd * 16 + 16)
                    if kind != "d":
                        pool.tensor_tensor(weight_tile(raw[:, r, :]), weight_tile(raw[:, r, :]),
                                           gains[:, gain, :].unsqueeze(2).to_broadcast([P, KD, P]),
                                           ALU.mult).then_inc(scaled, 1)
                    else:
                        pool.sem_inc(scaled, 1)
                    pool.wait_ge(scaled, n + 1)
                    if pos >= 3:
                        pool.wait_ge(used, n - 2)
                    pool.tensor_tensor(wh[:, b, :], raw[:, r, :], unit, ALU.mult).then_inc(hi_s, 1)
                    pool.wait_ge(hi_s, n + 1)
                    pool.tensor_tensor(wl[:, b, :], raw[:, r, :], wh[:, b, :].bitcast(F32), ALU.subtract)\
                        .then_inc(split, 1)

                stream(pool, split_w)

            @block.tensor
            def _(pe):
                def gate_up(n, pos, set_, gu_n, dn_n, first=False):
                    b = pos % 3
                    pe.wait_ge(split, n + 1)
                    hi, lo = weight_tile(wh[:, b, :]), weight_tile(wl[:, b, :])
                    mm = product(pe, 3 * set_, lambda k: hi[:, k, :], lambda k: lo[:, k, :], KD, xh, xl,
                                 pr.lo if first else None)
                    mm.then_inc(gu_done, 1)
                    pe.wait_ge(gu_done, gu_n + 1)
                    pe.sem_inc(used, 1)

                def down(n, pos, dn_n):
                    b0, b1 = pos % 3, (pos + 1) % 3
                    pe.wait_ge(split, n + 2)
                    hi = [wh[:, b0, :], wh[:, b1, :]]
                    lo = [wl[:, b0, :], wl[:, b1, :]]
                    for m in range(KD):
                        if m == 1:
                            pe.wait_ge(gu_evac, down_gu)
                        if m >= 2:
                            pe.wait_ge(dn_evac, dn_n + m - 1)
                        mm = product(pe, 3 * ((m + 1) % 2), lambda k: hi[k][:, m * P:(m + 1) * P],
                                     lambda k: lo[k][:, m * P:(m + 1) * P], 2, hidh, hidl)
                        mm.then_inc(dn_done, 1)
                    pe.wait_ge(dn_done, dn_n + KD)
                    pe.sem_inc(used, 2)

                for q in range(4):
                    if q >= 2:
                        pe.wait_ge(gu_evac, q - 1)
                    gate_up(q, q, q % 2, q, 0, first=(q == 0))
                    if q == 0:
                        pr.pe_total(pe)
                with pe.Fori(0, NG - 1) as i:
                    n, g4, d8 = i * 6 + 4, i * 4 + 4, i * 8
                    pe.wait_ge(gu_evac, g4 - 1)
                    gate_up(n, 4, 0, g4, d8)
                    down_gu = g4 + 1
                    pe.wait_ge(hlo, i * 2 + 2)
                    pe.wait_ge(gu_evac, g4)
                    down(n + 1, 5, d8)
                    pe.wait_ge(dn_evac, d8 + 7)
                    gate_up(n + 3, 7, 1, g4 + 1, d8)
                    pe.wait_ge(dn_evac, d8 + 8)
                    gate_up(n + 4, 8, 0, g4 + 2, d8)
                    pe.wait_ge(gu_evac, g4 + 2)
                    gate_up(n + 5, 9, 1, g4 + 3, d8)
                N = 4 + 6 * (NG - 1)
                down_gu = 4 * NG
                pe.wait_ge(hlo, 2 * NG)
                pe.wait_ge(gu_evac, 4 * NG)
                down(N, N, 8 * (NG - 1))

            def gate_part(act, n2):
                act.wait_ge(gu_evac, n2 * 2 + 1)
                act.activation(gate[:], gate[:], ACT.Silu).then_inc(silu, 1)

            def hidden_part(act, n2, s):
                act.wait_ge(hid, n2 + 1)
                act.activation(hidh[:, s, :], up[:], ACT.Copy).then_inc(hhi, 1)

            @block.scalar
            def _(act):
                pr.act_split(act)
                pr.act_root(act)
                for s in range(2):
                    gate_part(act, s)
                    hidden_part(act, s, s)
                with act.Fori(1, NG) as i:
                    for s in range(2):
                        gate_part(act, i * 2 + s)
                        hidden_part(act, i * 2 + s, s)

            @block.vector
            def _(dve):
                pr.dve_split(dve)
                pr.dve_rstd(dve)
                dve.wait_ge(pr.rstd, 3)

                def take(n, dst, set_):
                    dve.wait_ge(gu_done, n + 1)
                    for c, (t0, nt) in enumerate(TOK):
                        x = dve.tensor_tensor(dst[:, t0:t0 + nt], psum[:, 3 * set_ + c, 0:nt], rstd[:, t0:t0 + nt],
                                              ALU.mult)
                    x.then_inc(gu_evac, 1)

                def gate_out(n2, set_, first=False):
                    if not first:
                        dve.wait_ge(hid, n2)
                    take(n2 * 2, gate, set_)

                def up_out(n2, s, set_, first=False):
                    if not first:
                        dve.wait_ge(hlo, n2)
                        dve.wait_ge(hhi, n2)
                    take(n2 * 2 + 1, up, set_)
                    dve.wait_ge(gu_evac, n2 * 2 + 2)
                    dve.wait_ge(silu, n2 + 1)
                    dve.tensor_tensor(up[:], up[:], gate[:], ALU.mult).then_inc(hid, 1)
                    dve.wait_ge(hhi, n2 + 1)
                    dve.tensor_tensor(hidl[:, s, :], up[:], hidh[:, s, :].bitcast(F32), ALU.subtract).then_inc(hlo, 1)

                def down_out(d8):
                    for m in range(KD):
                        dve.wait_ge(dn_done, d8 + m + 1)
                        for c, (t0, nt) in enumerate(TOK):
                            x = dve.tensor_tensor(h[:, m, t0:t0 + nt], h[:, m, t0:t0 + nt],
                                                  psum[:, 3 * ((m + 1) % 2) + c, 0:nt], ALU.add)
                        x.then_inc(dn_evac, 1)

                gate_out(0, 0, True)
                up_out(0, 0, 1, True)
                gate_out(1, 0)
                up_out(1, 1, 1)
                with dve.Fori(1, NG) as i:
                    gate_out(i * 2, 0)
                    down_out(i * 8 - 8)
                    up_out(i * 2, 0, 1)
                    gate_out(i * 2 + 1, 0)
                    up_out(i * 2 + 1, 1, 1)
                down_out(8 * (NG - 1))

    S = dict(locals())
    if upto >= 0:
        run(setup)
    if upto >= 1:
        wi = wcols(a["a_w_in"][0])
        ga = a["a_w_in"][0].rearrange("(k p) n -> p k n", p=P)[:, :, 24 * P:24 * P + 8]
        run(dense, "in", [Group(0, 1, wi, 0, "store"),
                     Group(2, 7, lambda j: wi(j + 2), 0, "store"),
                     Group(16, 4, lambda j: wi(j + 16), 0, "sigmoid")], prep=True, gates=ga)
    if upto >= 2:
        run(mlstm, nc, a, S)
    if upto >= 3:
        wo = wcols(a["a_w_out"][0])
        run(dense, "out0", [Group(0, 1, wo, 1, "residual"), Group(2, 3, lambda j: wo(j + 2), 1, "residual")], load_x=og_d)
    if upto >= 4:
        run(ffn, "ffn0", a["w_gate_up"][0], a["w_down"][0], 2)
    if upto >= 5:
        wk, wv, wq = wcols(a["w_kv"]), wcols(a["w_kv"], 2 * P), wcols(a["b_w_q"][0])
        run(dense, "kvq", [Group(0, 1, wk, 3, "rope_k"), Group(2, 1, wv, 3, "plain_v"), Group(4, 4, wq, 4, "rope_q")],
              prep=True, tables=True)
    if upto >= 6:
        run(attention, nc, a, S)
    if upto >= 7:
        wo1 = wcols(a["b_w_o"][0])
        run(dense, "out1", [Group(0, 1, wo1, None, "residual"),
                       Group(2, 3, lambda j: wo1(j + 2), None, "residual")], load_x=og_d)
    if upto >= 8:
        run(ffn, "ffn1", a["w_gate_up"][1], a["w_down"][1], 5)
    if upto >= 9:
        run(final, nc, a, S)

def mlstm(nc, a, s):
    at, sem, psum, ident = s["at"], s["sem"], s["psum"], s["ident"]
    qkvo, gates_d, og_d, ones = s["qkvo"], s["gates_d"], s["og_d"], s["ones"]
    epsc = s["epsc"]
    place = [s["fixed_end"]]

    def sb(name, shape, dt=F32):
        t, place[0] = at("ml_" + name, shape, dt, place[0])
        return t

    E1 = DV + 1
    qc = sb("q", [P, 2, HA, MCH])
    kc = sb("k", [P, 2, HA, MCH])
    vc = sb("v", [P, 2, 2 * HA, MCH])
    oc = sb("o", [P, 2, 2 * HA, MCH])
    ex = sb("exp", [P, HA, MCH])
    pr = sb("weights", [P, HA, MCH])
    va = sb("v_ones", [P, HA, E1])
    kw = sb("k_weighted", [P, HA, MCH])
    inter = sb("inter", [P, HA, E1])
    num = sb("num", [P, HA, E1])
    hn = sb("hn", [P, HA, DV])
    junk = sb("junk", [P, DV])
    C = sb("state", [P, HA, E1])
    col = sb("cols", [P, 10, 100])
    cc = sb("chunk_cols", [P, 100])
    dec = sb("decays", [P, HA, 17])
    dc = sb("chunk_decay", [P, HA])
    small = sb("small", [P, 8, HA])
    sel = sb("select_head", [HA, HA, P])
    gi, gf, lsf, bb, mm, nm = (sb(x, [HA, T]) for x in ("logi", "f", "logf", "cumulated", "stabiliser", "neg_M"))
    t1, keep = sb("t1", [HA, T]), sb("keep", [HA, T])
    rows = sb("rows", [P, T])
    sm = sb("state_m", [HA, NB])
    bg = sb("gate_bias", [HA, 2])
    dr = sb("decay_rows", [HA, 17])
    CS = sb("decode_state", [P, NB, HA, E1])
    qm = sb("q_masked", [P, NB, MCH])
    kwm = sb("k_weighted_seq", [P, 2, MCH])

    g_load, consts, rows_pe, dec_pe = (sem("ml_" + x) for x in ("gates_loaded", "consts", "rows_turned", "decays_pe"))
    dv, ac = sem("ml_rows_dve"), sem("ml_rows_act")
    cols_ev, dec_ev, st_load, m_out = (sem("ml_" + x) for x in ("cols_evac", "decays_evac", "states_loaded", "m_stored"))
    c_load = [sem(f"ml_chunk_loaded{u}") for u in range(2)]
    (mb, sc, kt, vt, qcs, pv, upd, ht) = (sem("ml_pe_" + x) for x in
                                          ("minus_m", "scores", "k_turned", "v_turned", "inter", "intra", "update", "h_turned"))
    (exps, kws, ints, ssq, root) = (sem("ml_act_" + x) for x in ("exp", "k_weighted", "inter", "squares", "root"))
    (prs, vas, nums, den, rden, rinv, fac, hns, cup, ogs) = (
        sem("ml_dve_" + x) for x in ("weights", "values", "num", "den", "rden", "rinv", "factor", "hn", "state", "gated"))
    (ccs, msk) = (sem("ml_pool_" + x) for x in ("chunk_cols", "masked"))
    og_st = [sem(f"ml_out_stored{u}") for u in range(2)]
    c_out, qms, kwms, cs_up, cs_out, cs_pe, zero = (sem("ml_" + x) for x in (
        "state_stored", "q_masked", "seq_k_weighted", "seq_state", "seq_state_stored", "seq_update", "zeroed"))

    dcs = sem("ml_pool_chunk_decay")
    qcs_h, local, aden = sem("ml_pe_inter_head"), sem("ml_rows_local"), sem("ml_dve_abs_den")

    def diag_blocks(t):
        x = t[:]
        return bass.AP(x.tensor, x.offset, [list(x.ap[0]), [MCH + TS, NB], [1, TS]])

    CHN = [(0, 0, META)] + [(c, META + MCH * (c - 1), MCH) for c in range(1, NMC + 1)] + [(NMC + 1, T_S, NS)]

    def chunks(eng, body):
        body(0, 0, META, 0, 0)
        with eng.Fori(0, NMC // 2) as i:
            for u in range(2):
                body(i * 2 + (1 + u), i * (2 * MCH) + (META + u * MCH), MCH, (1 + u) % 2, i + u)
        body(NMC + 1, T_S, NS, (NMC + 1) % 2, NMC // 2)

    with nc.Block() as block:
        @block.sync
        def _(sp):
            sp.dma_start(gi[:], gates_d[0]).then_inc(g_load, 16)
            sp.dma_start(gf[:], gates_d[1]).then_inc(g_load, 16)
            with nc.allow_non_contiguous_dma("small"):
                sp.dma_start(bg[:], a["a_b_gate"][0].rearrange("(i h) -> h i", i=2)).then_inc(g_load, 16)
                sp.dma_start(sm[:], a["state_m"].rearrange("b a h -> h (a b)")).then_inc(g_load, 16)

            def load(c, t0, n, u, r):
                if not (isinstance(c, int) and c < 2):
                    sp.wait_ge(og_st[u], r * 16)
                for dst, r0, nr in ((qc, 0, 4), (kc, 4, 4), (vc, 8, 8), (oc, 16, 8)):
                    sp.dma_start(dst[:, u, :, 0:n], qkvo[r0:r0 + nr, :, ds(t0, n)].rearrange("j p t -> p j t"))\
                        .then_inc(c_load[u], 16)

            load(0, 0, META, 0, 0)
            load(1, META, MCH, 1, 0)
            for b in range(NB):
                sp.dma_start(CS[:, b, :, 0:DV], a["state_c"][b, 0].rearrange("h d e -> d h e")).then_inc(st_load, 16)
                with nc.allow_non_contiguous_dma("normaliser columns"):
                    sp.dma_start(CS[:, b, :, DV], a["state_n"][b, 0].rearrange("h d -> d h")).then_inc(st_load, 16)
            load(2, META + MCH, MCH, 0, 1)
            with sp.Fori(1, NMC // 2) as i:
                for u in range(2):
                    load(i * 2 + (1 + u), i * (2 * MCH) + (META + u * MCH), MCH, (1 + u) % 2, i + u)
            load(NMC + 1, T_S, NS, 1, NMC // 2)
            sp.wait_ge(dv, 5)
            with nc.allow_non_contiguous_dma("small"):
                sp.dma_start(a["m_p"].rearrange("b a h -> h (a b)"), mm[:, T_S - 1:T_S]).then_inc(m_out, 16)
                sp.dma_start(a["m_s"].rearrange("b a h -> h (a b)"), mm[:, T_S + TS - 1:T:TS]).then_inc(m_out, 16)
            sp.wait_ge(m_out, 32)

        @block.gpsimd
        def _(pool):
            pool.memset(sel[:], 0.0).then_inc(zero, 1)
            pool.wait_ge(zero, 1)
            pool.affine_select(out=sel[:], in_=sel[:], compare_op=ALU.not_equal, fill=1.0, base=0,
                               pattern=[[-1, HA], [0, P]], channel_multiplier=1).then_inc(consts, 1)
            pool.memset(va[:, :, DV:E1], 1.0).then_inc(consts, 1)
            pool.memset(qm[:], 0.0).then_inc(consts, 1)

            def step(c, t0, n, u, r):
                if not (isinstance(c, int) and c == 0):
                    pool.wait_ge(hns, c * HA)
                    pool.wait_ge(cup, c * HA)
                else:
                    pool.wait_ge(cols_ev, 10)
                    pool.wait_ge(dec_ev, 1)
                if isinstance(c, int):
                    pool.tensor_copy(cc[0:n, :], col[0:n, c, :]).then_inc(ccs, 1)
                    pool.wait_ge(exps, c * HA + HA)
                    pool.tensor_copy(dc[:], dec[:, :, c]).then_inc(dcs, 1)
                else:
                    pool.tensor_copy(cc[:], col[:, ds(c, 1), :].rearrange("p a x -> p (a x)")).then_inc(ccs, 1)
                    pool.wait_ge(exps, c * HA + HA)
                    pool.tensor_copy(dc[:], dec[:, :, ds(c, 1)].rearrange("p h a -> p (h a)")).then_inc(dcs, 1)
                e = ex[0:n, :, 0:n]
                x = pool.affine_select(out=e, in_=e, compare_op=ALU.is_ge, fill=0.0, base=0,
                                       pattern=[[0, HA], [1, n]], channel_multiplier=-1)
                x.then_inc(msk, 1)
                if isinstance(c, int) and c == NMC + 1:
                    pool.wait_ge(msk, c + 1)
                    e = ex[:].rearrange("p h (b t) -> p h b t", t=TS)
                    pool.affine_select(out=e, in_=e, compare_op=ALU.is_ge, fill=0.0, base=0,
                                       pattern=[[0, HA], [-TS, NB], [0, TS]], channel_multiplier=1).then_inc(msk, 1)

            chunks(pool, step)

        def masked(c):
            return NMC + 3 if isinstance(c, int) and c == NMC + 1 else c + 1

        @block.tensor
        def _(pe):
            pe.wait_ge(consts, 3)
            pe.wait_ge(ac, 5)
            pe.wait_ge(dv, 11)
            for c, t0, n in CHN:
                if c >= 4:
                    pe.wait_ge(cols_ev, c - 3)
                pe.transpose(psum[0:n, c % 4, 0:100], rows[0:100, t0:t0 + n], ident[0:100, 0:100]).then_inc(rows_pe, 1)
            for hd in range(HA):
                x = pe.matmul(psum[:, 4, hd * 17:hd * 17 + 17], sel[:, hd, :], dr[:], start=True, stop=True)
            x.then_inc(dec_pe, 1)

            def step(c, t0, n, u, r):
                last = isinstance(c, int) and c == NMC + 1
                first = isinstance(c, int) and c == 0
                if first:
                    pe.wait_ge(cols_ev, 10)
                    pe.wait_ge(dec_ev, 1)
                else:
                    pe.wait_ge(ogs, c * 2)
                for hd in range(HA):
                    rhs = nm[:, t0:t0 + n] if isinstance(c, int) else nm[:, ds(t0, n)]
                    x = pe.matmul(psum[0:n, 6, hd * MCH:hd * MCH + n], sel[:, hd, 0:n], rhs, start=True, stop=True)
                x.then_inc(mb, 1)
                pe.wait_ge(c_load[u], r * 64 + 64)
                if not first:
                    pe.wait_ge(cup, c * HA)
                for hd in range(HA):
                    x = pe.matmul(psum[0:n, 0, hd * MCH:hd * MCH + n], kc[:, u, hd, 0:n], qc[:, u, hd, 0:n],
                                  start=True, stop=True)
                x.then_inc(sc, 1)
                for hd in range(HA):
                    x = pe.transpose(psum[0:n, 7, hd * MCH:hd * MCH + MCH], kc[:, u, hd, 0:n], ident[:])
                x.then_inc(kt, 1)
                if not first:
                    pe.wait_ge(nums, c * HA)
                for j in range(2 * HA):
                    x = pe.transpose(psum[0:n, 1 + j // 4, (j % 4) * P:(j % 4 + 1) * P], vc[:, u, j, 0:n], ident[:])
                x.then_inc(vt, 1)
                if last:
                    pe.wait_ge(st_load, 16 * 2 * NB)
                for hd in range(HA):
                    o = psum[0:n, 3 + hd % 2, 0:E1]
                    if first:
                        continue
                    if hd >= 2:
                        pe.wait_ge(ints, (c - 1) * HA + hd - 1)
                    if not last:
                        pe.matmul(o, qc[:, u, hd, 0:n], C[:, hd, :], start=True, stop=True).then_inc(qcs_h, 1)
                    else:
                        pe.wait_ge(qms, hd + 1)
                        for b in range(NB):
                            x = pe.matmul(o, qm[:, b, :], CS[:, b, hd, :], start=(b == 0), stop=(b == NB - 1))
                        x.then_inc(qcs_h, 1)
                if first:
                    pe.wait_ge(vt, 1)
                    pe.sem_inc(qcs, 1)
                else:
                    pe.wait_ge(qcs_h, c * HA)
                    pe.sem_inc(qcs, 1)
                pe.wait_ge(vas, c * 2 + 2)
                pe.wait_ge(prs, c + 1)
                for hd in range(HA):
                    if hd >= 2:
                        pe.wait_ge(nums, c * HA + hd - 1)
                    pe.matmul(psum[0:n, 1 + hd % 2, 0:E1], pr[0:n, hd, 0:n], va[0:n, hd, :], start=True, stop=True)\
                        .then_inc(pv, 1)
                if not last:
                    for hd in range(HA):
                        pe.wait_ge(kws, c * HA + hd + 1)
                        if hd >= 2:
                            pe.wait_ge(cup, c * HA + hd - 1)
                        pe.matmul(psum[:, 5 if hd % 2 else 0, 0:E1], kw[0:n, hd, :], va[0:n, hd, :],
                                  start=True, stop=True).then_inc(upd, 1)
                else:
                    for n2 in range(NB * HA):
                        pe.wait_ge(kwms, n2 + 1)
                        if n2 >= 2:
                            pe.wait_ge(cs_up, n2 - 1)
                        pe.matmul(psum[:, 5 if n2 % 2 else 0, 0:E1], kwm[:, n2 % 2, :], va[:, n2 // NB, :],
                                  start=True, stop=True).then_inc(cs_pe, 1)
                pe.wait_ge(hns, c * HA + HA)
                pe.wait_ge(exps, c * HA + HA)
                if not last:
                    pe.wait_ge(kws, c * HA + HA)
                for j in range(2 * HA):
                    x = pe.transpose(psum[:, 6 + j // 4, (j % 4) * MCH:(j % 4) * MCH + n],
                                     hn[0:n, j // 2, (j % 2) * P:(j % 2 + 1) * P], ident[0:n, 0:n])
                    if j % 4 == 3:
                        x.then_inc(ht, 1)

            chunks(pe, step)

        @block.scalar
        def _(act):
            act.wait_ge(dv, 1)
            act.activation(t1[:], t1[:], ACT.Exp, scale=-1.0).then_inc(ac, 1)
            act.wait_ge(ac, 1)
            act.activation(t1[:], t1[:], ACT.Ln, bias=ones[0:HA, 0:1]).then_inc(ac, 1)
            act.wait_ge(dv, 9)
            act.activation(rows[32:32 + HA, :], t1[:], ACT.Exp).then_inc(ac, 1)
            act.activation(rows[64:64 + HA, :], mm[:], ACT.Exp, scale=-1.0).then_inc(ac, 1)
            act.activation(rows[0:HA, :], keep[:], ACT.Copy).then_inc(ac, 1)

            def step(c, t0, n, u, r):
                last = isinstance(c, int) and c == NMC + 1
                first = isinstance(c, int) and c == 0
                act.wait_ge(mb, c + 1)
                act.wait_ge(ccs, c + 1)
                if not first:
                    act.wait_ge(prs, c)
                    act.wait_ge(kws, c * HA)
                for hd in range(HA):
                    act.activation(ex[0:n, hd, 0:n], psum[0:n, 6, hd * MCH:hd * MCH + n], ACT.Exp,
                                   bias=cc[0:n, hd:hd + 1]).then_inc(exps, 1)
                if not last:
                    act.wait_ge(kt, c + 1)
                    act.wait_ge(msk, masked(c))
                    if not first:
                        act.wait_ge(upd, c * HA)
                    for hd in range(HA):
                        act.activation(kw[0:n, hd, :], psum[0:n, 7, hd * MCH:(hd + 1) * MCH], ACT.Copy,
                                       scale=ex[0:n, hd, n - 1:n]).then_inc(kws, 1)
                for hd in range(HA):
                    if first:
                        continue
                    act.wait_ge(qcs_h, (c - 1) * HA + hd + 1)
                    act.wait_ge(nums, c * HA)
                    act.activation(inter[0:n, hd, :], psum[0:n, 3 + hd % 2, 0:E1], ACT.Copy,
                                   scale=cc[0:n, 96 + hd:97 + hd]).then_inc(ints, 1)
                act.wait_ge(rden, c + 1)
                for hd in range(HA):
                    if not (first and hd == 0):
                        act.wait_ge(ssq, c * HA + hd)
                    act.activation(junk[0:n, :], num[0:n, hd, 0:DV], ACT.Square, scale=small[0:n, 1, hd:hd + 1],
                                   accum_out=small[0:n, 2, hd:hd + 1]).then_inc(ssq, 1)
                act.wait_ge(ssq, c * HA + HA)
                act.activation(small[0:n, 3, :], small[0:n, 2, :], ACT.Sqrt, scale=1.0 / DV,
                               bias=epsc[0:n, 0:1]).then_inc(root, 1)
                if last:
                    act.wait_ge(kt, c + 1)
                    act.wait_ge(msk, masked(c))
                    for hd in range(HA):
                        for b in range(NB):
                            n2 = hd * NB + b
                            if n2 >= 2:
                                act.wait_ge(cs_pe, n2 - 1)
                            act.activation(kwm[:, n2 % 2, :], psum[:, 7, hd * MCH:(hd + 1) * MCH], ACT.Copy,
                                           scale=ex[:, hd, TS * b + TS - 1:TS * b + TS]).then_inc(kwms, 1)
                act.wait_ge(ogs, c * 2 + 2)
                act.dma_start(og_d[:, :, ds(t0, n)].rearrange("j p t -> p j t"), oc[:, u, :, 0:n])\
                    .then_inc(og_st[u], 16)

            chunks(act, step)
            for u in range(2):
                act.wait_ge(og_st[u], 16 * 5)

        @block.vector
        def _(dve):
            dve.wait_ge(g_load, 64)
            dve.tensor_scalar(gf[:], gf[:], bg[:, 1:2], None, ALU.add).then_inc(local, 1)
            dve.tensor_scalar(gi[:], gi[:], bg[:, 0:1], None, ALU.add).then_inc(local, 1)
            dve.memset(keep[:], 1.0).then_inc(local, 1)
            dve.memset(rows[:], 0.0).then_inc(local, 1)
            dve.wait_ge(local, 4)
            dve.scalar_tensor_tensor(t1[:], gf[:], -1.0, gf[:], ALU.mult, ALU.max).then_inc(dv, 1)
            dve.memset(keep[:, META:T_S:MCH], 0.0).then_inc(local, 1)
            dve.memset(keep[:, T_S:T:TS], 0.0).then_inc(local, 1)
            dve.wait_ge(ac, 2)
            dve.scalar_tensor_tensor(lsf[:], gf[:], 0.0, t1[:], ALU.min, ALU.subtract).then_inc(dv, 1)
            dve.wait_ge(dv, 2)
            dve.wait_ge(local, 6)
            dve.tensor_tensor_scan(bb[:], keep[:], lsf[:], 0.0, ALU.mult, ALU.add).then_inc(dv, 1)
            dve.tensor_tensor_scan(mm[:, 0:T_S], lsf[:, 0:T_S], gi[:, 0:T_S], 0.0, ALU.add, ALU.max).then_inc(dv, 1)
            for b in range(NB):
                w = slice(T_S + b * TS, T_S + (b + 1) * TS)
                x = dve.tensor_tensor_scan(mm[:, w], lsf[:, w], gi[:, w], sm[:, b:b + 1], ALU.add, ALU.max)
            x.then_inc(dv, 1)
            dve.wait_ge(dv, 5)
            dve.tensor_tensor(nm[:], bb[:], mm[:], ALU.subtract).then_inc(dv, 1)
            dve.wait_ge(dv, 6)
            dve.tensor_copy(t1[:, 0:META], nm[:, 0:META]).then_inc(local, 1)
            v = lambda x, w, n: x.rearrange("p (c t) -> p c t", t=n)
            dve.tensor_tensor(v(t1[:, META:T_S], 0, MCH), v(nm[:, META:T_S], 0, MCH),
                              mm[:, META - 1:T_S - 1:MCH].unsqueeze(2).to_broadcast([HA, NMC, MCH]), ALU.add)\
                .then_inc(dv, 1)
            dve.tensor_tensor(v(t1[:, T_S:T], 0, TS), v(nm[:, T_S:T], 0, TS),
                              sm[:].unsqueeze(2).to_broadcast([HA, NB, TS]), ALU.add).then_inc(dv, 1)
            dve.wait_ge(local, 7)
            dve.tensor_tensor(keep[:], gi[:], bb[:], ALU.subtract).then_inc(dv, 1)
            dve.wait_ge(ac, 3)
            dve.tensor_scalar(rows[96:96 + HA, :], rows[32:32 + HA, :], QSCALE, None, ALU.mult).then_inc(dv, 1)
            dve.tensor_copy(dr[:, 0:1], rows[32:32 + HA, META - 1:META]).then_inc(local, 1)
            dve.tensor_copy(dr[:, 1:1 + NMC], rows[32:32 + HA, META + MCH - 1:T_S:MCH]).then_inc(local, 1)
            dve.tensor_copy(dr[:, 1 + NMC:], rows[32:32 + HA, T_S + TS - 1:T:TS]).then_inc(local, 1)
            dve.wait_ge(local, 10)
            dve.sem_inc(dv, 1)
            for c, t0, n in CHN:
                dve.wait_ge(rows_pe, c + 1)
                dve.tensor_copy(col[0:n, c, :], psum[0:n, c % 4, 0:100]).then_inc(cols_ev, 1)
            dve.wait_ge(dec_pe, 1)
            dve.tensor_copy(dec[:], psum[:, 4, 0:HA * 17].rearrange("p (h x) -> p h x", h=HA)).then_inc(dec_ev, 1)

            def step(c, t0, n, u, r):
                last = isinstance(c, int) and c == NMC + 1
                first = isinstance(c, int) and c == 0
                dve.wait_ge(vt, c + 1)
                if not first:
                    dve.wait_ge(upd, c * HA)
                for j in range(2):
                    dve.tensor_copy(va[0:n, 2 * j:2 * j + 2, 0:DV],
                                    psum[0:n, 1 + j, :].rearrange("p (h e) -> p h e", h=2)).then_inc(vas, 1)
                dve.wait_ge(sc, c + 1)
                dve.wait_ge(msk, masked(c))
                if not first:
                    dve.wait_ge(pv, c * HA)
                dve.scalar_tensor_tensor(pr[0:n, :, 0:n], psum[0:n, 0, :].rearrange("p (h t) -> p h t", h=HA)[:, :, 0:n],
                                         QSCALE, ex[0:n, :, 0:n], ALU.mult, ALU.mult).then_inc(prs, 1)
                if last:
                    for hd in range(HA):
                        if hd == 0:
                            dve.wait_ge(c_load[u], r * 64 + 64)
                        else:
                            dve.wait_ge(qcs_h, (c - 1) * HA + hd)
                        dve.tensor_copy(diag_blocks(qm), qc[:, u, hd, :].rearrange("p (b t) -> p b t", t=TS))\
                            .then_inc(qms, 1)
                if not first:
                    dve.wait_ge(ssq, c * HA)
                    dve.wait_ge(hns, c * HA)
                for hd in range(HA):
                    dve.wait_ge(pv, c * HA + hd + 1)
                    o = psum[0:n, 1 + hd % 2, 0:E1]
                    if first:
                        dve.tensor_copy(num[0:n, hd, :], o).then_inc(nums, 1)
                    else:
                        dve.wait_ge(ints, (c - 1) * HA + hd + 1)
                        dve.tensor_tensor(num[0:n, hd, :], inter[0:n, hd, :], o, ALU.add).then_inc(nums, 1)
                dve.wait_ge(nums, c * HA + HA)
                dve.scalar_tensor_tensor(small[0:n, 6, :], num[0:n, :, DV], -1.0, num[0:n, :, DV],
                                         ALU.mult, ALU.max).then_inc(aden, 1)
                dve.wait_ge(aden, c + 1)
                dve.tensor_tensor(small[0:n, 0, :], small[0:n, 6, :], cc[0:n, 64:64 + HA], ALU.max).then_inc(den, 1)
                dve.wait_ge(den, c + 1)
                dve.reciprocal(small[0:n, 1, :], small[0:n, 0, :]).then_inc(rden, 1)
                if not last:
                    dve.wait_ge(dcs, c + 1)
                    for hd in range(HA):
                        dve.wait_ge(upd, c * HA + hd + 1)
                        o = psum[:, 5 if hd % 2 else 0, 0:E1]
                        if first:
                            dve.tensor_copy(C[:, hd, :], o).then_inc(cup, 1)
                        else:
                            dve.scalar_tensor_tensor(C[:, hd, :], C[:, hd, :], dc[:, hd:hd + 1], o,
                                                     ALU.mult, ALU.add).then_inc(cup, 1)
                dve.wait_ge(root, c + 1)
                dve.reciprocal(small[0:n, 4, :], small[0:n, 3, :]).then_inc(rinv, 1)
                dve.wait_ge(rinv, c + 1)
                dve.tensor_tensor(small[0:n, 5, :], small[0:n, 4, :], small[0:n, 1, :], ALU.mult).then_inc(fac, 1)
                dve.wait_ge(fac, c + 1)
                if not first:
                    dve.wait_ge(ht, c * 2)
                for hd in range(HA):
                    dve.tensor_scalar(hn[0:n, hd, :], num[0:n, hd, 0:DV], small[0:n, 5, hd:hd + 1], None, ALU.mult)\
                        .then_inc(hns, 1)
                if last:
                    for n2 in range(NB * HA):
                        hd, b = n2 // NB, n2 % NB
                        dve.wait_ge(cs_pe, n2 + 1)
                        dve.scalar_tensor_tensor(CS[:, b, hd, :], CS[:, b, hd, :], dec[:, hd, 1 + NMC + b:2 + NMC + b],
                                                 psum[:, 5 if n2 % 2 else 0, 0:E1], ALU.mult, ALU.add).then_inc(cs_up, 1)
                for j in range(2):
                    dve.wait_ge(ht, c * 2 + j + 1)
                    o = oc[:, u, 4 * j:4 * j + 4, 0:n]
                    dve.tensor_tensor(o, o, psum[:, 6 + j, :].rearrange("p (k t) -> p k t", k=4)[:, :, 0:n], ALU.mult)\
                        .then_inc(ogs, 1)

            chunks(dve, step)

    with nc.Block() as block:
        @block.sync
        def _(sp):
            sp.dma_start(a["c_p"][0, 0].rearrange("h d e -> d h e"), C[:, :, 0:DV]).then_inc(c_out, 16)
            with nc.allow_non_contiguous_dma("normaliser columns"):
                sp.dma_start(a["n_p"][0, 0].rearrange("h d -> d h"), C[:, :, DV]).then_inc(c_out, 16)
                for b in range(NB):
                    sp.dma_start(a["c_s"][b, 0].rearrange("h d e -> d h e"), CS[:, b, :, 0:DV]).then_inc(c_out, 16)
                    sp.dma_start(a["n_s"][b, 0].rearrange("h d -> d h"), CS[:, b, :, DV]).then_inc(c_out, 16)
            sp.wait_ge(c_out, 16 * (2 + 2 * NB))



def attention(nc, a, s):
    at, sem, psum, ident = s["at"], s["sem"], s["psum"], s["ident"]
    k2_d, vt_d, qr_d, og_d = s["k2_d"], s["vt_d"], s["qr_d"], s["og_d"]
    place = [s["fixed_end"]]

    def sb(name, shape, dt=F32):
        t, place[0] = at("at_" + name, shape, dt, place[0])
        return t

    NU = 2 * KVH
    KW = META + WINDOW
    SK = META + CHUNK + TS
    CACHED = META + CHUNK
    groups = [(0, META), (T_S - WINDOW, WINDOW), (T_S, NS)]
    kk, vv = sb("k_out", [P, 3, 2, P]), sb("v_out", [P, 3, 2, P])
    kv = sb("kv_rows", [P, 3, 2, 2 * P])
    q = sb("q", [P, 2, KD, CHUNK])
    qd = sb("q_decode", [P, 2, KD, TS])
    k = sb("k", [P, 2, KVH, WINDOW])
    v = sb("v", [P, 2, 2, WINDOW])
    km = sb("k_meta", [P, KVH, META])
    vm = sb("v_meta", [P, NU, HD])
    pbm = sb("prob_meta", [P, NU, META])
    vw = sb("v_window", [P, 2 * P])
    pb = sb("prob", [P, NU, KW])
    pt = sb("prob_turned", [P, NU, P])
    pm = sb("prob_meta_turned", [P, P])
    ob = sb("out", [P, 2, KD, CHUNK])
    st = sb("stats", [P, 8, NU])
    sink = sb("sink", [P, NU])
    sinks = sb("sink_decode", [2 * TS, NU])
    kct = sb("k_cached", [SK, 2, 2 * P])
    vct = sb("v_cached", [SK, 2, 2 * P])
    ks = sb("k_decode", [P, KVH, SK])

    kvl, kvt, kve, kvo = (sem("at_kv_" + x) for x in ("loaded", "turned", "evac", "stored"))
    cst, vmz = sem("at_constants_loaded"), sem("at_v_meta_zeroed")
    ld = [sem(f"at_chunk_loaded{u}") for u in range(2)]
    st_o = [sem(f"at_out_stored{u}") for u in range(2)]
    (sc, vt, ptd, pmd, pv) = (sem("at_pe_" + x) for x in ("scores", "v_turned", "p_turned", "p_meta_turned", "values"))
    (ex, es) = (sem("at_act_" + x) for x in ("exp", "sink"))
    (mx, mxs, neg, dsk, den, rdn, nrm, vws, pts, pms, obs) = (sem("at_dve_" + x) for x in (
        "max", "max_sink", "neg_max", "sink_less_max", "den", "rden", "normal", "v_window", "p_turned", "p_meta", "out"))

    with nc.Block() as block:
        @block.sync
        def _(sp):
            for g, (t0, n) in enumerate(groups):
                for t in range(2):
                    for hh in range(2):
                        sp.dma_start(kk[HD * hh:HD * hh + HD, g, t, 0:n], k2_d[2 * t + hh, 0:HD, t0:t0 + n])\
                            .then_inc(kvl, 16)
                    sp.dma_start(vv[:, g, t, 0:n], vt_d[t, :, t0:t0 + n]).then_inc(kvl, 16)
            sp.wait_ge(kve, 6)
            for x, (m, w, d) in enumerate((("meta_k_p", "win_k_p", "win_k_s"), ("meta_v_p", "win_v_p", "win_v_s"))):
                sp.dma_start(a[m][0].rearrange("t h d -> t (h d)"), kv[0:META, 0, x, :]).then_inc(kvo, 16)
                sp.dma_start(a[w][0].rearrange("t h d -> t (h d)"), kv[:, 1, x, :]).then_inc(kvo, 16)
                for b in range(NB):
                    sp.dma_start(a[d][b, WINDOW - TS:WINDOW].rearrange("t h d -> t (h d)"),
                                 kv[TS * b:TS * b + TS, 2, x, :]).then_inc(kvo, 16)
            sp.wait_ge(kvo, 16 * 2 * (2 + NB))

        @block.tensor
        def _(pe):
            pe.wait_ge(kvl, 16 * 18)
            for g, (t0, n) in enumerate(groups):
                for x, src in enumerate((kk, vv)):
                    for t in range(2):
                        y = pe.transpose(psum[0:n, 2 * g + x, t * P:(t + 1) * P], src[:, g, t, 0:n], ident[:])
                    y.then_inc(kvt, 1)

        @block.vector
        def _(dve):
            for g, (t0, n) in enumerate(groups):
                for x in range(2):
                    dve.wait_ge(kvt, 2 * g + x + 1)
                    dve.tensor_copy(kv[0:n, g, x, :], psum[0:n, 2 * g + x, 0:2 * P]).then_inc(kve, 1)

    def softmax_act(act, i, n, banks, per, width):
        act.wait_ge(neg, i + 1)
        if not (isinstance(i, int) and i == 0):
            act.wait_ge(ptd, i)
            act.wait_ge(pmd, i)
        for u in range(NU):
            x = act.activation(pb[0:n, u, 0:width], psum[0:n, banks + u // per, (u % per) * width:(u % per + 1) * width],
                               ACT.Exp, scale=SCORE_SCALE, bias=st[0:n, 2, u:u + 1], accum_out=st[0:n, 3, u:u + 1])
        x.then_inc(ex, 1)
        act.wait_ge(dsk, i + 1)
        act.activation(st[0:n, 5, :], st[0:n, 4, :], ACT.Exp).then_inc(es, 1)

    def softmax_dve(dve, i, n, banks, per, width, snk, meta=None):
        dve.wait_ge(sc, i + 1)
        for b in range(-(-NU // per)):
            m = min(per, NU - b * per)
            x = dve.tensor_reduce(st[0:n, 0, b * per:b * per + m],
                                  psum[0:n, banks + b, 0:m * width].rearrange("p (u k) -> p u k", k=width),
                                  AX_X, ALU.max)
        x.then_inc(mx, 1)
        dve.wait_ge(mx, i + 1)
        dve.scalar_tensor_tensor(st[0:n, 1, :], st[0:n, 0, :], SCORE_SCALE, snk, ALU.mult, ALU.max).then_inc(mxs, 1)
        dve.wait_ge(mxs, i + 1)
        dve.tensor_scalar(st[0:n, 2, :], st[0:n, 1, :], -1.0, None, ALU.mult).then_inc(neg, 1)
        dve.tensor_tensor(st[0:n, 4, :], snk, st[0:n, 1, :], ALU.subtract).then_inc(dsk, 1)
        dve.wait_ge(ex, i + 1)
        dve.wait_ge(es, i + 1)
        dve.tensor_tensor(st[0:n, 6, :], st[0:n, 3, :], st[0:n, 5, :], ALU.add).then_inc(den, 1)
        dve.wait_ge(den, i + 1)
        dve.reciprocal(st[0:n, 7, :], st[0:n, 6, :]).then_inc(rdn, 1)
        dve.wait_ge(rdn, i + 1)
        first = META if meta is not None else 0
        p = pb[0:n, :, first:width]
        if meta is not None:
            if not (isinstance(i, int) and i == 0):
                dve.wait_ge(pmd, i)
            dve.tensor_tensor(meta[:], pb[:, :, 0:META], st[:, 7, :].unsqueeze(2).to_broadcast([P, NU, META]), ALU.mult)
        width -= first
        dve.tensor_tensor(p, p, st[0:n, 7, :].unsqueeze(2).to_broadcast([n, NU, width]), ALU.mult).then_inc(nrm, 1)

    def steps(eng, body):
        body(0, CHUNK, 0, 0)
        body(1, WINDOW, 1, 0)
        with eng.Fori(1, SEQ // CHUNK // 2) as i:
            for u in range(2):
                body(i * 2 + u, WINDOW, u, i)

    NP = SEQ // CHUNK

    with nc.Block() as block:
        @block.sync
        def _(sp):
            with nc.allow_non_contiguous_dma("sinks"):
                for j in range(2):
                    for half in range(2):
                        src = a["b_sinks"].rearrange("a (k j p) -> a k j p", j=2, p=2)[0:1, :, j, half]
                        for dst, m in ((sink, CHUNK), (sinks, TS)):
                            sp.dma_start(dst[j * m:(j + 1) * m, KVH * half:KVH * half + KVH],
                                         src.to_broadcast([m, KVH])).then_inc(cst, 16)
            sp.wait_ge(vmz, 1)
            for un in range(NU):
                sp.dma_start(vm[META * un:META * un + META, un, :], a["meta_v_p"][0, :, un % KVH, :])\
                    .then_inc(cst, 16)
            sp.dma_start(km[:], k2_d[:, :, 0:META].rearrange("h p t -> p h t")).then_inc(cst, 16)

            def load(i, w, u, r):
                if not (isinstance(i, int) and i < 2):
                    sp.wait_ge(st_o[u], r * 16)
                t = META + CHUNK * i if isinstance(i, int) else i * CHUNK + META
                w0 = t + CHUNK - w
                sp.dma_start(q[:, u], qr_d[:, :, ds(t, CHUNK)].rearrange("j p t -> p j t")).then_inc(ld[u], 16)
                sp.dma_start(k[:, u, :, 0:w], k2_d[:, :, ds(w0, w)].rearrange("j p t -> p j t")).then_inc(ld[u], 16)
                sp.dma_start(v[:, u, :, 0:w], vt_d[:, :, ds(w0, w)].rearrange("j p t -> p j t")).then_inc(ld[u], 16)

            steps(sp, load)

        @block.gpsimd
        def _(pool):
            pool.memset(vm[:], 0.0).then_inc(vmz, 1)

        @block.tensor
        def _(pe):
            pe.wait_ge(cst, 16 * 17)

            def step(i, w, u, r):
                first = isinstance(i, int) and i == 0
                pe.wait_ge(ld[u], r * 48 + 48)
                if not first:
                    pe.wait_ge(ex, i)
                for un in range(NU):
                    kh, half = un % KVH, HD * (un // KVH)
                    ql = q[half:half + HD, u, 2 * kh:2 * kh + 2, :]
                    o = psum[:, un // 2, (un % 2) * (META + w):(un % 2 + 1) * (META + w)]
                    pe.matmul(o[:, 0:META], ql, km[half:half + HD, kh, :], start=True, stop=True)
                    x = pe.matmul(o[:, META:META + w], ql, k[half:half + HD, u, kh, 0:w], start=True, stop=True)
                x.then_inc(sc, 1)
                if not first:
                    pe.wait_ge(obs, i)
                for t in range(2):
                    x = pe.transpose(psum[0:w, 7, t * P:(t + 1) * P], v[:, u, t, 0:w], ident[:])
                x.then_inc(vt, 1)
                pe.wait_ge(nrm, i + 1)
                if not first:
                    pe.wait_ge(pts, i * 2)
                    pe.wait_ge(pms, i)
                for un in range(NU):
                    x = pe.transpose(psum[0:w, 4 + un // 4, (un % 4) * P:(un % 4 + 1) * P], pb[:, un, META:META + w],
                                     ident[:])
                x.then_inc(ptd, 1)
                pe.transpose(psum[:, 6, 0:P], pbm[:].rearrange("p u k -> p (u k)"), ident[:]).then_inc(pmd, 1)
                pe.wait_ge(vws, i + 1)
                pe.wait_ge(pts, i * 2 + 2)
                pe.wait_ge(pms, i + 1)
                for un in range(NU):
                    kh, half = un % KVH, HD * (un // KVH)
                    o = psum[half:half + HD, 7, kh * P:(kh + 1) * P]
                    pe.matmul(o, vw[0:w, kh * HD:(kh + 1) * HD], pt[0:w, un, :], start=True, stop=False)
                    x = pe.matmul(o, vm[:, un, :], pm[:], start=False, stop=True)
                x.then_inc(pv, 1)

            steps(pe, step)

        @block.scalar
        def _(act):
            def step(i, w, u, r):
                softmax_act(act, i, P, 0, 2, META + w)
                act.wait_ge(pmd, i + 1)
                if not (isinstance(i, int) and i == 0):
                    act.wait_ge(pv, i)
                act.activation(pm[:], psum[:, 6, 0:P], ACT.Copy).then_inc(pms, 1)
                act.wait_ge(obs, i + 1)
                t = META + CHUNK * i if isinstance(i, int) else i * CHUNK + META
                act.dma_start(og_d[:, :, ds(t, CHUNK)].rearrange("j p t -> p j t"), ob[:, u]).then_inc(st_o[u], 16)

            steps(act, step)
            for u in range(2):
                act.wait_ge(st_o[u], 16 * NP // 2)

        @block.vector
        def _(dve):
            dve.wait_ge(cst, 16 * 17)

            def step(i, w, u, r):
                first = isinstance(i, int) and i == 0
                softmax_dve(dve, i, P, 0, 2, META + w, sink[:], pbm)
                dve.wait_ge(vt, i + 1)
                if not first:
                    dve.wait_ge(pv, i)
                dve.tensor_copy(vw[0:w, :], psum[0:w, 7, 0:2 * P]).then_inc(vws, 1)
                dve.wait_ge(ptd, i + 1)
                for j in range(2):
                    dve.tensor_copy(pt[0:w, 4 * j:4 * j + 4, :],
                                    psum[0:w, 4 + j, :].rearrange("p (u r) -> p u r", u=4)).then_inc(pts, 1)
                dve.wait_ge(pv, i + 1)
                if not (isinstance(i, int) and i < 2):
                    dve.wait_ge(st_o[u], r * 16)
                dve.tensor_copy(ob[:, u], psum[:, 7, :].rearrange("p (j t) -> p j t", j=KD)).then_inc(obs, 1)

            steps(dve, step)

    dl = [sem(f"at_decode_loaded{u}") for u in range(2)]
    ds_o = [sem(f"at_decode_stored{u}") for u in range(2)]
    kct_t, kse = sem("at_pe_k_decode_turned"), sem("at_dve_k_decode")
    with nc.Block() as block:
        def seqs(eng, body):
            for b in range(NB):
                body(b, NP + b, b % 2, b // 2)

        @block.sync
        def _(sp):
            def load(b, i, u, r):
                if not (isinstance(b, int) and b < 2):
                    sp.wait_ge(ds_o[u], r * 16)
                t = T_S + TS * b if isinstance(b, int) else b * TS + T_S
                sp.dma_start(qd[:, u], qr_d[:, :, ds(t, TS)].rearrange("j p t -> p j t")).then_inc(dl[u], 16)
                for dst, meta, win, new in ((kct, "cache_meta_k", "cache_win_k", "win_k_s"),
                                            (vct, "cache_meta_v", "cache_win_v", "win_v_s")):
                    flat = lambda x, lo, hi: x[ds(b, 1), lo:hi].rearrange("a t h d -> (a t) (h d)")
                    sp.dma_start(dst[0:META, u, :], flat(a[meta], 0, META)).then_inc(dl[u], 16)
                    sp.dma_start(dst[META:CACHED, u, :], flat(a[win], WINDOW - CHUNK, WINDOW)).then_inc(dl[u], 16)
                    sp.dma_start(dst[CACHED:SK, u, :], flat(a[new], WINDOW - TS, WINDOW)).then_inc(dl[u], 16)

            seqs(sp, load)

        R = 2 * TS

        @block.tensor
        def _(pe):
            def step(b, i, u, r):
                first = isinstance(b, int) and b == 0
                pe.wait_ge(dl[u], r * 112 + 112)
                if not first:
                    pe.wait_ge(kse, b)
                for t in range(2):
                    x = pe.transpose(psum[:, 6, t * P:t * P + SK], kct[:, u, t * P:(t + 1) * P], ident[0:SK, 0:SK])
                x.then_inc(kct_t, 1)
                pe.wait_ge(kse, b + 1)
                if not first:
                    pe.wait_ge(ex, i)
                for un in range(NU):
                    kh, half = un % KVH, HD * (un // KVH)
                    x = pe.matmul(psum[0:R, un // 4, (un % 4) * SK:(un % 4 + 1) * SK],
                                  qd[half:half + HD, u, 2 * kh:2 * kh + 2, :], ks[half:half + HD, kh, :],
                                  start=True, stop=True)
                x.then_inc(sc, 1)
                pe.wait_ge(nrm, i + 1)
                if not first:
                    pe.wait_ge(pts, b + 2 * NP)
                for un in range(NU):
                    x = pe.transpose(psum[0:SK, 3, un * R:(un + 1) * R], pb[0:R, un, 0:SK], ident[0:R, 0:R])
                x.then_inc(ptd, 1)
                pe.sem_inc(pmd, 1)
                pe.wait_ge(pts, b + (2 * NP + 1))
                if not first:
                    pe.wait_ge(obs, i)
                for un in range(NU):
                    kh, half = un % KVH, HD * (un // KVH)
                    x = pe.matmul(psum[half:half + HD, 7, kh * R:(kh + 1) * R], vct[:, u, kh * HD:(kh + 1) * HD],
                                  pt[0:SK, un, 0:R], start=True, stop=True)
                x.then_inc(pv, 1)

            seqs(pe, step)

        @block.scalar
        def _(act):
            def step(b, i, u, r):
                softmax_act(act, i, R, 0, 4, SK)
                act.wait_ge(obs, i + 1)
                t = T_S + TS * b if isinstance(b, int) else b * TS + T_S
                act.dma_start(og_d[:, :, ds(t, TS)].rearrange("j p t -> p j t"), ob[:, u, :, 0:TS])\
                    .then_inc(ds_o[u], 16)

            seqs(act, step)
            for u in range(2):
                act.wait_ge(ds_o[u], 16 * NB // 2)

        @block.vector
        def _(dve):
            def step(b, i, u, r):
                first = isinstance(b, int) and b == 0
                dve.wait_ge(kct_t, b + 1)
                if not first:
                    dve.wait_ge(sc, i)
                for kh in range(KVH):
                    for dup in range(2):
                        x = dve.tensor_copy(ks[HD * dup:HD * dup + HD, kh, :],
                                            psum[HD * (kh % 2):HD * (kh % 2) + HD, 6, (kh // 2) * P:(kh // 2) * P + SK])
                x.then_inc(kse, 1)
                softmax_dve(dve, i, R, 0, 4, SK, sinks[:])
                dve.wait_ge(ptd, i + 1)
                dve.wait_ge(pv, i)
                dve.tensor_copy(pt[0:SK, :, 0:R], psum[0:SK, 3, 0:NU * R].rearrange("p (u r) -> p u r", u=NU))\
                    .then_inc(pts, 1)
                dve.wait_ge(pv, i + 1)
                if not (isinstance(b, int) and b < 2):
                    dve.wait_ge(ds_o[u], r * 16)
                dve.tensor_copy(ob[:, u, :, 0:TS], psum[:, 7, 0:NU // 2 * R].rearrange("p (j t) -> p j t", j=KD))\
                    .then_inc(obs, 1)

            seqs(dve, step)


def final(nc, a, s):
    at, sem, psum, ident, ones, h = s["at"], s["sem"], s["psum"], s["ident"], s["ones"], s["h"]
    epsc = s["epsc"]
    gf, e = at("fi_gain", [P, D], F32, s["fixed_end"])
    y, e = at("fi_y", [P, 3, D], F32, e)
    junk, e = at("fi_junk", [P, 512], F32, e)
    ss, e = at("fi_sums", [P, 9, 5], F32, e)
    gl = sem("fi_gain_loaded")
    turned, sqr, tot, root, rs, ev = (sem("fi_" + x) for x in ("turned", "squares", "sum", "root", "rstd", "evac"))
    sto = [sem(f"fi_stored{i}") for i in range(3)]
    NT = (T - META) // P
    with nc.Block() as block:
        @block.sync
        def _(sp):
            sp.dma_start(gf[:], a["g_final"].rearrange("(a d) -> a d", a=1).to_broadcast([P, D])).then_inc(gl, 16)
            for i in range(NT):
                sp.wait_ge(ev, 2 * i + 2)
                dst = a["y_p"][0, i * P:(i + 1) * P, :] if i < NT - 1 else a["y_s"].rearrange("b t d -> (b t) d")
                sp.dma_start(dst, y[:, i % 3, :]).then_inc(sto[i % 3], 16)
            for b in range(3):
                sp.wait_ge(sto[b], 16 * (NT // 3))

        @block.tensor
        def _(pe):
            for i in range(NT):
                for half in range(2):
                    u = 2 * i + half
                    if i >= 4:
                        pe.wait_ge(ev, u - 7)
                    for k in range(4):
                        x = pe.transpose(psum[:, u % 8, k * P:(k + 1) * P],
                                         h[:, 4 * half + k, META + i * P:META + (i + 1) * P], ident[:])
                    x.then_inc(turned, 1)

        @block.scalar
        def _(act):
            for i in range(NT):
                for half in range(2):
                    u = 2 * i + half
                    act.wait_ge(turned, u + 1)
                    if u:
                        act.wait_ge(sqr, u)
                    act.activation(junk[:], psum[:, u % 8, :], ACT.Square, accum_out=ss[:, i, half:half + 1])\
                        .then_inc(sqr, 1)
                act.wait_ge(tot, i + 1)
                act.activation(ss[:, i, 3:4], ss[:, i, 2:3], ACT.Sqrt, scale=1.0 / D, bias=epsc[:, 0:1]).then_inc(root, 1)

        @block.vector
        def _(dve):
            dve.wait_ge(gl, 16)
            for i in range(NT):
                dve.wait_ge(sqr, 2 * i + 2)
                dve.tensor_tensor(ss[:, i, 2:3], ss[:, i, 0:1], ss[:, i, 1:2], ALU.add).then_inc(tot, 1)
                dve.wait_ge(root, i + 1)
                dve.reciprocal(ss[:, i, 4:5], ss[:, i, 3:4]).then_inc(rs, 1)
                dve.wait_ge(rs, i + 1)
                if i >= 3:
                    dve.wait_ge(sto[i % 3], 16 * (i // 3))
                for half in range(2):
                    w = slice(512 * half, 512 * half + 512)
                    dve.scalar_tensor_tensor(y[:, i % 3, w], psum[:, (2 * i + half) % 8, :], ss[:, i, 4:5], gf[:, w],
                                             ALU.mult, ALU.mult).then_inc(ev, 1)



OUTS = [("y_p", (1, SEQ, D)), ("y_s", (NB, TS, D)),
        ("c_p", (1, 1, HA, DQK, DV)), ("n_p", (1, 1, HA, DQK)), ("m_p", (1, 1, HA)),
        ("meta_k_p", (1, META, KVH, HD)), ("meta_v_p", (1, META, KVH, HD)),
        ("win_k_p", (1, WINDOW, KVH, HD)), ("win_v_p", (1, WINDOW, KVH, HD)),
        ("c_s", (NB, 1, HA, DQK, DV)), ("n_s", (NB, 1, HA, DQK)), ("m_s", (NB, 1, HA)),
        ("win_k_s", (NB, WINDOW, KVH, HD)), ("win_v_s", (NB, WINDOW, KVH, HD))]


def rotary_tables():
    pos = np.concatenate([np.arange(T_S), np.tile(META + PAST + np.arange(TS), NB)]).astype(np.float32)
    half = HD // 2
    inv = (np.float32(10000.0) ** (-np.arange(half, dtype=np.float32) / np.float32(half))).astype(np.float32)
    ang = (pos[None, :] * inv[:, None]).astype(np.float32).astype(np.float64)
    cos, sin = np.cos(ang).astype(np.float32), np.sin(ang).astype(np.float32)
    return np.concatenate([cos] * 4), np.concatenate([-sin, sin] * 2)


def host_inputs(inputs):
    arrays = {n: np.ascontiguousarray(v) for n, v in inputs.items()}
    arrays["rope_cos"], arrays["rope_sin"] = rotary_tables()
    return arrays


def kernel(**inputs):
    import concourse.bacc as bacc
    from concourse.bass_utils import run_bass_kernel_spmd

    nc = bacc.Bacc("TRN2", target_bir_lowering=False, num_devices=1)
    arrays, aps = {}, {}
    for n, v in host_inputs(inputs).items():
        arrays["in_" + n] = v
        aps[n] = nc.dram_tensor("in_" + n, v.shape, mybir.dt.from_np(v.dtype), kind="ExternalInput").ap()
    for n, shape in OUTS:
        aps[n] = nc.dram_tensor(n, shape, F32, kind="ExternalOutput").ap()
    build(nc, aps)
    r = run_bass_kernel_spmd(nc, [arrays], core_ids=[0])
    return tuple(r.results[0][n] for n, _ in OUTS)
```

```python
from contextlib import ExitStack

import numpy as np

import concourse.bass as bass
from concourse import mybir
from concourse.alu_op_type import AluOpType as ALU

F32 = mybir.dt.float32
F32R = mybir.dt.float32r
ACT = mybir.ActivationFunctionType
AX_X = mybir.AxisListType.X
ds = bass.ds

P = 128
D = 1024
KD = D // P
META, SEQ, NB, TS = 16, 1024, 8, 16
NS = NB * TS
T = META + SEQ + NS
T_S = META + SEQ
TOK = [(0, 400), (400, 384), (784, 384)]
HA, DQK, DV = 4, 128, 256
QSCALE = DQK ** -0.5
DFF = 2816
HD, KVH = 64, 4
CHUNK, WINDOW, PAST = 64, 128, 512
EPS = 1e-6
SCORE_SCALE = HD ** -0.5
MCH = 128
NMC = SEQ // MCH


class Group:

    def __init__(self, n0, pairs, weight, gain, kind):
        self.n0, self.pairs, self.weight, self.gain, self.kind = n0, pairs, weight, gain, kind


def over(eng, groups, body):
    for g in groups:
        if g.pairs == 1:
            for u in range(2):
                body(g, u, g.n0 + u, u, g.n0 // 2)
        else:
            with eng.Fori(0, g.pairs) as i:
                for u in range(2):
                    body(g, 2 * i + u, g.n0 + 2 * i + u, u, i + g.n0 // 2)


def build(nc, a, upto=99):
    ctx = ExitStack()
    with ctx:
        _build(nc, a, ctx, upto)


def _build(nc, a, ctx, upto):
    base = [(nc.sbuf_base + 31) // 32 * 32]
    limit = nc.sbuf_usable_end

    def at(name, shape, dt=F32, offset=0):
        n = int(np.prod(shape[1:])) * 4
        assert offset + n <= limit, (name, offset + n, limit)
        return nc.alloc_sbuf_tensor_at(name, shape, dt, offset=offset), offset + (n + 31) // 32 * 32

    def sb(name, shape, dt=F32):
        t, base[0] = at(name, shape, dt, base[0])
        return t

    phase = [None]

    def sem(name):
        phase[0].append(nc.alloc_semaphore(name))
        return phase[0][-1]

    def run(step, *args, **kw):
        phase[0] = []
        step(*args, **kw)
        nc.clear_and_free_semaphores(phase[0])
        nc.all_engine_barrier()

    def dram(name, shape):
        return nc.dram_tensor(name, shape, F32, kind="Internal").ap()

    h = sb("h", [P, KD, T])
    rstd = sb("rstd", [P, T])
    ident = sb("ident", [P, P])
    ones = sb("ones", [P, P])
    gains = sb("gains", [P, 6, KD])
    epsc = sb("epsc", [P, 1])
    powc = sb("minus_half", [P, 1])
    raw = sb("raw", [P, 2, D])
    wh = sb("wh", [P, 3, D], F32R)
    wl = sb("wl", [P, 3, D], F32R)
    fixed_end = base[0]

    xh = sb("xh", [P, KD, T], F32R)
    xl = sb("xl", [P, KD, T], F32R)
    x_end = base[0]
    sq_at = base[0]
    sq = sb("sq", [P, 2, T])
    acc = sb("acc", [P, T])
    dense_end = base[0]
    tmp, e1 = at("tmp", [P, 2, T], F32, dense_end)
    swp, e2 = at("swp", [P, T], F32, e1)
    hidh, e1b = at("hidh", [P, 2, T], F32R, dense_end)
    hidl, e2b = at("hidl", [P, 2, T], F32R, e1b)
    cosr, e3 = at("cosr", [P, T], F32, e2)
    sinr, e4 = at("sinr", [P, T], F32, e3)
    gate, up_at = at("gate", [P, T], F32, sq_at)
    up, _ = at("up", [P, T], F32, up_at)

    qkvo = dram("qkvo", (24, P, T))
    gates_d = dram("gates_d", (2, 4, T))
    og_d = dram("og_d", (KD, P, T))
    k2_d = dram("k2_d", (KVH, P, T))
    vt_d = dram("vt_d", (2, P, T))
    qr_d = dram("qr_d", (KD, P, T))

    psum = ctx.enter_context(nc.psum_tensor("psum", [P, 8, 512], F32))

    unit = ones[:, 0:1].to_broadcast([P, D])

    def wcols(w, col0=0):
        v = w.rearrange("(k p) n -> p k n", p=P)
        return lambda j: v[:, :, ds(j * P + col0, P)]

    def weight_tile(b):
        return b.rearrange("p (k n) -> p k n", k=KD)

    class Prefetch:

        def __init__(self, name, tiles):
            self.tiles = tiles
            self.loaded = [sem(f"{name}_next_w_loaded{u}") for u in range(2)]
            self.scaled, self.hi, self.lo = (sem(f"{name}_next_w_{x}") for x in ("scaled", "hi", "split"))

        def load(self, sp, u):
            sp.dma_start(weight_tile(raw[:, u, :]), self.tiles[u][0]).then_inc(self.loaded[u], 16)

        def scale(self, pool, u):
            pool.wait_ge(self.loaded[u], 16)
            if self.tiles[u][1] is not None:
                pool.tensor_tensor(weight_tile(raw[:, u, :]), weight_tile(raw[:, u, :]),
                                   gains[:, self.tiles[u][1], :].unsqueeze(2).to_broadcast([P, KD, P]),
                                   ALU.mult).then_inc(self.scaled, 1)
            else:
                pool.sem_inc(self.scaled, 1)
            pool.wait_ge(self.scaled, u + 1)

        def split(self, pool, u):
            pool.tensor_tensor(wh[:, u, :], raw[:, u, :], unit, ALU.mult).then_inc(self.hi, 1)
            pool.wait_ge(self.hi, u + 1)
            pool.tensor_tensor(wl[:, u, :], raw[:, u, :], wh[:, u, :].bitcast(F32), ALU.subtract)\
                .then_inc(self.lo, 1)

    def setup(following):
        xin, e = at("xin", [P, 10, D], F32, x_end)
        identw = sem("su_ident")
        const = sem("su_const")
        loads = [sem(f"su_x{i}") for i in range(2)]
        gl = sem("su_gains")
        copies = sem("su_cache_copies")
        turned = sem("su_turned")
        placed = sem("su_placed")
        nx = Prefetch("su", following)
        with nc.Block() as block:
            @block.sync
            def _(sp):
                for i in range(8):
                    sp.dma_start(xin[:, i, :], a["x_prompt"][0, i * P:(i + 1) * P, :]).then_inc(loads[i // 4], 16)
                sp.dma_start(xin[:, 8, :], a["x_sample"].rearrange("b t d -> (b t) d")).then_inc(loads[1], 16)
                sp.dma_start(xin[0:META, 9, :], a["meta_tokens"]).then_inc(loads[1], 16)
                nx.load(sp, 0)
                nx.load(sp, 1)
                for w, c in (("win_k_s", "cache_win_k"), ("win_v_s", "cache_win_v")):
                    sp.dma_start(a[w][:, 0:WINDOW - TS], a[c][:, TS:WINDOW]).then_inc(copies, 16)
                sp.wait_ge(copies, 32)

            @block.scalar
            def _(act):
                for n, g in enumerate((a["norm_mix"][0], a["a_g_head"][0], a["norm_ffn"][0], a["g_kv"],
                                       a["norm_mix"][1], a["norm_ffn"][1])):
                    with nc.allow_non_contiguous_dma("gain columns"):
                        act.dma_start(gains[:, n, :], g.rearrange("(k p) -> p k", p=P)).then_inc(gl, 16)
                act.wait_ge(gl, 96)

            @block.gpsimd
            def _(pool):
                pool.memset(ident[:], 0.0).then_inc(identw, 1)
                pool.wait_ge(identw, 1)
                pool.affine_select(out=ident[:], in_=ident[:], compare_op=ALU.not_equal, fill=1.0, base=0,
                                   pattern=[[-1, P]], channel_multiplier=1).then_inc(const, 1)
                pool.memset(ones[:], 1.0).then_inc(const, 1)
                pool.memset(epsc[:], EPS).then_inc(const, 1)
                pool.memset(powc[:], -0.5).then_inc(const, 1)
                pool.wait_ge(const, 4)
                pool.wait_ge(gl, 96)
                for u in range(2):
                    nx.scale(pool, u)
                    nx.split(pool, u)

            @block.tensor
            def _(pe):
                pe.wait_ge(const, 4)
                for i in range(10):
                    n = META if i == 9 else P
                    if i == 0:
                        pe.wait_ge(loads[0], 16 * 4)
                    if i == 4:
                        pe.wait_ge(loads[1], 16 * 6)
                    for half in range(2):
                        u = 2 * i + half
                        if u >= 8:
                            pe.wait_ge(placed, u - 7)
                        for k in range(4):
                            t = pe.transpose(psum[:, u % 8, k * P:k * P + n],
                                             xin[0:n, i, (4 * half + k) * P:(4 * half + k + 1) * P], ident[0:n, 0:n])
                        t.then_inc(turned, 1)

            @block.vector
            def _(dve):
                for i in range(10):
                    n = META if i == 9 else P
                    col = 0 if i == 9 else META + i * P
                    for half in range(2):
                        u = 2 * i + half
                        dve.wait_ge(turned, u + 1)
                        dve.tensor_copy(h[:, 4 * half:4 * half + 4, col:col + n],
                                        psum[:, u % 8, :].rearrange("p (k t) -> p k t", k=4)[:, :, 0:n])\
                            .then_inc(placed, 1)

    class Prep:

        def __init__(self, name):
            self.hi, self.lo = sem(name + "_x_hi"), sem(name + "_x_lo")
            self.sq, self.summed = sem(name + "_squared"), sem(name + "_summed")
            self.total, self.root, self.rstd = sem(name + "_total"), sem(name + "_root"), sem(name + "_rstd")

        def act_split(self, act):
            for k in range(KD):
                act.activation(xh[:, k, :], h[:, k, :], ACT.Copy).then_inc(self.hi, 1)
            for k in range(KD):
                if k >= 2:
                    act.wait_ge(self.summed, k - 1)
                act.activation(sq[:, k % 2, :], h[:, k, :], ACT.Square).then_inc(self.sq, 1)

        def act_root(self, act):
            for c, (t0, n) in enumerate(TOK):
                act.wait_ge(self.total, c + 1)
                act.activation(rstd[:, t0:t0 + n], psum[:, 6 + c % 2, 0:n], ACT.Sqrt, scale=1.0 / D,
                               bias=epsc[:, 0:1]).then_inc(self.root, 1)

        def dve_split(self, dve):
            for k in range(KD):
                dve.wait_ge(self.hi, k + 1)
                dve.tensor_tensor(xl[:, k, :], h[:, k, :], xh[:, k, :].bitcast(F32), ALU.subtract)\
                    .then_inc(self.lo, 1)
            for k in range(KD):
                dve.wait_ge(self.sq, k + 1)
                if k == 0:
                    dve.tensor_copy(acc[:], sq[:, 0, :]).then_inc(self.summed, 1)
                else:
                    dve.wait_ge(self.summed, k)
                    dve.tensor_tensor(acc[:], acc[:], sq[:, k % 2, :], ALU.add).then_inc(self.summed, 1)

        def dve_rstd(self, dve):
            for c, (t0, n) in enumerate(TOK):
                dve.wait_ge(self.root, c + 1)
                dve.reciprocal(rstd[:, t0:t0 + n], rstd[:, t0:t0 + n]).then_inc(self.rstd, 1)

        def pe_total(self, pe):
            pe.wait_ge(self.summed, KD)
            for c, (t0, n) in enumerate(TOK):
                if c == 2:
                    pe.wait_ge(self.root, 1)
                pe.matmul(psum[:, 6 + c % 2, 0:n], ones[:], acc[:, t0:t0 + n], start=True, stop=True)\
                    .then_inc(self.total, 1)

    BETWEEN = 6

    def product(pe, bank, hi, lo, nk, bh, bl, ready=None, between=None):
        for k in range(nk):
            if ready is not None:
                pe.wait_ge(ready, k + 1)
            if between is not None and k == BETWEEN:
                between(pe)
            for n, (w, x) in enumerate(((hi, bh), (hi, bl), (lo, bh))):
                for c, (t0, nt) in enumerate(TOK):
                    mm = pe.matmul(psum[:, bank + c, 0:nt], w(k), x[:, k, t0:t0 + nt],
                                   start=(k == 0 and n == 0), stop=(k == nk - 1 and n == 2))
        return mm

    def dense(name, groups, following, prep=None, gates=None, load_x=None, tables=None):
        njobs = sum(2 * g.pairs for g in groups) + (1 if gates is not None else 0)
        loaded = [sem(f"{name}_w_loaded{u}") for u in range(2)]
        stored = [sem(f"{name}_stored{u}") for u in range(2)]
        scaled, hi_s, split = (sem(f"{name}_w_{x}") for x in ("scaled", "hi", "split"))
        job_done, evac, sig = (sem(f"{name}_{x}") for x in ("job_done", "evac", "activated"))
        swapped, part, xr, gm = (sem(f"{name}_{x}") for x in ("swapped", "part", "x_ready", "gate_memset"))
        xload = [sem(f"{name}_x_loaded{u}") for u in range(2)]
        tab = sem(f"{name}_tables")
        trot = sem(f"{name}_tables_scaled")
        gst = sem(f"{name}_gates_stored")
        gainful = any(g.gain is not None for g in groups)
        storing = groups[0].kind != "residual"
        pr = Prep(name) if prep else None
        nx = Prefetch(name, following) if following else None
        nst = [0]
        G = njobs - 1
        hi_x = sem(f"{name}_x_hi2")

        def stored_before(r):
            return r * 16 + (48 if groups[0].kind == "rope_k" else 0)

        with nc.Block() as block:
            @block.sync
            def _(sp):
                if tables is not None:
                    sp.dma_start(cosr[:], a["rope_cos"]).then_inc(tab, 16)
                    sp.dma_start(sinr[:], a["rope_sin"]).then_inc(tab, 16)

                def load(g, j, n, u, r):
                    if isinstance(n, int) and n < 2:
                        sp.sem_inc(loaded[u], 16)
                        return
                    sp.wait_ge(split, n - 1)
                    sp.dma_start(weight_tile(raw[:, u, :]), g.weight(j)).then_inc(loaded[u], 16)

                over(sp, groups, load)
                if gates is not None:
                    sp.wait_ge(gm, 1)
                    for half in range(2):
                        sp.dma_start(weight_tile(raw[:, 0, :])[:, :, 32 * half:32 * half + HA],
                                     gates[:, :, HA * half:HA * half + HA]).then_inc(loaded[0], 16)
                if nx:
                    for u in range(2):
                        sp.wait_ge(split, njobs - 1 + (u ^ njobs % 2))
                        nx.load(sp, u)

            @block.gpsimd
            def _(pool):
                def split_w(g, j, n, u, r, gate_tile=False):
                    pool.wait_ge(loaded[u], r * 16 + (32 if gate_tile else 16))
                    if isinstance(n, int) and n < 2:
                        for x in (scaled, hi_s, split):
                            pool.sem_inc(x, 1)
                        return
                    if g.gain is not None:
                        pool.tensor_tensor(weight_tile(raw[:, u, :]), weight_tile(raw[:, u, :]),
                                           gains[:, g.gain, :].unsqueeze(2).to_broadcast([P, KD, P]),
                                           ALU.mult).then_inc(scaled, 1)
                        pool.wait_ge(scaled, n + 1)
                    if not (isinstance(n, int) and n < 2):
                        pool.wait_ge(job_done, n - 1)
                    pool.tensor_tensor(wh[:, u, :], raw[:, u, :], unit, ALU.mult).then_inc(hi_s, 1)
                    pool.wait_ge(hi_s, n + 1)
                    pool.tensor_tensor(wl[:, u, :], raw[:, u, :], wh[:, u, :].bitcast(F32), ALU.subtract)\
                        .then_inc(split, 1)

                over(pool, groups, split_w)
                if gates is not None:
                    pool.memset(raw[:, 0, :], 0.0).then_inc(gm, 1)
                    split_w(groups[0], None, G, 0, G // 2, gate_tile=True)
                if nx:
                    for u in range(2):
                        nx.scale(pool, u)
                        pool.wait_ge(job_done, njobs - 1 + (u ^ njobs % 2))
                        nx.split(pool, u)

            @block.tensor
            def _(pe):
                def job(g, j, n, u, r, ready=None):
                    pe.wait_ge(split, n + 1)
                    if not (isinstance(n, int) and n < 2):
                        pe.wait_ge(evac, n - 1)
                    hi, lo = weight_tile(wh[:, u, :]), weight_tile(wl[:, u, :])
                    if ready is None and isinstance(n, int) and n == 0:
                        ready = pr.lo if pr else (xr if load_x is not None else None)
                    product(pe, 3 * u, lambda k: hi[:, k, :], lambda k: lo[:, k, :], KD, xh, xl, ready,
                            pr.pe_total if isinstance(n, int) and n == 1 and pr else None).then_inc(job_done, 1)

                over(pe, groups, job)
                if gates is not None:
                    job(None, None, G, 0, G // 2)

            @block.scalar
            def _(act):
                if load_x is not None:
                    for k in range(KD + 1):
                        if k < KD:
                            if k >= 2:
                                act.wait_ge(xr, k - 1)
                            act.dma_start(sq[:, k % 2, :], load_x[k]).then_inc(xload[k % 2], 16)
                        if k >= 1:
                            act.wait_ge(xload[(k - 1) % 2], 16 * ((k - 1) // 2 + 1))
                            act.activation(xh[:, k - 1, :], sq[:, (k - 1) % 2, :], ACT.Copy).then_inc(hi_x, 1)
                if pr:
                    pr.act_split(act)
                    pr.act_root(act)

                def finish(g, j, n, u, r):
                    if g.kind == "sigmoid":
                        act.wait_ge(part, n - g.n0 + 1)
                        act.activation(tmp[:, u, :], tmp[:, u, :], ACT.Sigmoid).then_inc(sig, 1)
                        act.wait_ge(sig, n - g.n0 + 1)
                        act.dma_start(qkvo[ds(j + g.n0, 1)].rearrange("a p t -> (a p) t"), tmp[:, u, :])\
                            .then_inc(stored[u], 16)
                    elif g.kind == "store":
                        act.wait_ge(evac, n + 1)
                        act.dma_start(qkvo[ds(j + g.n0, 1)].rearrange("a p t -> (a p) t"), tmp[:, u, :])\
                            .then_inc(stored[u], 16)
                    elif g.kind in ("rope_k", "rope_q"):
                        act.wait_ge(part, n + 1 if g.n0 == 0 else n - 1)
                        if not (isinstance(n, int) and n == 0):
                            act.wait_ge(evac, n)
                        for q in range(4):
                            o, i = 32 * q, 32 * (q ^ 1)
                            for c, (t0, nt) in enumerate(TOK):
                                x = act.activation(swp[o:o + 32, t0:t0 + nt], psum[i:i + 32, 3 * u + c, 0:nt],
                                                   ACT.Copy)
                        x.then_inc(swapped, 1)
                        act.wait_ge(evac, n + 1)
                        if g.kind == "rope_k":
                            for hh in range(2):
                                for dup in range(2):
                                    act.dma_start(k2_d[2 * j + hh, HD * dup:HD * dup + HD, :],
                                                  tmp[HD * hh:HD * hh + HD, u, :]).then_inc(stored[u], 16)
                        else:
                            act.dma_start(qr_d[ds(j, 1)].rearrange("a p t -> (a p) t"), tmp[:, u, :])\
                                .then_inc(stored[u], 16)
                    elif g.kind == "plain_v":
                        act.wait_ge(evac, n + 1)
                        act.dma_start(vt_d[j], tmp[:, u, :]).then_inc(stored[u], 16)

                over(act, groups, finish)
                if gates is not None:
                    act.wait_ge(evac, G + 1)
                    for half in range(2):
                        act.dma_start(gates_d[half], tmp[0:4, half, :]).then_inc(gst, 16)
                    act.wait_ge(gst, 32)
                if storing:
                    for u in range(2):
                        act.wait_ge(stored[u], stored_before(njobs // 2))

            @block.vector
            def _(dve):
                if load_x is not None:
                    for k in range(KD):
                        dve.wait_ge(hi_x, k + 1)
                        dve.tensor_tensor(xl[:, k, :], sq[:, k % 2, :], xh[:, k, :].bitcast(F32), ALU.subtract)\
                            .then_inc(xr, 1)
                if pr:
                    pr.dve_split(dve)
                    pr.dve_rstd(dve)
                    dve.wait_ge(pr.rstd, 3)
                if tables is not None:
                    dve.wait_ge(tab, 32)
                    dve.tensor_tensor(cosr[:], cosr[:], rstd[:], ALU.mult).then_inc(trot, 1)
                    dve.tensor_tensor(sinr[:], sinr[:], rstd[:], ALU.mult).then_inc(trot, 1)
                    dve.wait_ge(trot, 2)

                def leave(g, j, n, u, r):
                    dve.wait_ge(job_done, n + 1)
                    if g.kind == "residual":
                        for c, (t0, nt) in enumerate(TOK):
                            x = dve.tensor_tensor(hcol(j + g.n0, t0, nt), hcol(j + g.n0, t0, nt), psum[:, 3 * u + c, 0:nt], ALU.add)
                        x.then_inc(evac, 1)
                        return
                    if not (isinstance(n, int) and n < 2):
                        dve.wait_ge(stored[u], stored_before(r))
                    if g.kind in ("rope_k", "rope_q"):
                        for c, (t0, nt) in enumerate(TOK):
                            x = dve.tensor_tensor(tmp[:, u, t0:t0 + nt], psum[:, 3 * u + c, 0:nt],
                                                  cosr[:, t0:t0 + nt], ALU.mult)
                        x.then_inc(part, 1)
                        rc = rope_count(g, n)
                        dve.wait_ge(swapped, rc + 1)
                        dve.tensor_tensor(swp[:], swp[:], sinr[:], ALU.mult).then_inc(sig, 1)
                        dve.wait_ge(sig, rc + 1)
                        dve.wait_ge(part, rc + 1)
                        dve.tensor_tensor(tmp[:, u, :], tmp[:, u, :], swp[:], ALU.add).then_inc(evac, 1)
                    elif g.kind == "sigmoid":
                        for c, (t0, nt) in enumerate(TOK):
                            x = dve.tensor_tensor(tmp[:, u, t0:t0 + nt], psum[:, 3 * u + c, 0:nt],
                                                  rstd[:, t0:t0 + nt], ALU.mult)
                        x.then_inc(part, 1)
                        dve.wait_ge(part, n - g.n0 + 1)
                        dve.sem_inc(evac, 1)
                    else:
                        for c, (t0, nt) in enumerate(TOK):
                            x = dve.tensor_tensor(tmp[:, u, t0:t0 + nt], psum[:, 3 * u + c, 0:nt],
                                                  rstd[:, t0:t0 + nt], ALU.mult)
                        x.then_inc(evac, 1)

                def rope_count(g, n):
                    return n if g.n0 == 0 else n - 2

                def hcol(j, t0, nt):
                    if isinstance(j, int):
                        return h[:, j, t0:t0 + nt]
                    return h[:, ds(j, 1), t0:t0 + nt].rearrange("p a t -> p (a t)")

                over(dve, groups, leave)
                if gates is not None:
                    dve.wait_ge(job_done, G + 1)
                    for u in range(2):
                        dve.wait_ge(stored[u], stored_before(G // 2))
                    for half in range(2):
                        for c, (t0, nt) in enumerate(TOK):
                            x = dve.tensor_tensor(tmp[0:4, half, t0:t0 + nt],
                                                  psum[32 * half:32 * half + 4, c, 0:nt],
                                                  rstd[0:4, t0:t0 + nt], ALU.mult)
                    x.then_inc(evac, 1)

    def ffn(name, w_gu, w_dn, gain, following):
        NG = DFF // P // 2
        NW = 6 * NG
        assert NW % 3 == 0 and NW % 2 == 0
        loaded = [sem(f"{name}_w_loaded{u}") for u in range(2)]
        scaled, hi_s, split = (sem(f"{name}_w_{x}") for x in ("scaled", "hi", "split"))
        nx = Prefetch(name, following) if following else None
        gu_done, gu_evac, silu, hid = (sem(f"{name}_{x}") for x in ("gate_up_done", "gate_up_evac", "silu", "hidden"))
        hhi, hlo, dn_done, dn_evac = (sem(f"{name}_{x}") for x in ("hid_hi", "hid_lo", "down_done", "down_evac"))
        pr = Prep(name)
        gu = w_gu.rearrange("(k p) n -> p k n", p=P)

        def source(kind, g, s):
            if kind == "d":
                return w_dn[ds((g * 2 + s) * P, P), :]
            return gu[:, :, ds((g * 2 + s) * P + (DFF if kind == "u" else 0), P)]

        FIRST = [("g", 0), ("u", 0), ("g", 1), ("u", 1)]
        BODY = [("g", 0), ("d", 0), ("d", 1), ("u", 0), ("g", 1), ("u", 1)]

        def stream(eng, body):
            for n, (kind, s) in enumerate(FIRST):
                body(kind, 0, s, n, n, n // 2)
            with eng.Fori(0, NG - 1) as i:
                for q, (kind, s) in enumerate(BODY):
                    body(kind, i if kind == "d" else i + 1, s, i * 6 + 4 + q, 4 + q, i * 3 + (4 + q) // 2)
            for s in range(2):
                n = 4 + 6 * (NG - 1) + s
                body("d", NG - 1, s, n, n, n // 2)

        with nc.Block() as block:
            @block.sync
            def _(sp):
                def load(kind, g, s, n, pos, r):
                    if pos < 2:
                        sp.sem_inc(loaded[pos], 16)
                        return
                    sp.wait_ge(split, n - 1)
                    dst = raw[:, pos % 2, :] if kind == "d" else weight_tile(raw[:, pos % 2, :])
                    sp.dma_start(dst, source(kind, g, s)).then_inc(loaded[pos % 2], 16)

                stream(sp, load)
                if nx:
                    for u in range(2):
                        sp.wait_ge(split, NW - 1 + u)
                        nx.load(sp, u)

            @block.gpsimd
            def _(pool):
                def split_w(kind, g, s, n, pos, rnd):
                    r, b = pos % 2, pos % 3
                    pool.wait_ge(loaded[r], rnd * 16 + 16)
                    if pos < 2:
                        for x in (scaled, hi_s, split):
                            pool.sem_inc(x, 1)
                        return
                    if kind != "d":
                        pool.tensor_tensor(weight_tile(raw[:, r, :]), weight_tile(raw[:, r, :]),
                                           gains[:, gain, :].unsqueeze(2).to_broadcast([P, KD, P]),
                                           ALU.mult).then_inc(scaled, 1)
                    else:
                        pool.sem_inc(scaled, 1)
                    pool.wait_ge(scaled, n + 1)
                    if pos == 3:
                        pool.wait_ge(gu_done, 1)
                    elif pos > 3:
                        i, q = (g, pos - 4) if pos < 10 else (NG - 1, s)
                        i = i if kind == "d" else g - 1
                        if q < 4:
                            pool.wait_ge(gu_done, i * 4 + (2 + q))
                        else:
                            pool.wait_ge(dn_done, i * 8 + 8)
                    pool.tensor_tensor(wh[:, b, :], raw[:, r, :], unit, ALU.mult).then_inc(hi_s, 1)
                    pool.wait_ge(hi_s, n + 1)
                    pool.tensor_tensor(wl[:, b, :], raw[:, r, :], wh[:, b, :].bitcast(F32), ALU.subtract)\
                        .then_inc(split, 1)

                stream(pool, split_w)
                if nx:
                    for u in range(2):
                        nx.scale(pool, u)
                        pool.wait_ge(gu_done if u == 0 else dn_done, (4 if u == 0 else KD) * NG)
                        nx.split(pool, u)

            @block.tensor
            def _(pe):
                def gate_up(n, pos, set_, first=False, between=None):
                    b = pos % 3
                    pe.wait_ge(split, n + 1)
                    hi, lo = weight_tile(wh[:, b, :]), weight_tile(wl[:, b, :])
                    mm = product(pe, 3 * set_, lambda k: hi[:, k, :], lambda k: lo[:, k, :], KD, xh, xl,
                                 pr.lo if first else None, between)
                    mm.then_inc(gu_done, 1)

                def down(n, pos, dn_n):
                    b0, b1 = pos % 3, (pos + 1) % 3
                    pe.wait_ge(split, n + 2)
                    hi = [wh[:, b0, :], wh[:, b1, :]]
                    lo = [wl[:, b0, :], wl[:, b1, :]]
                    for m in range(KD):
                        if m == 1:
                            pe.wait_ge(gu_evac, down_gu)
                        if m >= 2:
                            pe.wait_ge(dn_evac, dn_n + m - 1)
                        mm = product(pe, 3 * ((m + 1) % 2), lambda k: hi[k][:, m * P:(m + 1) * P],
                                     lambda k: lo[k][:, m * P:(m + 1) * P], 2, hidh, hidl)
                        mm.then_inc(dn_done, 1)

                for q in range(4):
                    if q >= 2:
                        pe.wait_ge(gu_evac, q - 1)
                    gate_up(q, q, q % 2, q == 0, pr.pe_total if q == 1 else None)
                with pe.Fori(0, NG - 1) as i:
                    n, g4, d8 = i * 6 + 4, i * 4 + 4, i * 8
                    pe.wait_ge(gu_evac, g4 - 1)
                    gate_up(n, 4, 0)
                    down_gu = g4 + 1
                    pe.wait_ge(hlo, i * 2 + 2)
                    pe.wait_ge(gu_evac, g4)
                    down(n + 1, 5, d8)
                    pe.wait_ge(dn_evac, d8 + 7)
                    gate_up(n + 3, 7, 1)
                    pe.wait_ge(dn_evac, d8 + 8)
                    gate_up(n + 4, 8, 0)
                    pe.wait_ge(gu_evac, g4 + 2)
                    gate_up(n + 5, 9, 1)
                N = 4 + 6 * (NG - 1)
                down_gu = 4 * NG
                pe.wait_ge(hlo, 2 * NG)
                pe.wait_ge(gu_evac, 4 * NG)
                down(N, N, 8 * (NG - 1))

            def gate_part(act, n2):
                act.wait_ge(gu_evac, n2 * 2 + 1)
                act.activation(gate[:], gate[:], ACT.Silu).then_inc(silu, 1)

            def hidden_part(act, n2, s):
                act.wait_ge(hid, n2 + 1)
                act.activation(hidh[:, s, :], up[:], ACT.Copy).then_inc(hhi, 1)

            @block.scalar
            def _(act):
                pr.act_split(act)
                pr.act_root(act)
                for s in range(2):
                    gate_part(act, s)
                    hidden_part(act, s, s)
                with act.Fori(1, NG) as i:
                    for s in range(2):
                        gate_part(act, i * 2 + s)
                        hidden_part(act, i * 2 + s, s)

            @block.vector
            def _(dve):
                pr.dve_split(dve)
                pr.dve_rstd(dve)
                dve.wait_ge(pr.rstd, 3)

                def take(n, dst, set_):
                    dve.wait_ge(gu_done, n + 1)
                    for c, (t0, nt) in enumerate(TOK):
                        x = dve.tensor_tensor(dst[:, t0:t0 + nt], psum[:, 3 * set_ + c, 0:nt], rstd[:, t0:t0 + nt],
                                              ALU.mult)
                    x.then_inc(gu_evac, 1)

                def gate_out(n2, set_, first=False):
                    if not first:
                        dve.wait_ge(hid, n2)
                    take(n2 * 2, gate, set_)

                def up_out(n2, s, set_, first=False):
                    if not first:
                        dve.wait_ge(hlo, n2)
                        dve.wait_ge(hhi, n2)
                    take(n2 * 2 + 1, up, set_)
                    dve.wait_ge(gu_evac, n2 * 2 + 2)
                    dve.wait_ge(silu, n2 + 1)
                    dve.tensor_tensor(up[:], up[:], gate[:], ALU.mult).then_inc(hid, 1)
                    dve.wait_ge(hhi, n2 + 1)
                    dve.tensor_tensor(hidl[:, s, :], up[:], hidh[:, s, :].bitcast(F32), ALU.subtract).then_inc(hlo, 1)

                def down_out(d8):
                    for m in range(KD):
                        dve.wait_ge(dn_done, d8 + m + 1)
                        for c, (t0, nt) in enumerate(TOK):
                            x = dve.tensor_tensor(h[:, m, t0:t0 + nt], h[:, m, t0:t0 + nt],
                                                  psum[:, 3 * ((m + 1) % 2) + c, 0:nt], ALU.add)
                        x.then_inc(dn_evac, 1)

                gate_out(0, 0, True)
                up_out(0, 0, 1, True)
                gate_out(1, 0)
                up_out(1, 1, 1)
                with dve.Fori(1, NG) as i:
                    gate_out(i * 2, 0)
                    down_out(i * 8 - 8)
                    up_out(i * 2, 0, 1)
                    gate_out(i * 2 + 1, 0)
                    up_out(i * 2 + 1, 1, 1)
                down_out(8 * (NG - 1))

    wi, wo = wcols(a["a_w_in"][0]), wcols(a["a_w_out"][0])
    ga = a["a_w_in"][0].rearrange("(k p) n -> p k n", p=P)[:, :, 24 * P:24 * P + 2 * HA]
    wk, wv, wq = wcols(a["w_kv"]), wcols(a["w_kv"], 2 * P), wcols(a["b_w_q"][0])
    wo1 = wcols(a["b_w_o"][0])

    def two(w, gain):
        return [(w(0), gain), (w(1), gain)]

    def gate_and_up(layer, gain):
        w = a["w_gate_up"][layer]
        return [(wcols(w)(0), gain), (wcols(w, DFF)(0), gain)]

    S = dict(locals())
    phases = [
        lambda: run(setup, two(wi, 0)),
        lambda: run(dense, "in", [Group(0, 1, wi, 0, "store"), Group(2, 7, lambda j: wi(j + 2), 0, "store"),
                                  Group(16, 4, lambda j: wi(j + 16), 0, "sigmoid")], None, prep=True, gates=ga),
        lambda: run(mlstm, nc, a, S, two(wo, 1)),
        lambda: run(dense, "out0", [Group(0, 1, wo, 1, "residual"), Group(2, 3, lambda j: wo(j + 2), 1, "residual")],
                    gate_and_up(0, 2), load_x=og_d),
        lambda: run(ffn, "ffn0", a["w_gate_up"][0], a["w_down"][0], 2, two(wk, 3)),
        lambda: run(dense, "kvq", [Group(0, 1, wk, 3, "rope_k"), Group(2, 1, wv, 3, "plain_v"),
                                   Group(4, 4, wq, 4, "rope_q")], None, prep=True, tables=True),
        lambda: run(attention, nc, a, S, two(wo1, None)),
        lambda: run(dense, "out1", [Group(0, 1, wo1, None, "residual"),
                                    Group(2, 3, lambda j: wo1(j + 2), None, "residual")],
                    gate_and_up(1, 5), load_x=og_d),
        lambda: run(ffn, "ffn1", a["w_gate_up"][1], a["w_down"][1], 5, None),
        lambda: run(final, nc, a, S),
    ]
    for phase_ in phases[:upto + 1]:
        phase_()


def mlstm(nc, a, s, following):
    at, sem, psum, ident = s["at"], s["sem"], s["psum"], s["ident"]
    qkvo, gates_d, og_d, ones = s["qkvo"], s["gates_d"], s["og_d"], s["ones"]
    place = [s["fixed_end"]]

    def sb(name, shape, dt=F32):
        t, place[0] = at("ml_" + name, shape, dt, place[0])
        return t

    E1 = DV + 1
    qc = sb("q", [P, 2, HA, MCH])
    kc = sb("k", [P, 2, HA, MCH])
    vc = sb("v", [P, 2, 2 * HA, MCH])
    oc = sb("o", [P, 2, 2 * HA, MCH])
    ex = sb("exp", [P, HA, MCH])
    pr = sb("weights", [P, HA, MCH])
    va = sb("v_ones", [P, HA, E1])
    kw = sb("k_weighted", [P, HA, MCH])
    inter = sb("inter", [P, HA, E1])
    num = sb("num", [P, HA, E1])
    hn = sb("hn", [P, HA, DV])
    junk = sb("junk", [P, DV])
    C = sb("state", [P, HA, E1])
    col = sb("cols", [P, 10, 100])
    cc = sb("chunk_cols", [P, 100])
    dec = sb("decays", [P, HA, 17])
    dc = sb("chunk_decay", [P, HA])
    small = sb("small", [P, 8, HA])
    sel = sb("select_head", [HA, HA, P])
    gi, gf, lsf, bb, mm, nm = (sb(x, [HA, T]) for x in ("logi", "f", "logf", "cumulated", "stabiliser", "neg_M"))
    qm, _ = at("ml_q_masked", [P, NB, MCH], F32, place[0])
    t1, keep = sb("t1", [HA, T]), sb("keep", [HA, T])
    rows = sb("rows", [P, T])
    sm = sb("state_m", [HA, NB])
    bg = sb("gate_bias", [HA, 2])
    dr = sb("decay_rows", [HA, 17])
    CS = sb("decode_state", [P, NB, HA, E1])
    kwm = sb("k_weighted_seq", [P, 2, MCH])

    g_load, consts, rows_pe, dec_pe = (sem("ml_" + x) for x in ("gates_loaded", "consts", "rows_turned", "decays_pe"))
    dv, ac = sem("ml_rows_dve"), sem("ml_rows_act")
    cols_ev, dec_ev, st_load, m_out = (sem("ml_" + x) for x in ("cols_evac", "decays_evac", "states_loaded", "m_stored"))
    c_load = [sem(f"ml_chunk_loaded{u}") for u in range(2)]
    (mb, sc, kt, vt, qcs, pv, upd, ht) = (sem("ml_pe_" + x) for x in
                                          ("minus_m", "scores", "k_turned", "v_turned", "inter", "intra", "update", "h_turned"))
    (exps, kws, ints, ssq) = (sem("ml_act_" + x) for x in ("exp", "k_weighted", "inter", "squares"))
    (prs, vas, nums, den, rden, root, rinv, fac, hns, cup, ogs) = (
        sem("ml_dve_" + x) for x in ("weights", "values", "num", "den", "rden", "mean_square", "rinv", "factor", "hn", "state", "gated"))
    (ccs, msk) = (sem("ml_pool_" + x) for x in ("chunk_cols", "masked"))
    og_st = [sem(f"ml_out_stored{u}") for u in range(2)]
    c_out, qms, kwms, cs_up, cs_out, cs_pe, zero = (sem("ml_" + x) for x in (
        "state_stored", "q_masked", "seq_k_weighted", "seq_state", "seq_state_stored", "seq_update", "zeroed"))

    dcs = sem("ml_pool_chunk_decay")
    qzero = sem("ml_pool_q_masked_zeroed")
    nx = s["Prefetch"]("ml", following)
    qcs_h, local, aden = sem("ml_pe_inter_head"), sem("ml_rows_local"), sem("ml_dve_abs_den")

    def diag_blocks(t):
        x = t[:]
        return bass.AP(x.tensor, x.offset, [list(x.ap[0]), [MCH + TS, NB], [1, TS]])

    CHN = [(0, 0, META)] + [(c, META + MCH * (c - 1), MCH) for c in range(1, NMC + 1)] + [(NMC + 1, T_S, NS)]

    def chunks(eng, body):
        body(0, 0, META, 0, 0)
        with eng.Fori(0, NMC // 2) as i:
            for u in range(2):
                body(i * 2 + (1 + u), i * (2 * MCH) + (META + u * MCH), MCH, (1 + u) % 2, i + u)
        body(NMC + 1, T_S, NS, (NMC + 1) % 2, NMC // 2)

    with nc.Block() as block:
        @block.sync
        def _(sp):
            sp.dma_start(gi[:], gates_d[0]).then_inc(g_load, 16)
            sp.dma_start(gf[:], gates_d[1]).then_inc(g_load, 16)
            with nc.allow_non_contiguous_dma("small"):
                sp.dma_start(bg[:], a["a_b_gate"][0].rearrange("(i h) -> h i", i=2)).then_inc(g_load, 16)
                sp.dma_start(sm[:], a["state_m"].rearrange("b a h -> h (a b)")).then_inc(g_load, 16)

            def load(c, t0, n, u, r):
                if not (isinstance(c, int) and c < 2):
                    sp.wait_ge(og_st[u], r * 16)
                for dst, r0, nr in ((qc, 0, 4), (kc, 4, 4), (vc, 8, 8), (oc, 16, 8)):
                    sp.dma_start(dst[:, u, :, 0:n], qkvo[r0:r0 + nr, :, ds(t0, n)].rearrange("j p t -> p j t"))\
                        .then_inc(c_load[u], 16)

            load(0, 0, META, 0, 0)
            load(1, META, MCH, 1, 0)
            nx.load(sp, 0)
            nx.load(sp, 1)
            for b in range(NB):
                sp.dma_start(CS[:, b, :, 0:DV], a["state_c"][b, 0].rearrange("h d e -> d h e")).then_inc(st_load, 16)
                with nc.allow_non_contiguous_dma("normaliser columns"):
                    sp.dma_start(CS[:, b, :, DV], a["state_n"][b, 0].rearrange("h d -> d h")).then_inc(st_load, 16)
            load(2, META + MCH, MCH, 0, 1)
            with sp.Fori(1, NMC // 2) as i:
                for u in range(2):
                    load(i * 2 + (1 + u), i * (2 * MCH) + (META + u * MCH), MCH, (1 + u) % 2, i + u)
            load(NMC + 1, T_S, NS, 1, NMC // 2)
            sp.wait_ge(dv, 5)
            with nc.allow_non_contiguous_dma("small"):
                sp.dma_start(a["m_p"].rearrange("b a h -> h (a b)"), mm[:, T_S - 1:T_S]).then_inc(m_out, 16)
                sp.dma_start(a["m_s"].rearrange("b a h -> h (a b)"), mm[:, T_S + TS - 1:T:TS]).then_inc(m_out, 16)
            sp.wait_ge(m_out, 32)

        @block.gpsimd
        def _(pool):
            pool.memset(sel[:], 0.0).then_inc(zero, 1)
            pool.wait_ge(zero, 1)
            pool.affine_select(out=sel[:], in_=sel[:], compare_op=ALU.not_equal, fill=1.0, base=0,
                               pattern=[[-1, HA], [0, P]], channel_multiplier=1).then_inc(consts, 1)
            pool.memset(va[:, :, DV:E1], 1.0).then_inc(consts, 1)
            for u in range(2):
                nx.scale(pool, u)
                nx.split(pool, u)

            def step(c, t0, n, u, r):
                if not (isinstance(c, int) and c == 0):
                    pool.wait_ge(hns, c * HA)
                    pool.wait_ge(cup, c * HA)
                else:
                    pool.wait_ge(cols_ev, 10)
                    pool.wait_ge(dec_ev, 1)
                    pool.memset(qm[:], 0.0).then_inc(qzero, 1)
                if isinstance(c, int):
                    pool.tensor_copy(cc[0:n, :], col[0:n, c, :]).then_inc(ccs, 1)
                    pool.wait_ge(exps, c * HA + HA)
                    pool.tensor_copy(dc[:], dec[:, :, c]).then_inc(dcs, 1)
                else:
                    pool.tensor_copy(cc[:], col[:, ds(c, 1), :].rearrange("p a x -> p (a x)")).then_inc(ccs, 1)
                    pool.wait_ge(exps, c * HA + HA)
                    pool.tensor_copy(dc[:], dec[:, :, ds(c, 1)].rearrange("p h a -> p (h a)")).then_inc(dcs, 1)
                e = ex[0:n, :, 0:n]
                x = pool.affine_select(out=e, in_=e, compare_op=ALU.is_ge, fill=0.0, base=0,
                                       pattern=[[0, HA], [1, n]], channel_multiplier=-1)
                x.then_inc(msk, 1)
                if isinstance(c, int) and c == NMC + 1:
                    pool.wait_ge(msk, c + 1)
                    e = ex[:].rearrange("p h (b t) -> p h b t", t=TS)
                    pool.affine_select(out=e, in_=e, compare_op=ALU.is_ge, fill=0.0, base=0,
                                       pattern=[[0, HA], [-TS, NB], [0, TS]], channel_multiplier=1).then_inc(msk, 1)
                pool.wait_ge(root, c + 1)
                pool.tensor_tensor(small[0:n, 4, :], small[0:n, 3, :], s["powc"][0:n].to_broadcast([n, HA]), ALU.pow).then_inc(rinv, 1)

            chunks(pool, step)

        def masked(c):
            return NMC + 3 if isinstance(c, int) and c == NMC + 1 else c + 1

        @block.tensor
        def _(pe):
            pe.wait_ge(consts, 2)
            pe.wait_ge(ac, 5)
            pe.wait_ge(dv, 11)
            for c, t0, n in CHN:
                if c >= 4:
                    pe.wait_ge(cols_ev, c - 3)
                pe.transpose(psum[0:n, c % 4, 0:100], rows[0:100, t0:t0 + n], ident[0:100, 0:100]).then_inc(rows_pe, 1)
            for hd in range(HA):
                x = pe.matmul(psum[:, 4, hd * 17:hd * 17 + 17], sel[:, hd, :], dr[:], start=True, stop=True)
            x.then_inc(dec_pe, 1)

            def step(c, t0, n, u, r):
                last = isinstance(c, int) and c == NMC + 1
                first = isinstance(c, int) and c == 0
                if first:
                    pe.wait_ge(cols_ev, 10)
                    pe.wait_ge(dec_ev, 1)
                else:
                    pe.wait_ge(ogs, c * 2)
                for hd in range(HA):
                    rhs = nm[:, t0:t0 + n] if isinstance(c, int) else nm[:, ds(t0, n)]
                    x = pe.matmul(psum[0:n, 6, hd * MCH:hd * MCH + n], sel[:, hd, 0:n], rhs, start=True, stop=True)
                x.then_inc(mb, 1)
                pe.wait_ge(c_load[u], r * 64 + 64)
                if not first:
                    pe.wait_ge(cup, c * HA)
                for hd in range(HA):
                    x = pe.matmul(psum[0:n, 0, hd * MCH:hd * MCH + n], kc[:, u, hd, 0:n], qc[:, u, hd, 0:n],
                                  start=True, stop=True)
                x.then_inc(sc, 1)
                for hd in range(HA):
                    x = pe.transpose(psum[0:n, 7, hd * MCH:hd * MCH + MCH], kc[:, u, hd, 0:n], ident[:])
                x.then_inc(kt, 1)
                if not first:
                    pe.wait_ge(nums, c * HA)
                for j in range(2 * HA):
                    x = pe.transpose(psum[0:n, 1 + j // 4, (j % 4) * P:(j % 4 + 1) * P], vc[:, u, j, 0:n], ident[:])
                x.then_inc(vt, 1)
                if last:
                    pe.wait_ge(st_load, 16 * 2 * NB)
                for hd in range(HA):
                    o = psum[0:n, 3 + hd % 2, 0:E1]
                    if first:
                        continue
                    if hd >= 2:
                        pe.wait_ge(ints, (c - 1) * HA + hd - 1)
                    if not last:
                        pe.matmul(o, qc[:, u, hd, 0:n], C[:, hd, :], start=True, stop=True).then_inc(qcs_h, 1)
                    else:
                        pe.wait_ge(qms, hd + 1)
                        for b in range(NB):
                            x = pe.matmul(o, qm[:, b, :], CS[:, b, hd, :], start=(b == 0), stop=(b == NB - 1))
                        x.then_inc(qcs_h, 1)
                if first:
                    pe.wait_ge(vt, 1)
                    pe.sem_inc(qcs, 1)
                else:
                    pe.wait_ge(qcs_h, c * HA)
                    pe.sem_inc(qcs, 1)
                pe.wait_ge(vas, c * 2 + 2)
                pe.wait_ge(prs, c + 1)
                for hd in range(HA):
                    if hd >= 2:
                        pe.wait_ge(nums, c * HA + hd - 1)
                    pe.matmul(psum[0:n, 1 + hd % 2, 0:E1], pr[0:n, hd, 0:n], va[0:n, hd, :], start=True, stop=True)\
                        .then_inc(pv, 1)
                if not last:
                    for hd in range(HA):
                        pe.wait_ge(kws, c * HA + hd + 1)
                        if hd >= 2:
                            pe.wait_ge(cup, c * HA + hd - 1)
                        pe.matmul(psum[:, 5 if hd % 2 else 0, 0:E1], kw[0:n, hd, :], va[0:n, hd, :],
                                  start=True, stop=True).then_inc(upd, 1)
                else:
                    for n2 in range(NB * HA):
                        pe.wait_ge(kwms, n2 + 1)
                        if n2 >= 2:
                            pe.wait_ge(cs_up, n2 - 1)
                        pe.matmul(psum[:, 5 if n2 % 2 else 0, 0:E1], kwm[:, n2 % 2, :], va[:, n2 // NB, :],
                                  start=True, stop=True).then_inc(cs_pe, 1)
                pe.wait_ge(hns, c * HA + HA)
                pe.wait_ge(exps, c * HA + HA)
                if not last:
                    pe.wait_ge(kws, c * HA + HA)
                for j in range(2 * HA):
                    x = pe.transpose(psum[:, 6 + j // 4, (j % 4) * MCH:(j % 4) * MCH + n],
                                     hn[0:n, j // 2, (j % 2) * P:(j % 2 + 1) * P], ident[0:n, 0:n])
                    if j % 4 == 3:
                        x.then_inc(ht, 1)

            chunks(pe, step)

        @block.scalar
        def _(act):
            act.wait_ge(dv, 1)
            act.activation(t1[:], t1[:], ACT.Exp, scale=-1.0).then_inc(ac, 1)
            act.wait_ge(ac, 1)
            act.activation(t1[:], t1[:], ACT.Ln, bias=ones[0:HA, 0:1]).then_inc(ac, 1)
            act.wait_ge(dv, 9)
            act.activation(rows[32:32 + HA, :], t1[:], ACT.Exp).then_inc(ac, 1)
            act.activation(rows[64:64 + HA, :], mm[:], ACT.Exp, scale=-1.0).then_inc(ac, 1)
            act.activation(rows[0:HA, :], keep[:], ACT.Copy).then_inc(ac, 1)

            def step(c, t0, n, u, r):
                last = isinstance(c, int) and c == NMC + 1
                first = isinstance(c, int) and c == 0
                act.wait_ge(mb, c + 1)
                act.wait_ge(ccs, c + 1)
                if not first:
                    act.wait_ge(prs, c)
                    act.wait_ge(kws, c * HA)
                for hd in range(HA):
                    act.activation(ex[0:n, hd, 0:n], psum[0:n, 6, hd * MCH:hd * MCH + n], ACT.Exp,
                                   bias=cc[0:n, hd:hd + 1]).then_inc(exps, 1)
                if not last:
                    act.wait_ge(kt, c + 1)
                    act.wait_ge(msk, masked(c))
                    if not first:
                        act.wait_ge(upd, c * HA)
                    for hd in range(HA):
                        act.activation(kw[0:n, hd, :], psum[0:n, 7, hd * MCH:(hd + 1) * MCH], ACT.Copy,
                                       scale=ex[0:n, hd, n - 1:n]).then_inc(kws, 1)
                for hd in range(HA):
                    if first:
                        continue
                    act.wait_ge(qcs_h, (c - 1) * HA + hd + 1)
                    act.wait_ge(nums, c * HA)
                    act.activation(inter[0:n, hd, :], psum[0:n, 3 + hd % 2, 0:E1], ACT.Copy,
                                   scale=cc[0:n, 96 + hd:97 + hd]).then_inc(ints, 1)
                act.wait_ge(rden, c + 1)
                for hd in range(HA):
                    if not (first and hd == 0):
                        act.wait_ge(ssq, c * HA + hd)
                    act.activation(junk[0:n, :], num[0:n, hd, 0:DV], ACT.Square, scale=small[0:n, 1, hd:hd + 1],
                                   accum_out=small[0:n, 2, hd:hd + 1]).then_inc(ssq, 1)
                if last:
                    act.wait_ge(kt, c + 1)
                    act.wait_ge(msk, masked(c))
                    for hd in range(HA):
                        for b in range(NB):
                            n2 = hd * NB + b
                            if n2 >= 2:
                                act.wait_ge(cs_pe, n2 - 1)
                            act.activation(kwm[:, n2 % 2, :], psum[:, 7, hd * MCH:(hd + 1) * MCH], ACT.Copy,
                                           scale=ex[:, hd, TS * b + TS - 1:TS * b + TS]).then_inc(kwms, 1)
                act.wait_ge(ogs, c * 2 + 2)
                act.dma_start(og_d[:, :, ds(t0, n)].rearrange("j p t -> p j t"), oc[:, u, :, 0:n])\
                    .then_inc(og_st[u], 16)

            chunks(act, step)
            for u in range(2):
                act.wait_ge(og_st[u], 16 * 5)

        @block.vector
        def _(dve):
            dve.wait_ge(g_load, 64)
            dve.tensor_scalar(gf[:], gf[:], bg[:, 1:2], None, ALU.add).then_inc(local, 1)
            dve.tensor_scalar(gi[:], gi[:], bg[:, 0:1], None, ALU.add).then_inc(local, 1)
            dve.memset(keep[:], 1.0).then_inc(local, 1)
            dve.memset(rows[:], 0.0).then_inc(local, 1)
            dve.wait_ge(local, 4)
            dve.scalar_tensor_tensor(t1[:], gf[:], -1.0, gf[:], ALU.mult, ALU.max).then_inc(dv, 1)
            dve.memset(keep[:, META:T_S:MCH], 0.0).then_inc(local, 1)
            dve.memset(keep[:, T_S:T:TS], 0.0).then_inc(local, 1)
            dve.wait_ge(ac, 2)
            dve.scalar_tensor_tensor(lsf[:], gf[:], 0.0, t1[:], ALU.min, ALU.subtract).then_inc(dv, 1)
            dve.wait_ge(dv, 2)
            dve.wait_ge(local, 6)
            dve.tensor_tensor_scan(bb[:], keep[:], lsf[:], 0.0, ALU.mult, ALU.add).then_inc(dv, 1)
            dve.tensor_tensor_scan(mm[:, 0:T_S], lsf[:, 0:T_S], gi[:, 0:T_S], 0.0, ALU.add, ALU.max).then_inc(dv, 1)
            for b in range(NB):
                w = slice(T_S + b * TS, T_S + (b + 1) * TS)
                x = dve.tensor_tensor_scan(mm[:, w], lsf[:, w], gi[:, w], sm[:, b:b + 1], ALU.add, ALU.max)
            x.then_inc(dv, 1)
            dve.wait_ge(dv, 5)
            dve.tensor_tensor(nm[:], bb[:], mm[:], ALU.subtract).then_inc(dv, 1)
            dve.wait_ge(dv, 6)
            dve.tensor_copy(t1[:, 0:META], nm[:, 0:META]).then_inc(local, 1)
            v = lambda x, w, n: x.rearrange("p (c t) -> p c t", t=n)
            dve.tensor_tensor(v(t1[:, META:T_S], 0, MCH), v(nm[:, META:T_S], 0, MCH),
                              mm[:, META - 1:T_S - 1:MCH].unsqueeze(2).to_broadcast([HA, NMC, MCH]), ALU.add)\
                .then_inc(dv, 1)
            dve.tensor_tensor(v(t1[:, T_S:T], 0, TS), v(nm[:, T_S:T], 0, TS),
                              sm[:].unsqueeze(2).to_broadcast([HA, NB, TS]), ALU.add).then_inc(dv, 1)
            dve.wait_ge(local, 7)
            dve.tensor_tensor(keep[:], gi[:], bb[:], ALU.subtract).then_inc(dv, 1)
            dve.wait_ge(ac, 3)
            dve.tensor_scalar(rows[96:96 + HA, :], rows[32:32 + HA, :], QSCALE, None, ALU.mult).then_inc(dv, 1)
            dve.tensor_copy(dr[:, 0:1], rows[32:32 + HA, META - 1:META]).then_inc(local, 1)
            dve.tensor_copy(dr[:, 1:1 + NMC], rows[32:32 + HA, META + MCH - 1:T_S:MCH]).then_inc(local, 1)
            dve.tensor_copy(dr[:, 1 + NMC:], rows[32:32 + HA, T_S + TS - 1:T:TS]).then_inc(local, 1)
            dve.wait_ge(local, 10)
            dve.sem_inc(dv, 1)
            for c, t0, n in CHN:
                dve.wait_ge(rows_pe, c + 1)
                dve.tensor_copy(col[0:n, c, :], psum[0:n, c % 4, 0:100]).then_inc(cols_ev, 1)
            dve.wait_ge(dec_pe, 1)
            dve.tensor_copy(dec[:], psum[:, 4, 0:HA * 17].rearrange("p (h x) -> p h x", h=HA)).then_inc(dec_ev, 1)

            def step(c, t0, n, u, r):
                last = isinstance(c, int) and c == NMC + 1
                first = isinstance(c, int) and c == 0
                dve.wait_ge(vt, c + 1)
                if not first:
                    dve.wait_ge(upd, c * HA)
                for j in range(2):
                    dve.tensor_copy(va[0:n, 2 * j:2 * j + 2, 0:DV],
                                    psum[0:n, 1 + j, :].rearrange("p (h e) -> p h e", h=2)).then_inc(vas, 1)
                dve.wait_ge(sc, c + 1)
                dve.wait_ge(msk, masked(c))
                if not first:
                    dve.wait_ge(pv, c * HA)
                dve.scalar_tensor_tensor(pr[0:n, :, 0:n], psum[0:n, 0, :].rearrange("p (h t) -> p h t", h=HA)[:, :, 0:n],
                                         QSCALE, ex[0:n, :, 0:n], ALU.mult, ALU.mult).then_inc(prs, 1)
                if last:
                    for hd in range(HA):
                        if hd == 0:
                            dve.wait_ge(qzero, 1)
                            dve.wait_ge(c_load[u], r * 64 + 64)
                        else:
                            dve.wait_ge(qcs_h, (c - 1) * HA + hd)
                        dve.tensor_copy(diag_blocks(qm), qc[:, u, hd, :].rearrange("p (b t) -> p b t", t=TS))\
                            .then_inc(qms, 1)
                if not first:
                    dve.wait_ge(ssq, c * HA)
                    dve.wait_ge(hns, c * HA)
                for hd in range(HA):
                    dve.wait_ge(pv, c * HA + hd + 1)
                    o = psum[0:n, 1 + hd % 2, 0:E1]
                    if first:
                        dve.tensor_copy(num[0:n, hd, :], o).then_inc(nums, 1)
                    else:
                        dve.wait_ge(ints, (c - 1) * HA + hd + 1)
                        dve.tensor_tensor(num[0:n, hd, :], inter[0:n, hd, :], o, ALU.add).then_inc(nums, 1)
                dve.wait_ge(nums, c * HA + HA)
                dve.scalar_tensor_tensor(small[0:n, 6, :], num[0:n, :, DV], -1.0, num[0:n, :, DV],
                                         ALU.mult, ALU.max).then_inc(aden, 1)
                dve.wait_ge(aden, c + 1)
                dve.tensor_tensor(small[0:n, 0, :], small[0:n, 6, :], cc[0:n, 64:64 + HA], ALU.max).then_inc(den, 1)
                dve.wait_ge(den, c + 1)
                dve.reciprocal(small[0:n, 1, :], small[0:n, 0, :]).then_inc(rden, 1)
                if not last:
                    dve.wait_ge(dcs, c + 1)
                    for hd in range(HA):
                        dve.wait_ge(upd, c * HA + hd + 1)
                        o = psum[:, 5 if hd % 2 else 0, 0:E1]
                        if first:
                            dve.tensor_copy(C[:, hd, :], o).then_inc(cup, 1)
                        else:
                            dve.scalar_tensor_tensor(C[:, hd, :], C[:, hd, :], dc[:, hd:hd + 1], o,
                                                     ALU.mult, ALU.add).then_inc(cup, 1)
                dve.wait_ge(ssq, c * HA + HA)
                dve.tensor_scalar(small[0:n, 3, :], small[0:n, 2, :], 1.0 / DV, EPS, ALU.mult, ALU.add)\
                    .then_inc(root, 1)
                dve.wait_ge(rinv, c + 1)
                dve.tensor_tensor(small[0:n, 5, :], small[0:n, 4, :], small[0:n, 1, :], ALU.mult).then_inc(fac, 1)
                dve.wait_ge(fac, c + 1)
                if not first:
                    dve.wait_ge(ht, c * 2)
                for hd in range(HA):
                    dve.tensor_scalar(hn[0:n, hd, :], num[0:n, hd, 0:DV], small[0:n, 5, hd:hd + 1], None, ALU.mult)\
                        .then_inc(hns, 1)
                if last:
                    for n2 in range(NB * HA):
                        hd, b = n2 // NB, n2 % NB
                        dve.wait_ge(cs_pe, n2 + 1)
                        dve.scalar_tensor_tensor(CS[:, b, hd, :], CS[:, b, hd, :], dec[:, hd, 1 + NMC + b:2 + NMC + b],
                                                 psum[:, 5 if n2 % 2 else 0, 0:E1], ALU.mult, ALU.add).then_inc(cs_up, 1)
                for j in range(2):
                    dve.wait_ge(ht, c * 2 + j + 1)
                    o = oc[:, u, 4 * j:4 * j + 4, 0:n]
                    dve.tensor_tensor(o, o, psum[:, 6 + j, :].rearrange("p (k t) -> p k t", k=4)[:, :, 0:n], ALU.mult)\
                        .then_inc(ogs, 1)

            chunks(dve, step)

    with nc.Block() as block:
        @block.sync
        def _(sp):
            sp.dma_start(a["c_p"][0, 0].rearrange("h d e -> d h e"), C[:, :, 0:DV]).then_inc(c_out, 16)
            with nc.allow_non_contiguous_dma("normaliser columns"):
                sp.dma_start(a["n_p"][0, 0].rearrange("h d -> d h"), C[:, :, DV]).then_inc(c_out, 16)
                for b in range(NB):
                    sp.dma_start(a["c_s"][b, 0].rearrange("h d e -> d h e"), CS[:, b, :, 0:DV]).then_inc(c_out, 16)
                    sp.dma_start(a["n_s"][b, 0].rearrange("h d -> d h"), CS[:, b, :, DV]).then_inc(c_out, 16)
            sp.wait_ge(c_out, 16 * (2 + 2 * NB))



def attention(nc, a, s, following):
    at, sem, psum, ident = s["at"], s["sem"], s["psum"], s["ident"]
    k2_d, vt_d, qr_d, og_d = s["k2_d"], s["vt_d"], s["qr_d"], s["og_d"]
    place = [s["fixed_end"]]

    def sb(name, shape, dt=F32):
        t, place[0] = at("at_" + name, shape, dt, place[0])
        return t

    NU = 2 * KVH
    KW = META + WINDOW
    SK = META + CHUNK + TS
    CACHED = META + CHUNK
    NP = SEQ // CHUNK
    R = 2 * TS
    SB = P // R
    NSTEP = NP + NB // SB
    groups = [(0, META), (T_S - WINDOW, WINDOW), (T_S, NS)]
    kk, vv = sb("k_out", [P, 3, 2, P]), sb("v_out", [P, 3, 2, P])
    kv = sb("kv_rows", [P, 3, 2, 2 * P])
    q = sb("q", [P, 2, KD, CHUNK])
    qdl = sb("q_decode_loaded", [P, KD, NS])
    qd = sb("q_decode", [P, NB, KD, TS])
    k = sb("k", [P, 2, KVH, KW])
    v = sb("v", [P, 2, 2, WINDOW])
    vm = sb("v_meta", [P, NU, HD])
    pbm = sb("prob_meta", [P, 2, NU, META])
    vw = sb("v_window", [P, 2 * P])
    pb = sb("prob", [P, 2, NU, KW])
    pt = sb("prob_turned", [P, NU, P])
    pm = sb("prob_meta_turned", [P, P])
    ob = sb("out", [P, 2, KD, CHUNK])
    st = sb("stats", [P, 2, 8, NU])
    sink = sb("sink", [P, NU])
    sinks = sb("sink_decode", [P, NU])
    kct = sb("k_cached", [SK, NB, 2 * P])
    vct = sb("v_cached", [SK, NB, 2 * P])
    ks = sb("k_decode", [P, NB, KVH, SK])

    kvl, kvt, kve, kvo = (sem("at_kv_" + x) for x in ("loaded", "turned", "evac", "stored"))
    nx = s["Prefetch"]("at", following)
    cst, vml, vmz = sem("at_constants_loaded"), sem("at_v_meta_loaded"), sem("at_v_meta_zeroed")
    ld = [sem(f"at_chunk_loaded{u}") for u in range(2)]
    ldv = [sem(f"at_v_loaded{u}") for u in range(2)]
    st_o = [sem(f"at_out_stored{u}") for u in range(2)]
    dl = sem("at_decode_loaded")
    (sc, vt, ptd, pmd, pv) = (sem("at_pe_" + x) for x in ("scores", "v_turned", "p_turned", "p_meta_turned", "values"))
    (ex, es) = (sem("at_act_" + x) for x in ("exp", "sink"))
    (mx, mxs, neg, dsk, den, rdn, nrm, vws, pts, pms, obs) = (sem("at_dve_" + x) for x in (
        "max", "max_sink", "neg_max", "sink_less_max", "den", "rden", "normal", "v_window", "p_turned", "p_meta", "out"))
    kml = sem("at_k_meta_loaded")
    qde = sem("at_pool_q_decode")
    kct_t = sem("at_pe_k_decode_turned")
    kse = [sem("at_dve_k_decode"), sem("at_act_k_decode")]

    def ahead(eng, first_part, second_part, middle=None):
        first_part(0, CHUNK, 0, 0)
        for i in range(4):
            first_part(i + 1, WINDOW, (i + 1) % 2, (i + 1) // 2)
            if i == 3 and middle is not None:
                middle(eng)
            second_part(i, CHUNK if i == 0 else WINDOW, i % 2, i // 2)
        with eng.Fori(2, NP // 2 - 1) as i:
            for u in range(2):
                first_part(i * 2 + (u + 1), WINDOW, (u + 1) % 2, i + u)
                second_part(i * 2 + u, WINDOW, u, i)
        for i in range(NP - 2, NSTEP):
            if i + 1 < NSTEP:
                first_part(i + 1, WINDOW, (i + 1) % 2, (i + 1) // 2)
            second_part(i, WINDOW, i % 2, i // 2)

    def width(i):
        return SK if decode(i) else META + (CHUNK if isinstance(i, int) and i == 0 else WINDOW)

    CACHED_BANK = [[4, 5], [6, 5]]

    def decode(i):
        return isinstance(i, int) and i >= NP

    def later(i, than=0):
        return not isinstance(i, int) or i > than

    with nc.Block() as block:
        @block.sync
        def _(sp):
            for g, (t0, n) in enumerate(groups):
                for t in range(2):
                    for hh in range(2):
                        sp.dma_start(kk[HD * hh:HD * hh + HD, g, t, 0:n], k2_d[2 * t + hh, 0:HD, t0:t0 + n])\
                            .then_inc(kvl, 16)
                sp.dma_start(vv[:, g, :, 0:n], vt_d[:, :, t0:t0 + n].rearrange("a p t -> p a t")).then_inc(kvl, 16)

            def load(i, w, u):
                if decode(i):
                    return
                if later(i, 1):
                    sp.wait_ge(sc, i - 1)
                t = META + CHUNK * i if isinstance(i, int) else i * CHUNK + META
                w0 = t + CHUNK - w
                sp.dma_start(q[:, u], qr_d[:, :, ds(t, CHUNK)].rearrange("j p t -> p j t")).then_inc(ld[u], 16)
                sp.dma_start(k[:, u, :, META:META + w], k2_d[:, :, ds(w0, w)].rearrange("j p t -> p j t"))\
                    .then_inc(ld[u], 16)
                if later(i, 1):
                    sp.wait_ge(vt, i - 1)
                sp.dma_start(v[:, u, :, 0:w], vt_d[:, :, ds(w0, w)].rearrange("j p t -> p j t")).then_inc(ldv[u], 16)

            load(0, CHUNK, 0)
            load(1, WINDOW, 1)
            nx.load(sp, 0)
            nx.load(sp, 1)
            sp.wait_ge(kve, 6)
            sp.wait_ge(vmz, 1)
            for un in range(NU):
                sp.dma_start(vm[META * un:META * un + META, un, :],
                             kv[0:META, 0, 1, (un % KVH) * HD:(un % KVH + 1) * HD]).then_inc(vml, 16)
            for b in range(NB):
                for x, dst in enumerate((kct, vct)):
                    sp.dma_start(dst[CACHED:SK, b, :], kv[TS * b:TS * b + TS, 2, x, :]).then_inc(dl, 16)
            load(2, WINDOW, 0)
            with sp.Fori(1, NP // 2 - 1) as i:
                for u in range(2):
                    load(i * 2 + (u + 1), WINDOW, (u + 1) % 2)
            load(NP - 1, WINDOW, (NP - 1) % 2)
            for x, (m, w, d) in enumerate((("meta_k_p", "win_k_p", "win_k_s"), ("meta_v_p", "win_v_p", "win_v_s"))):
                sp.dma_start(a[m][0].rearrange("t h d -> t (h d)"), kv[0:META, 0, x, :]).then_inc(kvo, 16)
                sp.dma_start(a[w][0].rearrange("t h d -> t (h d)"), kv[:, 1, x, :]).then_inc(kvo, 16)
                for b in range(NB):
                    sp.dma_start(a[d][b, WINDOW - TS:WINDOW].rearrange("t h d -> t (h d)"),
                                 kv[TS * b:TS * b + TS, 2, x, :]).then_inc(kvo, 16)
            sp.wait_ge(kvo, 16 * 2 * (2 + NB))

        @block.gpsimd
        def _(pool):
            pool.memset(vm[:], 0.0).then_inc(vmz, 1)
            for u in range(2):
                nx.scale(pool, u)
                nx.split(pool, u)
            pool.wait_ge(dl, 16 * (5 + 2 * NB))
            pool.tensor_copy(qd[:].rearrange("p b j t -> p j b t"), qdl[:].rearrange("p j (b t) -> p j b t", t=TS))\
                .then_inc(qde, 1)

        @block.tensor
        def _(pe):
            pe.wait_ge(kvl, 16 * 15)
            for g, (t0, n) in enumerate(groups):
                for x, src in enumerate((kk, vv)):
                    for t in range(2):
                        y = pe.transpose(psum[0:n, 2 * g + x, t * P:(t + 1) * P], src[:, g, t, 0:n], ident[:])
                    y.then_inc(kvt, 1)
            pe.wait_ge(kve, 6)

            def scores(i, w, u, r):
                if decode(i):
                    g = i - NP
                    if g == 0:
                        pe.wait_ge(qde, 1)
                        pe.wait_ge(ex, i)
                    for b in range(SB):
                        for un in range(NU):
                            kh, half = un % KVH, HD * (un // KVH)
                            x = pe.matmul(psum[R * b:R * b + R, 2 * g + un // 4, (un % 4) * SK:(un % 4 + 1) * SK],
                                          qd[half:half + HD, g * SB + b, 2 * kh:2 * kh + 2, :],
                                          ks[half:half + HD, g * SB + b, kh, :], start=True, stop=True)
                    x.then_inc(sc, 1)
                    return
                pe.wait_ge(ld[u], r * 32 + 32)
                if later(i):
                    pe.wait_ge(ex, i)
                else:
                    pe.wait_ge(kml, 32)
                for un in range(NU):
                    kh, half = un % KVH, HD * (un // KVH)
                    ql = q[half:half + HD, u, 2 * kh:2 * kh + 2, :]
                    o = psum[:, un // 2, (un % 2) * (META + w):(un % 2 + 1) * (META + w)]
                    x = pe.matmul(o, ql, k[half:half + HD, u, kh, 0:META + w], start=True, stop=True)
                x.then_inc(sc, 1)

            def values(i, w, u, r):
                dec = decode(i)
                if not dec:
                    pe.wait_ge(ldv[u], r * 16 + 16)
                    for t in range(2):
                        x = pe.transpose(psum[0:w, 6, (t + 1) * P:(t + 2) * P], v[:, u, t, 0:w], ident[:])
                    x.then_inc(vt, 1)
                pe.wait_ge(nrm, i + 1)
                lo, n = (0, SK) if dec else (META, w)
                for un in range(NU):
                    x = pe.transpose(psum[0:n, 4 + un // 4, (un % 4) * P:(un % 4 + 1) * P],
                                     pb[:, u, un, lo:lo + n], ident[:])
                x.then_inc(ptd, 1)
                if not dec:
                    pe.wait_ge(vws, i + 1)
                    pe.transpose(psum[:, 6, 0:P], pbm[:, u].rearrange("p u k -> p (u k)"), ident[:]).then_inc(pmd, 1)
                    pe.wait_ge(pms, i + 1)
                pe.wait_ge(pts, i * 2 + 2)
                if later(i):
                    pe.wait_ge(obs, i)
                else:
                    pe.wait_ge(vml, 16 * NU)
                for un in range(NU):
                    kh, half = un % KVH, HD * (un // KVH)
                    if dec:
                        for b in range(SB):
                            x = pe.matmul(psum[half:half + HD, 7, kh * P + R * b:kh * P + R * b + R],
                                          vct[:, (i - NP) * SB + b, kh * HD:(kh + 1) * HD],
                                          pt[0:SK, un, R * b:R * b + R], start=True, stop=True)
                    else:
                        o = psum[half:half + HD, 7, kh * P:(kh + 1) * P]
                        pe.matmul(o, vw[0:w, kh * HD:(kh + 1) * HD], pt[0:w, un, :], start=True, stop=False)
                        x = pe.matmul(o, vm[:, un, :], pm[:], start=False, stop=True)
                x.then_inc(pv, 1)

            def turn_cached(pe):
                pe.wait_ge(dl, 16 * (5 + 2 * NB))
                for g in range(2):
                    for t in range(2):
                        if (g, t) == (1, 1):
                            pe.wait_ge(kse[1], 1)
                        for b in range(SB):
                            x = pe.transpose(psum[:, CACHED_BANK[g][t], b * SK:(b + 1) * SK],
                                             kct[:, g * SB + b, t * P:(t + 1) * P], ident[0:SK, 0:SK])
                    x.then_inc(kct_t, 1)
                for t in range(2):
                    pe.wait_ge(kse[t], 2)

            ahead(pe, scores, values, turn_cached)

        def cached(eng, t, copy):
            for g in range(2):
                eng.wait_ge(kct_t, g + 1)
                for kh in (2 * t, 2 * t + 1):
                    for dup in range(2):
                        x = copy(ks[HD * dup:HD * dup + HD, g * SB:(g + 1) * SB, kh, :],
                                 psum[HD * (kh % 2):HD * (kh % 2) + HD, CACHED_BANK[g][t], 0:SB * SK]
                                 .rearrange("p (b k) -> p b k", k=SK))
                x.then_inc(kse[t], 1)

        def unit_scores(i, per):
            b = 0 if not decode(i) else 2 * (i - NP)
            return psum[:, b:b + NU // per, 0:per * width(i)].rearrange("p b (u k) -> p b u k", u=per)

        @block.scalar
        def _(act):
            for u in range(2):
                act.dma_start(k[:, u, :, 0:META], k2_d[:, :, 0:META].rearrange("h p t -> p h t")).then_inc(kml, 16)
            with nc.allow_non_contiguous_dma("sinks"):
                for j in range(2):
                    for half in range(2):
                        src = a["b_sinks"].rearrange("a (k j p) -> a k j p", j=2, p=2)[0:1, :, j, half]
                        u = slice(KVH * half, KVH * half + KVH)
                        act.dma_start(sink[j * CHUNK:(j + 1) * CHUNK, u], src.to_broadcast([CHUNK, KVH]))\
                            .then_inc(cst, 16)
                        for b in range(SB):
                            act.dma_start(sinks[R * b + j * TS:R * b + (j + 1) * TS, u],
                                          src.to_broadcast([TS, KVH])).then_inc(cst, 16)
            for dst, meta, win in ((kct, "cache_meta_k", "cache_win_k"), (vct, "cache_meta_v", "cache_win_v")):
                act.dma_start(dst[0:META], a[meta].rearrange("b t h d -> t b (h d)")).then_inc(dl, 16)
                act.dma_start(dst[META:CACHED], a[win][:, WINDOW - CHUNK:WINDOW].rearrange("b t h d -> t b (h d)"))\
                    .then_inc(dl, 16)
            act.dma_start(qdl[:], qr_d[:, :, T_S:T].rearrange("j p t -> p j t")).then_inc(dl, 16)

            def exponentials(i, w, u, r):
                act.wait_ge(neg, i + 1)
                if later(i, 1):
                    act.wait_ge(ptd, i - 1)
                    act.wait_ge(pmd, i - 1)
                per = 4 if decode(i) else 2
                src = unit_scores(i, per)
                for un in range(NU):
                    x = act.activation(pb[:, u, un, 0:width(i)], src[:, un // per, un % per, :], ACT.Exp,
                                       scale=SCORE_SCALE, bias=st[:, u, 2, un:un + 1], accum_out=st[:, u, 3, un:un + 1])
                x.then_inc(ex, 1)
                act.wait_ge(dsk, i + 1)
                act.activation(st[:, u, 5, :], st[:, u, 4, :], ACT.Exp).then_inc(es, 1)

            def store(i, w, u, r):
                act.wait_ge(obs, i + 1)
                if decode(i):
                    t, n = T_S + (i - NP) * CHUNK, SB * TS
                else:
                    t, n = (META + CHUNK * i if isinstance(i, int) else i * CHUNK + META), CHUNK
                act.dma_start(og_d[:, :, ds(t, n)].rearrange("j p t -> p j t"), ob[:, u]).then_inc(st_o[u], 16)

            ahead(act, exponentials, store,
                  lambda e: cached(e, 1, lambda o, x: e.activation(o, x, ACT.Copy)))
            for u in range(2):
                act.wait_ge(st_o[u], 16 * NSTEP // 2)

        @block.vector
        def _(dve):
            for g, (t0, n) in enumerate(groups):
                for x in range(2):
                    dve.wait_ge(kvt, 2 * g + x + 1)
                    dve.tensor_copy(kv[0:n, g, x, :], psum[0:n, 2 * g + x, 0:2 * P]).then_inc(kve, 1)
            dve.wait_ge(cst, 16 * 2 * 2 * (1 + SB))

            def maxima(i, u):
                snk = sinks[:] if decode(i) else sink[:]
                per = 4 if decode(i) else 2
                dve.wait_ge(sc, i + 1)
                dve.tensor_reduce(st[:, u, 0, :].rearrange("p (b u) -> p b u", u=per), unit_scores(i, per), AX_X,
                                  ALU.max).then_inc(mx, 1)
                dve.wait_ge(mx, i + 1)
                dve.scalar_tensor_tensor(st[:, u, 1, :], st[:, u, 0, :], SCORE_SCALE, snk, ALU.mult, ALU.max)\
                    .then_inc(mxs, 1)
                dve.wait_ge(mxs, i + 1)
                dve.tensor_scalar(st[:, u, 2, :], st[:, u, 1, :], -1.0, None, ALU.mult).then_inc(neg, 1)
                dve.tensor_tensor(st[:, u, 4, :], snk, st[:, u, 1, :], ALU.subtract).then_inc(dsk, 1)

            def normalise(i, u):
                dve.wait_ge(ex, i + 1)
                dve.wait_ge(es, i + 1)
                dve.tensor_tensor(st[:, u, 6, :], st[:, u, 3, :], st[:, u, 5, :], ALU.add).then_inc(den, 1)
                dve.wait_ge(den, i + 1)
                dve.reciprocal(st[:, u, 7, :], st[:, u, 6, :]).then_inc(rdn, 1)
                dve.wait_ge(rdn, i + 1)
                if later(i, 1) and not decode(i):
                    dve.wait_ge(pmd, i - 1)
                lo = 0 if decode(i) else META
                if not decode(i):
                    dve.tensor_tensor(pbm[:, u], pb[:, u, :, 0:META],
                                      st[:, u, 7, :].unsqueeze(2).to_broadcast([P, NU, META]), ALU.mult)
                p = pb[:, u, :, lo:width(i)]
                dve.tensor_tensor(p, p, st[:, u, 7, :].unsqueeze(2).to_broadcast([P, NU, width(i) - lo]), ALU.mult)\
                    .then_inc(nrm, 1)

            def output(i, u, r):
                dve.wait_ge(pv, i + 1)
                if later(i, 1):
                    dve.wait_ge(st_o[u], r * 16)
                if decode(i):
                    for kh in range(KVH):
                        x = dve.tensor_copy(ob[:, u, 2 * kh:2 * kh + 2, :].rearrange("p j (s t) -> p s j t", s=SB),
                                            psum[:, 7, kh * P:(kh + 1) * P].rearrange("p (s j t) -> p s j t", s=SB, j=2))
                else:
                    x = dve.tensor_copy(ob[:, u], psum[:, 7, :].rearrange("p (j t) -> p j t", j=KD))
                x.then_inc(obs, 1)

            def first_part(i, w, u, r):
                if later(i):
                    normalise(i - 1, 1 - u)
                if later(i, 1):
                    output(i - 2, u, r - 1)
                maxima(i, u)

            def second_part(i, w, u, r):
                n = SK if decode(i) else w
                if isinstance(i, int) and i == NSTEP - 1:
                    normalise(i, u)
                    output(i - 1, 1 - u, (i - 1) // 2)
                if later(i):
                    dve.wait_ge(pv, i)
                if not decode(i):
                    dve.wait_ge(vt, i + 1)
                    dve.tensor_copy(vw[0:n, :], psum[0:n, 6, P:3 * P]).then_inc(vws, 1)
                dve.wait_ge(ptd, i + 1)
                for j in range(2):
                    dve.tensor_copy(pt[0:n, 4 * j:4 * j + 4, :],
                                    psum[0:n, 4 + j, :].rearrange("p (u r) -> p u r", u=4)).then_inc(pts, 1)
                if not decode(i):
                    dve.wait_ge(pmd, i + 1)
                    dve.tensor_copy(pm[:], psum[:, 6, 0:P]).then_inc(pms, 1)
                if isinstance(i, int) and i == NSTEP - 1:
                    output(i, u, r)

            ahead(dve, first_part, second_part, lambda e: cached(e, 0, e.tensor_copy))


def final(nc, a, s):
    at, sem, psum, ident, ones, h = s["at"], s["sem"], s["psum"], s["ident"], s["ones"], s["h"]
    gf, e = at("fi_gain", [P, D], F32, s["fixed_end"])
    y, e = at("fi_y", [P, 3, D], F32, e)
    junk, e = at("fi_junk", [P, 512], F32, e)
    ss, e = at("fi_sums", [P, 9, 5], F32, e)
    gl = sem("fi_gain_loaded")
    turned, sqr, tot, root, rs, ev = (sem("fi_" + x) for x in ("turned", "squares", "sum", "root", "rstd", "evac"))
    sto = [sem(f"fi_stored{i}") for i in range(3)]
    NT = (T - META) // P
    with nc.Block() as block:
        @block.sync
        def _(sp):
            sp.dma_start(gf[:], a["g_final"].rearrange("(a d) -> a d", a=1).to_broadcast([P, D])).then_inc(gl, 16)
            for i in range(NT):
                sp.wait_ge(ev, 2 * i + 2)
                dst = a["y_p"][0, i * P:(i + 1) * P, :] if i < NT - 1 else a["y_s"].rearrange("b t d -> (b t) d")
                sp.dma_start(dst, y[:, i % 3, :]).then_inc(sto[i % 3], 16)
            for b in range(3):
                sp.wait_ge(sto[b], 16 * (NT // 3))

        @block.tensor
        def _(pe):
            for i in range(NT):
                for half in range(2):
                    u = 2 * i + half
                    if i >= 4:
                        pe.wait_ge(ev, u - 7)
                    for k in range(4):
                        x = pe.transpose(psum[:, u % 8, k * P:(k + 1) * P],
                                         h[:, 4 * half + k, META + i * P:META + (i + 1) * P], ident[:])
                    x.then_inc(turned, 1)

        @block.scalar
        def _(act):
            for i in range(NT):
                for half in range(2):
                    u = 2 * i + half
                    act.wait_ge(turned, u + 1)
                    if u:
                        act.wait_ge(sqr, u)
                    act.activation(junk[:], psum[:, u % 8, :], ACT.Square, accum_out=ss[:, i, half:half + 1])\
                        .then_inc(sqr, 1)

        @block.gpsimd
        def _(pool):
            for i in range(NT):
                pool.wait_ge(root, i + 1)
                pool.tensor_tensor(ss[:, i, 4:5], ss[:, i, 3:4], s["powc"][:], ALU.pow).then_inc(rs, 1)

        @block.vector
        def _(dve):
            dve.wait_ge(gl, 16)
            for i in range(NT):
                dve.wait_ge(sqr, 2 * i + 2)
                dve.tensor_tensor(ss[:, i, 2:3], ss[:, i, 0:1], ss[:, i, 1:2], ALU.add).then_inc(tot, 1)
                dve.wait_ge(tot, i + 1)
                dve.tensor_scalar(ss[:, i, 3:4], ss[:, i, 2:3], 1.0 / D, EPS, ALU.mult, ALU.add).then_inc(root, 1)
                dve.wait_ge(rs, i + 1)
                if i >= 3:
                    dve.wait_ge(sto[i % 3], 16 * (i // 3))
                for half in range(2):
                    w = slice(512 * half, 512 * half + 512)
                    dve.scalar_tensor_tensor(y[:, i % 3, w], psum[:, (2 * i + half) % 8, :], ss[:, i, 4:5], gf[:, w],
                                             ALU.mult, ALU.mult).then_inc(ev, 1)



OUTS = [("y_p", (1, SEQ, D)), ("y_s", (NB, TS, D)),
        ("c_p", (1, 1, HA, DQK, DV)), ("n_p", (1, 1, HA, DQK)), ("m_p", (1, 1, HA)),
        ("meta_k_p", (1, META, KVH, HD)), ("meta_v_p", (1, META, KVH, HD)),
        ("win_k_p", (1, WINDOW, KVH, HD)), ("win_v_p", (1, WINDOW, KVH, HD)),
        ("c_s", (NB, 1, HA, DQK, DV)), ("n_s", (NB, 1, HA, DQK)), ("m_s", (NB, 1, HA)),
        ("win_k_s", (NB, WINDOW, KVH, HD)), ("win_v_s", (NB, WINDOW, KVH, HD))]


def rotary_tables():
    pos = np.concatenate([np.arange(T_S), np.tile(META + PAST + np.arange(TS), NB)]).astype(np.float32)
    half = HD // 2
    inv = (np.float32(10000.0) ** (-np.arange(half, dtype=np.float32) / np.float32(half))).astype(np.float32)
    ang = (pos[None, :] * inv[:, None]).astype(np.float32).astype(np.float64)
    cos, sin = np.cos(ang).astype(np.float32), np.sin(ang).astype(np.float32)
    return np.concatenate([cos] * 4), np.concatenate([-sin, sin] * 2)


def host_inputs(inputs):
    arrays = {n: np.ascontiguousarray(v) for n, v in inputs.items()}
    arrays["rope_cos"], arrays["rope_sin"] = rotary_tables()
    return arrays


def kernel(**inputs):
    import concourse.bacc as bacc
    from concourse.bass_utils import run_bass_kernel_spmd

    nc = bacc.Bacc("TRN2", target_bir_lowering=False, num_devices=1)
    arrays, aps = {}, {}
    for n, v in host_inputs(inputs).items():
        arrays["in_" + n] = v
        aps[n] = nc.dram_tensor("in_" + n, v.shape, mybir.dt.from_np(v.dtype), kind="ExternalInput").ap()
    for n, shape in OUTS:
        aps[n] = nc.dram_tensor(n, shape, F32, kind="ExternalOutput").ap()
    build(nc, aps)
    r = run_bass_kernel_spmd(nc, [arrays], core_ids=[0])
    return tuple(r.results[0][n] for n, _ in OUTS)
```

```python
from contextlib import ExitStack

import numpy as np

import concourse.bass as bass
from concourse import mybir
from concourse.alu_op_type import AluOpType as ALU

F32 = mybir.dt.float32
F32R = mybir.dt.float32r
ACT = mybir.ActivationFunctionType
AX_X = mybir.AxisListType.X
ds = bass.ds

P = 128
D = 1024
KD = D // P
META, SEQ, NB, TS = 16, 1024, 8, 16
NS = NB * TS
T = META + SEQ + NS
T_S = META + SEQ
TOK_ALL = [(0, 400), (400, 384), (784, 384)]
TOK_REAL = [(META + 384 * c, 384) for c in range(3)]
HA, DQK, DV = 4, 128, 256
QSCALE = DQK ** -0.5
DFF = 2816
HD, KVH = 64, 4
CHUNK, WINDOW, PAST = 64, 128, 512
EPS = 1e-6
SCORE_SCALE = HD ** -0.5
MCH = 128
NMC = SEQ // MCH


class Group:

    def __init__(self, n0, pairs, weight, gain, kind):
        self.n0, self.pairs, self.weight, self.gain, self.kind = n0, pairs, weight, gain, kind


def over(eng, groups, body):
    for g in groups:
        if g.pairs == 1:
            for u in range(2):
                body(g, u, g.n0 + u, u, g.n0 // 2)
        else:
            with eng.Fori(0, g.pairs) as i:
                for u in range(2):
                    body(g, 2 * i + u, g.n0 + 2 * i + u, u, i + g.n0 // 2)


def build(nc, a, upto=99):
    ctx = ExitStack()
    with ctx:
        _build(nc, a, ctx, upto)


def _build(nc, a, ctx, upto):
    base = [(nc.sbuf_base + 31) // 32 * 32]
    limit = nc.sbuf_usable_end

    def at(name, shape, dt=F32, offset=0):
        n = int(np.prod(shape[1:])) * 4
        assert offset + n <= limit, (name, offset + n, limit)
        return nc.alloc_sbuf_tensor_at(name, shape, dt, offset=offset), offset + (n + 31) // 32 * 32

    def sb(name, shape, dt=F32):
        t, base[0] = at(name, shape, dt, base[0])
        return t

    TOK = list(TOK_ALL)
    phase = [None]

    def sem(name):
        phase[0].append(nc.alloc_semaphore(name))
        return phase[0][-1]

    def run(step, *args, **kw):
        phase[0] = []
        step(*args, **kw)
        nc.clear_and_free_semaphores(phase[0])
        nc.all_engine_barrier()

    def dram(name, shape):
        return nc.dram_tensor(name, shape, F32, kind="Internal").ap()

    h = sb("h", [P, KD, T])
    rstd = sb("rstd", [P, T])
    ident = sb("ident", [P, P])
    ones = sb("ones", [P, P])
    gains = sb("gains", [P, 6, KD])
    epsc = sb("epsc", [P, 1])
    powc = sb("minus_half", [P, 1])
    raw = sb("raw", [P, 2, D])
    wh = sb("wh", [P, 3, D], F32R)
    wl = sb("wl", [P, 3, D], F32R)
    fixed_end = base[0]

    xh = sb("xh", [P, KD, T], F32R)
    xl = sb("xl", [P, KD, T], F32R)
    x_end = base[0]
    sq_at = base[0]
    sq = sb("sq", [P, 2, T])
    acc = sb("acc", [P, T])
    dense_end = base[0]
    tmp, e1 = at("tmp", [P, 2, T], F32, dense_end)
    swp, e2 = at("swp", [P, T], F32, e1)
    hidh, e1b = at("hidh", [P, 2, T], F32R, dense_end)
    hidl, e2b = at("hidl", [P, 2, T], F32R, e1b)
    cosr, e3 = at("cosr", [P, T], F32, e2)
    sinr, e4 = at("sinr", [P, T], F32, e3)
    xring, x_ring_end = at("x_loaded", [P, 4, T], F32, sq_at)
    gate, up_at = at("gate", [P, T], F32, sq_at)
    up, _ = at("up", [P, T], F32, up_at)

    qkvo = dram("qkvo", (24, P, T))
    states_stored = nc.alloc_semaphore("ml_states_stored")
    N_STATE_STORES = HA + 2 + NB
    gates_d = dram("gates_d", (2, 4, T))
    og_d = dram("og_d", (KD, P, T))
    k2_d = dram("k2_d", (KVH, P, T))
    vt_d = dram("vt_d", (2, P, T))
    qr_d = dram("qr_d", (KD, P, T))

    psum = ctx.enter_context(nc.psum_tensor("psum", [P, 8, 512], F32))

    unit = ones[:, 0:1].to_broadcast([P, D])

    def wcols(w, col0=0):
        v = w.rearrange("(k p) n -> p k n", p=P)
        return lambda j: v[:, :, ds(j * P + col0, P)]

    def weight_tile(b):
        return b.rearrange("p (k n) -> p k n", k=KD)

    class Prefetch:

        def __init__(self, name, tiles):
            self.tiles = tiles
            self.loaded = [sem(f"{name}_next_w_loaded{u}") for u in range(2)]
            self.scaled, self.hi, self.lo = (sem(f"{name}_next_w_{x}") for x in ("scaled", "hi", "split"))

        def load(self, sp, u):
            sp.dma_start(weight_tile(raw[:, u, :]), self.tiles[u][0]).then_inc(self.loaded[u], 16)

        def scale(self, pool, u):
            pool.wait_ge(self.loaded[u], 16)
            if self.tiles[u][1] is not None:
                pool.tensor_tensor(weight_tile(raw[:, u, :]), weight_tile(raw[:, u, :]),
                                   gains[:, self.tiles[u][1], :].unsqueeze(2).to_broadcast([P, KD, P]),
                                   ALU.mult).then_inc(self.scaled, 1)
            else:
                pool.sem_inc(self.scaled, 1)
            pool.wait_ge(self.scaled, u + 1)

        def split(self, pool, u):
            pool.tensor_tensor(wh[:, u, :], raw[:, u, :], unit, ALU.mult).then_inc(self.hi, 1)
            pool.wait_ge(self.hi, u + 1)
            pool.tensor_tensor(wl[:, u, :], raw[:, u, :], wh[:, u, :].bitcast(F32), ALU.subtract)\
                .then_inc(self.lo, 1)

    def setup(following):
        xin, e = at("xin", [P, 10, D], F32, x_end)
        identw = sem("su_ident")
        const = sem("su_const")
        loads = [sem(f"su_x{i}") for i in range(2)]
        gl = sem("su_gains")
        copies = sem("su_cache_copies")
        turned = sem("su_turned")
        placed = sem("su_placed")
        nx = Prefetch("su", following)
        with nc.Block() as block:
            @block.sync
            def _(sp):
                for i in range(8):
                    if i == 4:
                        nx.load(sp, 0)
                        nx.load(sp, 1)
                    sp.dma_start(xin[:, i, :], a["x_prompt"][0, i * P:(i + 1) * P, :]).then_inc(loads[i // 4], 16)
                sp.dma_start(xin[:, 8, :], a["x_sample"].rearrange("b t d -> (b t) d")).then_inc(loads[1], 16)
                sp.dma_start(xin[0:META, 9, :], a["meta_tokens"]).then_inc(loads[1], 16)
                for w, c in (("win_k_s", "cache_win_k"), ("win_v_s", "cache_win_v")):
                    sp.dma_start(a[w][:, 0:WINDOW - TS], a[c][:, TS:WINDOW]).then_inc(copies, 16)
                sp.wait_ge(copies, 32)

            @block.scalar
            def _(act):
                for n, g in enumerate((a["norm_mix"][0], a["a_g_head"][0], a["norm_ffn"][0], a["g_kv"],
                                       a["norm_mix"][1], a["norm_ffn"][1])):
                    with nc.allow_non_contiguous_dma("gain columns"):
                        act.dma_start(gains[:, n, :], g.rearrange("(k p) -> p k", p=P)).then_inc(gl, 16)
                act.wait_ge(gl, 96)

            @block.gpsimd
            def _(pool):
                pool.memset(ident[:], 0.0).then_inc(identw, 1)
                pool.wait_ge(identw, 1)
                pool.affine_select(out=ident[:], in_=ident[:], compare_op=ALU.not_equal, fill=1.0, base=0,
                                   pattern=[[-1, P]], channel_multiplier=1).then_inc(const, 1)
                pool.memset(ones[:], 1.0).then_inc(const, 1)
                pool.memset(epsc[:], EPS).then_inc(const, 1)
                pool.memset(powc[:], -0.5).then_inc(const, 1)
                pool.wait_ge(const, 4)
                pool.wait_ge(gl, 96)
                for u in range(2):
                    nx.scale(pool, u)
                    nx.split(pool, u)

            @block.tensor
            def _(pe):
                pe.wait_ge(const, 4)
                for i in range(10):
                    n = META if i == 9 else P
                    if i == 0:
                        pe.wait_ge(loads[0], 16 * 4)
                    if i == 4:
                        pe.wait_ge(loads[1], 16 * 6)
                    for half in range(2):
                        u = 2 * i + half
                        if u >= 8:
                            pe.wait_ge(placed, u - 7)
                        for k in range(4):
                            t = pe.transpose(psum[:, u % 8, k * P:k * P + n],
                                             xin[0:n, i, (4 * half + k) * P:(4 * half + k + 1) * P], ident[0:n, 0:n])
                        t.then_inc(turned, 1)

            @block.vector
            def _(dve):
                for i in range(10):
                    n = META if i == 9 else P
                    col = 0 if i == 9 else META + i * P
                    for half in range(2):
                        u = 2 * i + half
                        dve.wait_ge(turned, u + 1)
                        dve.tensor_copy(h[:, 4 * half:4 * half + 4, col:col + n],
                                        psum[:, u % 8, :].rearrange("p (k t) -> p k t", k=4)[:, :, 0:n])\
                            .then_inc(placed, 1)

    class Prep:

        def __init__(self, name):
            self.hi, self.lo = sem(name + "_x_hi"), sem(name + "_x_lo")
            self.sq, self.summed = sem(name + "_squared"), sem(name + "_summed")
            self.total, self.root, self.rstd = sem(name + "_total"), sem(name + "_root"), sem(name + "_rstd")

        def act_split(self, act):
            for k in range(KD):
                act.activation(xh[:, k, :], h[:, k, :], ACT.Copy).then_inc(self.hi, 1)
            for k in range(KD):
                if k >= 2:
                    act.wait_ge(self.summed, k - 1)
                act.activation(sq[:, k % 2, :], h[:, k, :], ACT.Square).then_inc(self.sq, 1)

        def act_root(self, act):
            for c, (t0, n) in enumerate(TOK):
                act.wait_ge(self.total, c + 1)
                act.activation(rstd[:, t0:t0 + n], psum[:, 6 + c % 2, 0:n], ACT.Sqrt, scale=1.0 / D,
                               bias=epsc[:, 0:1]).then_inc(self.root, 1)

        def dve_split(self, dve):
            for k in range(KD):
                dve.wait_ge(self.hi, k + 1)
                dve.tensor_tensor(xl[:, k, :], h[:, k, :], xh[:, k, :].bitcast(F32), ALU.subtract)\
                    .then_inc(self.lo, 1)
            for k in range(KD):
                dve.wait_ge(self.sq, k + 1)
                if k == 0:
                    dve.tensor_copy(acc[:], sq[:, 0, :]).then_inc(self.summed, 1)
                else:
                    dve.wait_ge(self.summed, k)
                    dve.tensor_tensor(acc[:], acc[:], sq[:, k % 2, :], ALU.add).then_inc(self.summed, 1)

        def dve_rstd(self, dve):
            for c, (t0, n) in enumerate(TOK):
                dve.wait_ge(self.root, c + 1)
                dve.reciprocal(rstd[:, t0:t0 + n], rstd[:, t0:t0 + n]).then_inc(self.rstd, 1)

        def pe_total(self, pe):
            pe.wait_ge(self.summed, KD)
            for c, (t0, n) in enumerate(TOK):
                if c == 2:
                    pe.wait_ge(self.root, 1)
                pe.matmul(psum[:, 6 + c % 2, 0:n], ones[:], acc[:, t0:t0 + n], start=True, stop=True)\
                    .then_inc(self.total, 1)

    BETWEEN = 4

    def product(pe, bank, hi, lo, nk, bh, bl, ready=None, between=None):
        for k in range(nk):
            if ready is not None:
                pe.wait_ge(ready, k + 1)
            if between is not None and k == BETWEEN:
                between(pe)
            for n, (w, x) in enumerate(((hi, bh), (hi, bl), (lo, bh))):
                for c, (t0, nt) in enumerate(TOK):
                    mm = pe.matmul(psum[:, bank + c, 0:nt], w(k), x[:, k, t0:t0 + nt],
                                   start=(k == 0 and n == 0), stop=(k == nk - 1 and n == 2))
        return mm

    def dense(name, groups, following, prep=None, gates=None, load_x=None, tables=None):
        njobs = sum(2 * g.pairs for g in groups) + (1 if gates is not None else 0)
        loaded = [sem(f"{name}_w_loaded{u}") for u in range(2)]
        stored = [sem(f"{name}_stored{u}") for u in range(2)]
        scaled, hi_s, split = (sem(f"{name}_w_{x}") for x in ("scaled", "hi", "split"))
        job_done, evac, sig = (sem(f"{name}_{x}") for x in ("job_done", "evac", "activated"))
        swapped, part, xr, gm = (sem(f"{name}_{x}") for x in ("swapped", "part", "x_ready", "gate_memset"))
        xload = [sem(f"{name}_x_loaded{u}") for u in range(4)]
        tab = sem(f"{name}_tables")
        trot = sem(f"{name}_tables_scaled")
        gst = sem(f"{name}_gates_stored")
        storing = groups[0].kind != "residual"
        pr = Prep(name) if prep else None
        nx = Prefetch(name, following) if following else None
        G = njobs - 1
        hi_x = sem(f"{name}_x_hi2")

        def stored_before(r):
            return r * 16 + (48 if groups[0].kind == "rope_k" else 0)

        with nc.Block() as block:
            @block.sync
            def _(sp):
                if tables is not None:
                    sp.dma_start(cosr[:], a["rope_cos"]).then_inc(tab, 16)
                    sp.dma_start(sinr[:], a["rope_sin"]).then_inc(tab, 16)

                for u in range(2):
                    sp.sem_inc(loaded[u], 16)
                if load_x is not None:
                    for k in range(KD):
                        if k >= 4:
                            sp.wait_ge(xr, k - 3)
                        sp.dma_start(xring[:, k % 4, :], load_x[k]).then_inc(xload[k % 4], 16)

                def load(g, j, n, u, r):
                    if isinstance(n, int) and n < 2:
                        return
                    sp.wait_ge(split, n - 1)
                    sp.dma_start(weight_tile(raw[:, u, :]), g.weight(j)).then_inc(loaded[u], 16)

                over(sp, groups, load)
                if name == "out0":
                    sp.wait_ge(states_stored, 16 * N_STATE_STORES)
                if gates is not None:
                    sp.wait_ge(gm, 1)
                    for half in range(2):
                        sp.dma_start(weight_tile(raw[:, 0, :])[:, :, 32 * half:32 * half + HA],
                                     gates[:, :, HA * half:HA * half + HA]).then_inc(loaded[0], 16)
                if nx:
                    for u in range(2):
                        sp.wait_ge(split, njobs - 1 + (u ^ njobs % 2))
                        nx.load(sp, u)

            @block.gpsimd
            def _(pool):
                def split_w(g, j, n, u, r, gate_tile=False):
                    pool.wait_ge(loaded[u], r * 16 + (32 if gate_tile else 16))
                    if isinstance(n, int) and n < 2:
                        for x in (scaled, hi_s, split):
                            pool.sem_inc(x, 1)
                        return
                    if g.gain is not None:
                        pool.tensor_tensor(weight_tile(raw[:, u, :]), weight_tile(raw[:, u, :]),
                                           gains[:, g.gain, :].unsqueeze(2).to_broadcast([P, KD, P]),
                                           ALU.mult).then_inc(scaled, 1)
                        pool.wait_ge(scaled, n + 1)
                    if not (isinstance(n, int) and n < 2):
                        pool.wait_ge(job_done, n - 1)
                    pool.tensor_tensor(wh[:, u, :], raw[:, u, :], unit, ALU.mult).then_inc(hi_s, 1)
                    pool.wait_ge(hi_s, n + 1)
                    pool.tensor_tensor(wl[:, u, :], raw[:, u, :], wh[:, u, :].bitcast(F32), ALU.subtract)\
                        .then_inc(split, 1)

                over(pool, groups, split_w)
                if gates is not None:
                    pool.memset(raw[:, 0, :], 0.0).then_inc(gm, 1)
                    split_w(groups[0], None, G, 0, G // 2, gate_tile=True)
                if nx:
                    for u in range(2):
                        nx.scale(pool, u)
                        pool.wait_ge(job_done, njobs - 1 + (u ^ njobs % 2))
                        nx.split(pool, u)

            @block.tensor
            def _(pe):
                def job(g, j, n, u, r, ready=None):
                    pe.wait_ge(split, n + 1)
                    if not (isinstance(n, int) and n < 2):
                        rotary = tables is not None
                        pe.wait_ge(swapped if rotary else evac, n - 1)
                    hi, lo = weight_tile(wh[:, u, :]), weight_tile(wl[:, u, :])
                    if ready is None and isinstance(n, int) and n == 0:
                        ready = pr.lo if pr else (xr if load_x is not None else None)
                    product(pe, 3 * u, lambda k: hi[:, k, :], lambda k: lo[:, k, :], KD, xh, xl, ready,
                            pr.pe_total if isinstance(n, int) and n == 1 and pr else None).then_inc(job_done, 1)

                over(pe, groups, job)
                if gates is not None:
                    job(None, None, G, 0, G // 2)

            @block.scalar
            def _(act):
                if load_x is not None:
                    for k in range(KD):
                        act.wait_ge(xload[k % 4], 16 * (k // 4 + 1))
                        act.activation(xh[:, k, :], xring[:, k % 4, :], ACT.Copy).then_inc(hi_x, 1)
                if pr:
                    pr.act_split(act)
                    pr.act_root(act)

                def finish(g, j, n, u, r):
                    if g.kind == "sigmoid":
                        act.wait_ge(part, n - g.n0 + 1)
                        act.activation(tmp[:, u, :], tmp[:, u, :], ACT.Sigmoid).then_inc(sig, 1)
                        act.wait_ge(sig, n - g.n0 + 1)
                        act.dma_start(qkvo[ds(j + g.n0, 1)].rearrange("a p t -> (a p) t"), tmp[:, u, :])\
                            .then_inc(stored[u], 16)
                    elif g.kind == "store":
                        act.wait_ge(evac, n + 1)
                        act.dma_start(qkvo[ds(j + g.n0, 1)].rearrange("a p t -> (a p) t"), tmp[:, u, :])\
                            .then_inc(stored[u], 16)
                    elif g.kind in ("rope_k", "rope_q"):
                        act.wait_ge(part, n + 1)
                        if not (isinstance(n, int) and n == 0):
                            act.wait_ge(evac, n)
                        for q in range(4):
                            o, i = 32 * q, 32 * (q ^ 1)
                            for c, (t0, nt) in enumerate(TOK):
                                x = act.activation(swp[o:o + 32, t0:t0 + nt], psum[i:i + 32, 3 * u + c, 0:nt],
                                                   ACT.Copy)
                        x.then_inc(swapped, 1)
                        act.wait_ge(evac, n + 1)
                        if g.kind == "rope_k":
                            for hh in range(2):
                                for dup in range(2):
                                    act.dma_start(k2_d[2 * j + hh, HD * dup:HD * dup + HD, :],
                                                  tmp[HD * hh:HD * hh + HD, u, :]).then_inc(stored[u], 16)
                        else:
                            act.dma_start(qr_d[ds(j, 1)].rearrange("a p t -> (a p) t"), tmp[:, u, :])\
                                .then_inc(stored[u], 16)
                    elif g.kind == "plain_v":
                        act.wait_ge(evac, n + 1)
                        act.dma_start(vt_d[j], tmp[:, u, :]).then_inc(stored[u], 16)

                over(act, groups, finish)
                if gates is not None:
                    act.wait_ge(evac, G + 1)
                    for half in range(2):
                        act.dma_start(gates_d[half], tmp[0:4, half, :]).then_inc(gst, 16)
                    act.wait_ge(gst, 32)
                if storing:
                    for u in range(2):
                        act.wait_ge(stored[u], stored_before(njobs // 2))

            @block.vector
            def _(dve):
                if load_x is not None:
                    for k in range(KD):
                        dve.wait_ge(hi_x, k + 1)
                        dve.tensor_tensor(xl[:, k, :], xring[:, k % 4, :], xh[:, k, :].bitcast(F32), ALU.subtract)\
                            .then_inc(xr, 1)
                if pr:
                    pr.dve_split(dve)
                    pr.dve_rstd(dve)
                    dve.wait_ge(pr.rstd, 3)
                if tables is not None:
                    dve.wait_ge(tab, 32)
                    dve.tensor_tensor(cosr[:], cosr[:], rstd[:], ALU.mult).then_inc(trot, 1)
                    dve.tensor_tensor(sinr[:], sinr[:], rstd[:], ALU.mult).then_inc(trot, 1)
                    dve.wait_ge(trot, 2)

                def leave(g, j, n, u, r):
                    dve.wait_ge(job_done, n + 1)
                    if g.kind == "residual":
                        for c, (t0, nt) in enumerate(TOK):
                            x = dve.tensor_tensor(hcol(j + g.n0, t0, nt), hcol(j + g.n0, t0, nt), psum[:, 3 * u + c, 0:nt], ALU.add)
                        x.then_inc(evac, 1)
                        return
                    if not (isinstance(n, int) and n < 2):
                        dve.wait_ge(stored[u], stored_before(r))
                    if g.kind in ("rope_k", "rope_q"):
                        for c, (t0, nt) in enumerate(TOK):
                            x = dve.tensor_tensor(tmp[:, u, t0:t0 + nt], psum[:, 3 * u + c, 0:nt],
                                                  cosr[:, t0:t0 + nt], ALU.mult)
                        x.then_inc(part, 1)
                        dve.wait_ge(swapped, n + 1)
                        dve.tensor_tensor(swp[:], swp[:], sinr[:], ALU.mult).then_inc(sig, 1)
                        dve.wait_ge(sig, n + 1)
                        dve.wait_ge(part, n + 1)
                        dve.tensor_tensor(tmp[:, u, :], tmp[:, u, :], swp[:], ALU.add).then_inc(evac, 1)
                    elif g.kind == "sigmoid":
                        for c, (t0, nt) in enumerate(TOK):
                            x = dve.tensor_tensor(tmp[:, u, t0:t0 + nt], psum[:, 3 * u + c, 0:nt],
                                                  rstd[:, t0:t0 + nt], ALU.mult)
                        x.then_inc(part, 1)
                        dve.wait_ge(part, n - g.n0 + 1)
                        dve.sem_inc(evac, 1)
                    else:
                        for c, (t0, nt) in enumerate(TOK):
                            x = dve.tensor_tensor(tmp[:, u, t0:t0 + nt], psum[:, 3 * u + c, 0:nt],
                                                  rstd[:, t0:t0 + nt], ALU.mult)
                        x.then_inc(evac, 1)

                def hcol(j, t0, nt):
                    if isinstance(j, int):
                        return h[:, j, t0:t0 + nt]
                    return h[:, ds(j, 1), t0:t0 + nt].rearrange("p a t -> p (a t)")

                over(dve, groups, leave)
                if gates is not None:
                    dve.wait_ge(job_done, G + 1)
                    for u in range(2):
                        dve.wait_ge(stored[u], stored_before(G // 2))
                    for half in range(2):
                        for c, (t0, nt) in enumerate(TOK):
                            x = dve.tensor_tensor(tmp[0:4, half, t0:t0 + nt],
                                                  psum[32 * half:32 * half + 4, c, 0:nt],
                                                  rstd[0:4, t0:t0 + nt], ALU.mult)
                    x.then_inc(evac, 1)

    def ffn(name, w_gu, w_dn, gain, following):
        cols = slice(TOK[0][0], T)
        NG = DFF // P // 2
        NW = 6 * NG
        assert NW % 3 == 0 and NW % 2 == 0
        loaded = [sem(f"{name}_w_loaded{u}") for u in range(2)]
        scaled, hi_s, split = (sem(f"{name}_w_{x}") for x in ("scaled", "hi", "split"))
        nx = Prefetch(name, following) if following else None
        gu_done, gu_evac, silu, hid = (sem(f"{name}_{x}") for x in ("gate_up_done", "gate_up_evac", "silu", "hidden"))
        hhi, hlo, dn_done, dn_evac = (sem(f"{name}_{x}") for x in ("hid_hi", "hid_lo", "down_done", "down_evac"))
        pr = Prep(name)
        gu = w_gu.rearrange("(k p) n -> p k n", p=P)

        def source(kind, g, s):
            if kind == "d":
                return w_dn[ds((g * 2 + s) * P, P), :]
            return gu[:, :, ds((g * 2 + s) * P + (DFF if kind == "u" else 0), P)]

        FIRST = [("g", 0), ("u", 0), ("g", 1), ("u", 1)]
        BODY = [("g", 0), ("d", 0), ("d", 1), ("u", 0), ("g", 1), ("u", 1)]

        def stream(eng, body):
            for n, (kind, s) in enumerate(FIRST):
                body(kind, 0, s, n, n, n // 2)
            with eng.Fori(0, NG - 1) as i:
                for q, (kind, s) in enumerate(BODY):
                    body(kind, i if kind == "d" else i + 1, s, i * 6 + 4 + q, 4 + q, i * 3 + (4 + q) // 2)
            for s in range(2):
                n = 4 + 6 * (NG - 1) + s
                body("d", NG - 1, s, n, n, n // 2)

        with nc.Block() as block:
            @block.sync
            def _(sp):
                def load(kind, g, s, n, pos, r):
                    if pos < 2:
                        sp.sem_inc(loaded[pos], 16)
                        return
                    sp.wait_ge(split, n - 1)
                    dst = raw[:, pos % 2, :] if kind == "d" else weight_tile(raw[:, pos % 2, :])
                    sp.dma_start(dst, source(kind, g, s)).then_inc(loaded[pos % 2], 16)

                stream(sp, load)
                if nx:
                    for u in range(2):
                        sp.wait_ge(split, NW - 1 + u)
                        nx.load(sp, u)

            @block.gpsimd
            def _(pool):
                def split_w(kind, g, s, n, pos, rnd):
                    r, b = pos % 2, pos % 3
                    pool.wait_ge(loaded[r], rnd * 16 + 16)
                    if pos < 2:
                        for x in (scaled, hi_s, split):
                            pool.sem_inc(x, 1)
                        return
                    if kind != "d":
                        pool.tensor_tensor(weight_tile(raw[:, r, :]), weight_tile(raw[:, r, :]),
                                           gains[:, gain, :].unsqueeze(2).to_broadcast([P, KD, P]),
                                           ALU.mult).then_inc(scaled, 1)
                    else:
                        pool.sem_inc(scaled, 1)
                    pool.wait_ge(scaled, n + 1)
                    if pos == 3:
                        pool.wait_ge(gu_done, 1)
                    elif pos > 3:
                        i, q = (g, pos - 4) if pos < 10 else (NG - 1, s)
                        i = i if kind == "d" else g - 1
                        if q < 4:
                            pool.wait_ge(gu_done, i * 4 + (2 + q))
                        else:
                            pool.wait_ge(dn_done, i * 8 + 8)
                    pool.tensor_tensor(wh[:, b, :], raw[:, r, :], unit, ALU.mult).then_inc(hi_s, 1)
                    pool.wait_ge(hi_s, n + 1)
                    pool.tensor_tensor(wl[:, b, :], raw[:, r, :], wh[:, b, :].bitcast(F32), ALU.subtract)\
                        .then_inc(split, 1)

                stream(pool, split_w)
                if nx:
                    for u in range(2):
                        nx.scale(pool, u)
                        pool.wait_ge(gu_done if u == 0 else dn_done, (4 if u == 0 else KD) * NG)
                        nx.split(pool, u)

            @block.tensor
            def _(pe):
                def gate_up(n, pos, set_, first=False, between=None):
                    b = pos % 3
                    pe.wait_ge(split, n + 1)
                    hi, lo = weight_tile(wh[:, b, :]), weight_tile(wl[:, b, :])
                    mm = product(pe, 3 * set_, lambda k: hi[:, k, :], lambda k: lo[:, k, :], KD, xh, xl,
                                 pr.lo if first else None, between)
                    mm.then_inc(gu_done, 1)

                def down(n, pos, dn_n):
                    b0, b1 = pos % 3, (pos + 1) % 3
                    pe.wait_ge(split, n + 2)
                    hi = [wh[:, b0, :], wh[:, b1, :]]
                    lo = [wl[:, b0, :], wl[:, b1, :]]
                    for m in range(KD):
                        if m == 1:
                            pe.wait_ge(gu_evac, down_gu)
                        if m >= 2:
                            pe.wait_ge(dn_evac, dn_n + m - 1)
                        mm = product(pe, 3 * ((m + 1) % 2), lambda k: hi[k][:, m * P:(m + 1) * P],
                                     lambda k: lo[k][:, m * P:(m + 1) * P], 2, hidh, hidl)
                        mm.then_inc(dn_done, 1)

                for q in range(4):
                    if q >= 2:
                        pe.wait_ge(gu_evac, q - 1)
                    gate_up(q, q, q % 2, q == 0, pr.pe_total if q == 1 else None)
                with pe.Fori(0, NG - 1) as i:
                    n, g4, d8 = i * 6 + 4, i * 4 + 4, i * 8
                    pe.wait_ge(gu_evac, g4 - 1)
                    gate_up(n, 4, 0)
                    down_gu = g4 + 1
                    pe.wait_ge(hlo, i * 2 + 2)
                    pe.wait_ge(gu_evac, g4)
                    down(n + 1, 5, d8)
                    pe.wait_ge(dn_evac, d8 + 7)
                    gate_up(n + 3, 7, 1)
                    pe.wait_ge(dn_evac, d8 + 8)
                    gate_up(n + 4, 8, 0)
                    pe.wait_ge(gu_evac, g4 + 2)
                    gate_up(n + 5, 9, 1)
                N = 4 + 6 * (NG - 1)
                down_gu = 4 * NG
                pe.wait_ge(hlo, 2 * NG)
                pe.wait_ge(gu_evac, 4 * NG)
                down(N, N, 8 * (NG - 1))

            def gate_part(act, n2):
                act.wait_ge(gu_evac, n2 * 2 + 1)
                act.activation(gate[:, cols], gate[:, cols], ACT.Silu).then_inc(silu, 1)

            def hidden_part(act, n2, s):
                act.wait_ge(hid, n2 + 1)
                act.activation(hidh[:, s, cols], up[:, cols], ACT.Copy).then_inc(hhi, 1)

            @block.scalar
            def _(act):
                pr.act_split(act)
                pr.act_root(act)
                for s in range(2):
                    gate_part(act, s)
                    hidden_part(act, s, s)
                with act.Fori(1, NG) as i:
                    for s in range(2):
                        gate_part(act, i * 2 + s)
                        hidden_part(act, i * 2 + s, s)

            @block.vector
            def _(dve):
                pr.dve_split(dve)
                pr.dve_rstd(dve)
                dve.wait_ge(pr.rstd, 3)

                def take(n, dst, set_):
                    dve.wait_ge(gu_done, n + 1)
                    for c, (t0, nt) in enumerate(TOK):
                        x = dve.tensor_tensor(dst[:, t0:t0 + nt], psum[:, 3 * set_ + c, 0:nt], rstd[:, t0:t0 + nt],
                                              ALU.mult)
                    x.then_inc(gu_evac, 1)

                def gate_out(n2, set_, first=False):
                    if not first:
                        dve.wait_ge(hid, n2)
                    take(n2 * 2, gate, set_)

                def up_out(n2, s, set_, first=False):
                    if not first:
                        dve.wait_ge(hlo, n2)
                        dve.wait_ge(hhi, n2)
                    take(n2 * 2 + 1, up, set_)
                    dve.wait_ge(gu_evac, n2 * 2 + 2)
                    dve.wait_ge(silu, n2 + 1)
                    dve.tensor_tensor(up[:, cols], up[:, cols], gate[:, cols], ALU.mult).then_inc(hid, 1)
                    dve.wait_ge(hhi, n2 + 1)
                    dve.tensor_tensor(hidl[:, s, cols], up[:, cols], hidh[:, s, cols].bitcast(F32), ALU.subtract)\
                        .then_inc(hlo, 1)

                def down_out(d8):
                    for m in range(KD):
                        dve.wait_ge(dn_done, d8 + m + 1)
                        for c, (t0, nt) in enumerate(TOK):
                            x = dve.tensor_tensor(h[:, m, t0:t0 + nt], h[:, m, t0:t0 + nt],
                                                  psum[:, 3 * ((m + 1) % 2) + c, 0:nt], ALU.add)
                        x.then_inc(dn_evac, 1)

                gate_out(0, 0, True)
                up_out(0, 0, 1, True)
                gate_out(1, 0)
                up_out(1, 1, 1)
                with dve.Fori(1, NG) as i:
                    gate_out(i * 2, 0)
                    down_out(i * 8 - 8)
                    up_out(i * 2, 0, 1)
                    gate_out(i * 2 + 1, 0)
                    up_out(i * 2 + 1, 1, 1)
                down_out(8 * (NG - 1))

    wi, wo = wcols(a["a_w_in"][0]), wcols(a["a_w_out"][0])
    ga = a["a_w_in"][0].rearrange("(k p) n -> p k n", p=P)[:, :, 24 * P:24 * P + 2 * HA]
    wk, wv, wq = wcols(a["w_kv"]), wcols(a["w_kv"], 2 * P), wcols(a["b_w_q"][0])
    wo1 = wcols(a["b_w_o"][0])

    def two(w, gain):
        return [(w(0), gain), (w(1), gain)]

    def gate_and_up(layer, gain):
        w = a["w_gate_up"][layer]
        return [(wcols(w)(0), gain), (wcols(w, DFF)(0), gain)]

    def layer1_out():
        TOK[:] = TOK_REAL
        run(dense, "out1", [Group(0, 1, wo1, None, "residual"),
                            Group(2, 3, lambda j: wo1(j + 2), None, "residual")], gate_and_up(1, 5), load_x=og_d)

    S = dict(locals())
    phases = [
        lambda: run(setup, two(wi, 0)),
        lambda: run(dense, "in", [Group(0, 1, wi, 0, "store"), Group(2, 7, lambda j: wi(j + 2), 0, "store"),
                                  Group(16, 4, lambda j: wi(j + 16), 0, "sigmoid")], None, prep=True, gates=ga),
        lambda: run(mlstm, nc, a, S, two(wo, 1)),
        lambda: run(dense, "out0", [Group(0, 1, wo, 1, "residual"), Group(2, 3, lambda j: wo(j + 2), 1, "residual")],
                    gate_and_up(0, 2), load_x=og_d),
        lambda: run(ffn, "ffn0", a["w_gate_up"][0], a["w_down"][0], 2, two(wk, 3)),
        lambda: run(dense, "kvq", [Group(0, 1, wk, 3, "rope_k"), Group(2, 4, wq, 4, "rope_q"),
                                   Group(10, 1, wv, 3, "plain_v")], None, prep=True, tables=True),
        lambda: run(attention, nc, a, S, two(wo1, None)),
        layer1_out,
        lambda: run(ffn, "ffn1", a["w_gate_up"][1], a["w_down"][1], 5, None),
        lambda: run(final, nc, a, S),
    ]
    for phase_ in phases[:upto + 1]:
        phase_()


def mlstm(nc, a, s, following):
    at, sem, psum, ident = s["at"], s["sem"], s["psum"], s["ident"]
    qkvo, gates_d, og_d, ones = s["qkvo"], s["gates_d"], s["og_d"], s["ones"]
    place = [s["fixed_end"]]

    def sb(name, shape, dt=F32):
        t, place[0] = at("ml_" + name, shape, dt, place[0])
        return t

    top = [s["limit"] // 32 * 32]

    def sb_top(name, shape):
        top[0] -= int(np.prod(shape[1:])) * 4 // 32 * 32 + 32
        assert top[0] >= s["x_ring_end"]
        return at("ml_" + name, shape, F32, top[0])[0]

    E1 = DV + 1
    qc = sb("q", [P, 2, HA, MCH])
    kc = sb("k", [P, 2, HA, MCH])
    vc = sb("v", [P, 2, 2 * HA, MCH])
    oc = sb("o", [P, 2, 2 * HA, MCH])
    ex = sb("exp", [P, HA, MCH])
    pr = sb("weights", [P, HA, MCH])
    va = sb("v_ones", [P, HA, E1])
    kw = sb("k_weighted", [P, HA, MCH])
    inter = sb("inter", [P, HA, E1])
    num = sb("num", [P, HA, E1])
    hn = sb("hn", [P, HA, DV])
    junk = sb("junk", [P, DV])
    C = sb_top("state", [P, HA, E1])
    CS = sb_top("decode_state", [P, NB, HA, E1])
    col = sb("cols", [P, 10, 100])
    cc = sb("chunk_cols", [P, 2, 100])
    dec = sb("decays", [P, HA, 17])
    dc = sb("chunk_decay", [P, HA])
    small = sb("small", [P, 8, HA])
    sel = sb("select_head", [HA, HA, P])
    gi, gf, lsf, bb, mm, nm = (sb(x, [HA, T]) for x in ("logi", "f", "logf", "cumulated", "stabiliser", "neg_M"))
    qm, _ = at("ml_q_masked", [P, NB, MCH], F32, place[0])
    t1, keep = sb("t1", [HA, T]), sb("keep", [HA, T])
    rows = sb("rows", [P, T])
    sm = sb("state_m", [HA, NB])
    bg = sb("gate_bias", [HA, 2])
    dr = sb("decay_rows", [HA, 17])

    assert place[0] <= top[0]
    g_load, consts, rows_pe, dec_pe = (sem("ml_" + x) for x in ("gates_loaded", "consts", "rows_turned", "decays_pe"))
    dv, ac = sem("ml_rows_dve"), sem("ml_rows_act")
    cols_ev, dec_ev, st_load, m_out = (sem("ml_" + x) for x in ("cols_evac", "decays_evac", "states_loaded", "m_stored"))
    o_load = [sem(f"ml_gate_loaded{u}") for u in range(2)]
    c_load = [sem(f"ml_chunk_loaded{u}") for u in range(2)]
    (mb, sc, kt, vt, pv, upd, ht) = (sem("ml_pe_" + x) for x in
                                          ("minus_m", "scores", "k_turned", "v_turned", "intra", "update", "h_turned"))
    (exps, kws, ints, ssq) = (sem("ml_act_" + x) for x in ("exp", "k_weighted", "inter", "squares"))
    (prs, vas, nums, den, rden, root, rinv, fac, hns, cup, ogs) = (
        sem("ml_dve_" + x) for x in ("weights", "values", "num", "den", "rden", "mean_square", "rinv", "factor", "hn", "state", "gated"))
    (ccs, msk) = (sem("ml_pool_" + x) for x in ("chunk_cols", "masked"))
    og_st = [sem(f"ml_out_stored{u}") for u in range(2)]
    c_out = s["states_stored"]
    qms, kwms, cs_up, cs_pe, zero = (sem("ml_" + x) for x in (
        "q_masked", "seq_k_weighted", "seq_state", "seq_update", "zeroed"))

    dcs = sem("ml_pool_chunk_decay")
    kept = sem("ml_keep_and_rows_set")
    qzero = sem("ml_pool_q_masked_zeroed")
    nx = s["Prefetch"]("ml", following)
    qcs_h, local, aden = sem("ml_pe_inter_head"), sem("ml_rows_local"), sem("ml_dve_abs_den")

    def diag_blocks(t):
        x = t[:]
        return bass.AP(x.tensor, x.offset, [list(x.ap[0]), [MCH + TS, NB], [1, TS]])

    CHN = [(0, 0, META)] + [(c, META + MCH * (c - 1), MCH) for c in range(1, NMC + 1)] + [(NMC + 1, T_S, NS)]

    def chunks(eng, body):
        m = (0, 0, META, 0, 0)
        body(*m, None)
        c1 = (1, META, MCH, 1, 0)
        body(*c1, m)
        c2 = (2, META + MCH, MCH, 0, 1)
        body(*c2, c1)
        with eng.Fori(1, NMC // 2) as i:
            t = i * (2 * MCH)
            for u in range(2):
                body(i * 2 + (1 + u), t + (META + u * MCH), MCH, (1 + u) % 2, i + u,
                     (i * 2 + u, t + (META + (u - 1) * MCH), MCH, u, i))
        body(*LAST, (NMC, T_S - MCH, MCH, 0, NMC // 2))

    SEQ_BANKS = [0, 5, 3, 4]
    LAST = (NMC + 1, T_S, NS, 1, NMC // 2)

    with nc.Block() as block:
        @block.sync
        def _(sp):
            sp.dma_start(gi[:], gates_d[0]).then_inc(g_load, 16)
            sp.dma_start(gf[:], gates_d[1]).then_inc(g_load, 16)
            with nc.allow_non_contiguous_dma("small"):
                sp.dma_start(bg[:], a["a_b_gate"][0].rearrange("(i h) -> h i", i=2)).then_inc(g_load, 16)
                sp.dma_start(sm[:], a["state_m"].rearrange("b a h -> h (a b)")).then_inc(g_load, 16)

            def load(c, t0, n, u, r):
                if not (isinstance(c, int) and c < 2):
                    sp.wait_ge(upd, c * HA - HA)
                for dst, r0, nr in ((qc, 0, 4), (kc, 4, 4), (vc, 8, 8)):
                    sp.dma_start(dst[:, u, :, 0:n], qkvo[r0:r0 + nr, :, ds(t0, n)].rearrange("j p t -> p j t"))\
                        .then_inc(c_load[u], 16)
                if not (isinstance(c, int) and c < 2):
                    sp.wait_ge(og_st[u], r * 16)
                sp.dma_start(oc[:, u, :, 0:n], qkvo[16:24, :, ds(t0, n)].rearrange("j p t -> p j t"))\
                    .then_inc(o_load[u], 16)

            load(0, 0, META, 0, 0)
            load(1, META, MCH, 1, 0)
            nx.load(sp, 0)
            nx.load(sp, 1)
            for b in range(NB):
                sp.dma_start(CS[:, b, :, 0:DV], a["state_c"][b, 0].rearrange("h d e -> d h e")).then_inc(st_load, 16)
                with nc.allow_non_contiguous_dma("normaliser columns"):
                    sp.dma_start(CS[:, b, :, DV], a["state_n"][b, 0].rearrange("h d -> d h")).then_inc(st_load, 16)
            load(2, META + MCH, MCH, 0, 1)
            with sp.Fori(1, NMC // 2) as i:
                for u in range(2):
                    load(i * 2 + (1 + u), i * (2 * MCH) + (META + u * MCH), MCH, (1 + u) % 2, i + u)
            load(NMC + 1, T_S, NS, 1, NMC // 2)
            for hd in range(HA):
                sp.wait_ge(cs_up, NB * (hd + 1))
                sp.dma_start(a["c_s"][:, 0, hd].rearrange("b d e -> d b e"), CS[:, :, hd, 0:DV]).then_inc(c_out, 16)
            sp.dma_start(a["c_p"][0, 0].rearrange("h d e -> d h e"), C[:, :, 0:DV]).then_inc(c_out, 16)
            with nc.allow_non_contiguous_dma("normaliser columns"):
                sp.dma_start(a["n_p"][0, 0].rearrange("h d -> d h"), C[:, :, DV]).then_inc(c_out, 16)
                for b in range(NB):
                    sp.dma_start(a["n_s"][b, 0].rearrange("h d -> d h"), CS[:, b, :, DV]).then_inc(c_out, 16)
            sp.wait_ge(dv, 5)
            with nc.allow_non_contiguous_dma("small"):
                sp.dma_start(a["m_p"].rearrange("b a h -> h (a b)"), mm[:, T_S - 1:T_S]).then_inc(m_out, 16)
                sp.dma_start(a["m_s"].rearrange("b a h -> h (a b)"), mm[:, T_S + TS - 1:T:TS]).then_inc(m_out, 16)
            sp.wait_ge(m_out, 32)

        @block.gpsimd
        def _(pool):
            pool.memset(keep[:], 1.0).then_inc(kept, 1)
            pool.wait_ge(kept, 1)
            pool.memset(keep[:, META:T_S:MCH], 0.0).then_inc(kept, 1)
            pool.memset(keep[:, T_S:T:TS], 0.0).then_inc(kept, 1)
            pool.memset(rows[:], 0.0).then_inc(kept, 1)
            pool.memset(sel[:], 0.0).then_inc(zero, 1)
            pool.wait_ge(zero, 1)
            pool.affine_select(out=sel[:], in_=sel[:], compare_op=ALU.not_equal, fill=1.0, base=0,
                               pattern=[[-1, HA], [0, P]], channel_multiplier=1).then_inc(consts, 1)
            pool.memset(va[:, :, DV:E1], 1.0).then_inc(consts, 1)
            for u in range(2):
                nx.scale(pool, u)
                nx.split(pool, u)

            def rms(c, n):
                pool.wait_ge(root, c + 1)
                pool.tensor_tensor(small[0:n, 4, :], small[0:n, 3, :], s["powc"][0:n].to_broadcast([n, HA]), ALU.pow)\
                    .then_inc(rinv, 1)

            def step(c, t0, n, u, r, before):
                if isinstance(c, int) and c == 0:
                    pool.wait_ge(cols_ev, 10)
                    pool.wait_ge(dec_ev, 1)
                    pool.memset(qm[:], 0.0).then_inc(qzero, 1)
                elif not (isinstance(c, int) and c == 1):
                    pool.wait_ge(hns, c * HA - HA)
                if isinstance(c, int):
                    pool.tensor_copy(cc[0:n, u, :], col[0:n, c, :]).then_inc(ccs, 1)
                else:
                    pool.tensor_copy(cc[:, u, :], col[:, ds(c, 1), :].rearrange("p a x -> p (a x)")).then_inc(ccs, 1)
                if before:
                    rms(before[0], before[2])
                    pool.wait_ge(cup, c * HA)
                pool.wait_ge(exps, c * HA + HA)
                if isinstance(c, int):
                    pool.tensor_copy(dc[:], dec[:, :, c]).then_inc(dcs, 1)
                else:
                    pool.tensor_copy(dc[:], dec[:, :, ds(c, 1)].rearrange("p h a -> p (h a)")).then_inc(dcs, 1)
                e = ex[0:n, :, 0:n]
                x = pool.affine_select(out=e, in_=e, compare_op=ALU.is_ge, fill=0.0, base=0,
                                       pattern=[[0, HA], [1, n]], channel_multiplier=-1)
                x.then_inc(msk, 1)
                if isinstance(c, int) and c == NMC + 1:
                    pool.wait_ge(msk, c + 1)
                    e = ex[:].rearrange("p h (b t) -> p h b t", t=TS)
                    pool.affine_select(out=e, in_=e, compare_op=ALU.is_ge, fill=0.0, base=0,
                                       pattern=[[0, HA], [-TS, NB], [0, TS]], channel_multiplier=1).then_inc(msk, 1)

            chunks(pool, step)
            rms(LAST[0], LAST[2])

        def masked(c):
            return NMC + 3 if isinstance(c, int) and c == NMC + 1 else c + 1

        @block.tensor
        def _(pe):
            pe.wait_ge(consts, 2)
            pe.wait_ge(ac, 5)
            pe.wait_ge(dv, 11)
            for c, t0, n in CHN:
                if c >= 4:
                    pe.wait_ge(cols_ev, c - 3)
                pe.transpose(psum[0:n, c % 4, 0:100], rows[0:100, t0:t0 + n], ident[0:100, 0:100]).then_inc(rows_pe, 1)
            for hd in range(HA):
                x = pe.matmul(psum[:, 4, hd * 17:hd * 17 + 17], sel[:, hd, :], dr[:], start=True, stop=True)
            x.then_inc(dec_pe, 1)

            def turn_back(c, n):
                pe.wait_ge(hns, c * HA + HA)
                for j in range(2 * HA):
                    x = pe.transpose(psum[:, 5 + j // 4, (j % 4) * MCH:(j % 4) * MCH + n],
                                     hn[0:n, j // 2, (j % 2) * P:(j % 2 + 1) * P], ident[0:n, 0:n])
                    if j % 4 == 3:
                        x.then_inc(ht, 1)

            def step(c, t0, n, u, r, before):
                last = isinstance(c, int) and c == NMC + 1
                first = isinstance(c, int) and c == 0
                if first:
                    pe.wait_ge(cols_ev, 10)
                    pe.wait_ge(dec_ev, 1)
                elif not (isinstance(c, int) and c == 1):
                    pe.wait_ge(ogs, c * 2 - 2)
                if not first:
                    pe.wait_ge(exps, c * HA)
                for hd in range(HA):
                    rhs = nm[:, t0:t0 + n] if isinstance(c, int) else nm[:, ds(t0, n)]
                    x = pe.matmul(psum[0:n, 6, hd * MCH:hd * MCH + n], sel[:, hd, 0:n], rhs, start=True, stop=True)
                x.then_inc(mb, 1)
                pe.wait_ge(c_load[u], r * 48 + 48)
                if not first:
                    pe.wait_ge(kws, c * HA)
                for hd in range(HA):
                    x = pe.transpose(psum[0:n, 7, hd * MCH:hd * MCH + MCH], kc[:, u, hd, 0:n], ident[:])
                x.then_inc(kt, 1)
                if not first:
                    pe.wait_ge(nums, c * HA)
                for j in range(2 * HA):
                    x = pe.transpose(psum[0:n, 1 + j // 4, (j % 4) * P:(j % 4 + 1) * P], vc[:, u, j, 0:n], ident[:])
                x.then_inc(vt, 1)
                if not first:
                    pe.wait_ge(cup, c * HA)
                for hd in range(HA):
                    x = pe.matmul(psum[0:n, 0, hd * MCH:hd * MCH + n], kc[:, u, hd, 0:n], qc[:, u, hd, 0:n],
                                  start=True, stop=True)
                x.then_inc(sc, 1)
                if last:
                    pe.wait_ge(st_load, 16 * 2 * NB)
                for hd in range(HA):
                    o = psum[0:n, 3 + hd % 2, 0:E1]
                    if first:
                        continue
                    if hd >= 2:
                        pe.wait_ge(ints, (c - 1) * HA + hd - 1)
                    if not last:
                        pe.matmul(o, qc[:, u, hd, 0:n], C[:, hd, :], start=True, stop=True).then_inc(qcs_h, 1)
                    else:
                        pe.wait_ge(qms, hd + 1)
                        for b in range(NB):
                            x = pe.matmul(o, qm[:, b, :], CS[:, b, hd, :], start=(b == 0), stop=(b == NB - 1))
                        x.then_inc(qcs_h, 1)
                if not first:
                    pe.wait_ge(exps, c * HA + HA)
                    turn_back(before[0], before[2])
                pe.wait_ge(vas, c * 2 + 2)
                pe.wait_ge(prs, c + 1)
                for hd in range(HA):
                    if hd >= 2:
                        pe.wait_ge(nums, c * HA + hd - 1)
                    pe.matmul(psum[0:n, 1 + hd % 2, 0:E1], pr[0:n, hd, 0:n], va[0:n, hd, :], start=True, stop=True)\
                        .then_inc(pv, 1)
                if not first:
                    pe.wait_ge(ogs, c * 2)
                if not last:
                    for hd in range(HA):
                        pe.wait_ge(kws, c * HA + hd + 1)
                        if hd >= 2:
                            pe.wait_ge(cup, c * HA + hd - 1)
                        pe.matmul(psum[:, 5 if hd % 2 else 0, 0:E1], kw[0:n, hd, :], va[0:n, hd, :],
                                  start=True, stop=True).then_inc(upd, 1)
                else:
                    for n2 in range(NB * HA):
                        pe.wait_ge(kwms, n2 + 1)
                        if n2 >= 4:
                            pe.wait_ge(cs_up, n2 - 3)
                        pe.matmul(psum[:, SEQ_BANKS[n2 % 4], 0:E1], kw[:, n2 % 4, :], va[:, n2 // NB, :],
                                  start=True, stop=True).then_inc(cs_pe, 1)

            chunks(pe, step)
            pe.wait_ge(cs_up, NB * HA)
            turn_back(LAST[0], LAST[2])

        @block.scalar
        def _(act):
            act.wait_ge(dv, 1)
            act.activation(t1[:], t1[:], ACT.Exp, scale=-1.0).then_inc(ac, 1)
            act.wait_ge(ac, 1)
            act.activation(t1[:], t1[:], ACT.Ln, bias=ones[0:HA, 0:1]).then_inc(ac, 1)
            act.wait_ge(kept, 4)
            act.wait_ge(dv, 9)
            act.activation(rows[32:32 + HA, :], t1[:], ACT.Exp).then_inc(ac, 1)
            act.activation(rows[64:64 + HA, :], mm[:], ACT.Exp, scale=-1.0).then_inc(ac, 1)
            act.activation(rows[0:HA, :], keep[:], ACT.Copy).then_inc(ac, 1)

            def store(c, t0, n, u, r):
                act.wait_ge(ogs, c * 2 + 2)
                act.dma_start(og_d[:, :, ds(t0, n)].rearrange("j p t -> p j t"), oc[:, u, :, 0:n])\
                    .then_inc(og_st[u], 16)

            def step(c, t0, n, u, r, before):
                last = isinstance(c, int) and c == NMC + 1
                first = isinstance(c, int) and c == 0
                act.wait_ge(mb, c + 1)
                act.wait_ge(ccs, c + 1)
                if not first:
                    act.wait_ge(prs, c)
                    act.wait_ge(kws, c * HA)
                for hd in range(HA):
                    act.activation(ex[0:n, hd, 0:n], psum[0:n, 6, hd * MCH:hd * MCH + n], ACT.Exp,
                                   bias=cc[0:n, u, hd:hd + 1]).then_inc(exps, 1)
                if not last:
                    act.wait_ge(kt, c + 1)
                    act.wait_ge(msk, masked(c))
                    if not first:
                        act.wait_ge(upd, c * HA)
                    for hd in range(HA):
                        act.activation(kw[0:n, hd, :], psum[0:n, 7, hd * MCH:(hd + 1) * MCH], ACT.Copy,
                                       scale=ex[0:n, hd, n - 1:n]).then_inc(kws, 1)
                for hd in range(HA):
                    if first:
                        continue
                    act.wait_ge(qcs_h, (c - 1) * HA + hd + 1)
                    act.wait_ge(nums, c * HA)
                    act.activation(inter[0:n, hd, :], psum[0:n, 3 + hd % 2, 0:E1], ACT.Copy,
                                   scale=cc[0:n, u, 96 + hd:97 + hd]).then_inc(ints, 1)
                if before:
                    store(*before)
                act.wait_ge(rden, c + 1)
                for hd in range(HA):
                    if not (first and hd == 0):
                        act.wait_ge(ssq, c * HA + hd)
                    act.activation(junk[0:n, :], num[0:n, hd, 0:DV], ACT.Square, scale=small[0:n, 1, hd:hd + 1],
                                   accum_out=small[0:n, 2, hd:hd + 1]).then_inc(ssq, 1)
                if last:
                    act.wait_ge(kt, c + 1)
                    act.wait_ge(msk, masked(c))
                    act.wait_ge(upd, c * HA)
                    for hd in range(HA):
                        for b in range(NB):
                            n2 = hd * NB + b
                            if n2 >= 4:
                                act.wait_ge(cs_pe, n2 - 3)
                            act.activation(kw[:, n2 % 4, :], psum[:, 7, hd * MCH:(hd + 1) * MCH], ACT.Copy,
                                           scale=ex[:, hd, TS * b + TS - 1:TS * b + TS]).then_inc(kwms, 1)

            chunks(act, step)
            store(*LAST)
            for u in range(2):
                act.wait_ge(og_st[u], 16 * 5)

        @block.vector
        def _(dve):
            dve.wait_ge(g_load, 64)
            dve.tensor_scalar(gf[:], gf[:], bg[:, 1:2], None, ALU.add).then_inc(local, 1)
            dve.wait_ge(local, 1)
            dve.scalar_tensor_tensor(t1[:], gf[:], -1.0, gf[:], ALU.mult, ALU.max).then_inc(dv, 1)
            dve.tensor_scalar(gi[:], gi[:], bg[:, 0:1], None, ALU.add).then_inc(local, 1)
            dve.wait_ge(local, 2)
            dve.wait_ge(ac, 2)
            dve.scalar_tensor_tensor(lsf[:], gf[:], 0.0, t1[:], ALU.min, ALU.subtract).then_inc(dv, 1)
            dve.wait_ge(dv, 2)
            dve.wait_ge(kept, 4)
            dve.tensor_tensor_scan(bb[:], keep[:], lsf[:], 0.0, ALU.mult, ALU.add).then_inc(dv, 1)
            dve.tensor_tensor_scan(mm[:, 0:T_S], lsf[:, 0:T_S], gi[:, 0:T_S], 0.0, ALU.add, ALU.max).then_inc(dv, 1)
            for b in range(NB):
                w = slice(T_S + b * TS, T_S + (b + 1) * TS)
                x = dve.tensor_tensor_scan(mm[:, w], lsf[:, w], gi[:, w], sm[:, b:b + 1], ALU.add, ALU.max)
            x.then_inc(dv, 1)
            dve.wait_ge(dv, 5)
            dve.tensor_tensor(nm[:], bb[:], mm[:], ALU.subtract).then_inc(dv, 1)
            dve.wait_ge(dv, 6)
            dve.tensor_copy(t1[:, 0:META], nm[:, 0:META]).then_inc(local, 1)
            v = lambda x, w, n: x.rearrange("p (c t) -> p c t", t=n)
            dve.tensor_tensor(v(t1[:, META:T_S], 0, MCH), v(nm[:, META:T_S], 0, MCH),
                              mm[:, META - 1:T_S - 1:MCH].unsqueeze(2).to_broadcast([HA, NMC, MCH]), ALU.add)\
                .then_inc(dv, 1)
            dve.tensor_tensor(v(t1[:, T_S:T], 0, TS), v(nm[:, T_S:T], 0, TS),
                              sm[:].unsqueeze(2).to_broadcast([HA, NB, TS]), ALU.add).then_inc(dv, 1)
            dve.wait_ge(local, 3)
            dve.tensor_tensor(keep[:], gi[:], bb[:], ALU.subtract).then_inc(dv, 1)
            dve.wait_ge(ac, 3)
            dve.tensor_scalar(rows[96:96 + HA, :], rows[32:32 + HA, :], QSCALE, None, ALU.mult).then_inc(dv, 1)
            dve.tensor_copy(dr[:, 0:1], rows[32:32 + HA, META - 1:META]).then_inc(local, 1)
            dve.tensor_copy(dr[:, 1:1 + NMC], rows[32:32 + HA, META + MCH - 1:T_S:MCH]).then_inc(local, 1)
            dve.tensor_copy(dr[:, 1 + NMC:], rows[32:32 + HA, T_S + TS - 1:T:TS]).then_inc(local, 1)
            dve.wait_ge(local, 6)
            dve.sem_inc(dv, 1)
            for c, t0, n in CHN:
                dve.wait_ge(rows_pe, c + 1)
                dve.tensor_copy(col[0:n, c, :], psum[0:n, c % 4, 0:100]).then_inc(cols_ev, 1)
            dve.wait_ge(dec_pe, 1)
            dve.tensor_copy(dec[:], psum[:, 4, 0:HA * 17].rearrange("p (h x) -> p h x", h=HA)).then_inc(dec_ev, 1)

            def gated(c, t0, n, u, r):
                dve.wait_ge(o_load[u], r * 16 + 16)
                for j in range(2):
                    dve.wait_ge(ht, c * 2 + j + 1)
                    o = oc[:, u, 4 * j:4 * j + 4, 0:n]
                    dve.tensor_tensor(o, o, psum[:, 5 + j, :].rearrange("p (k t) -> p k t", k=4)[:, :, 0:n], ALU.mult)\
                        .then_inc(ogs, 1)

            def step(c, t0, n, u, r, before):
                last = isinstance(c, int) and c == NMC + 1
                first = isinstance(c, int) and c == 0
                dve.wait_ge(vt, c + 1)
                if not first:
                    dve.wait_ge(upd, c * HA)
                for j in range(2):
                    dve.tensor_copy(va[0:n, 2 * j:2 * j + 2, 0:DV],
                                    psum[0:n, 1 + j, :].rearrange("p (h e) -> p h e", h=2)).then_inc(vas, 1)
                dve.wait_ge(sc, c + 1)
                dve.wait_ge(msk, masked(c))
                if not first:
                    dve.wait_ge(pv, c * HA)
                dve.scalar_tensor_tensor(pr[0:n, :, 0:n], psum[0:n, 0, :].rearrange("p (h t) -> p h t", h=HA)[:, :, 0:n],
                                         QSCALE, ex[0:n, :, 0:n], ALU.mult, ALU.mult).then_inc(prs, 1)
                if last:
                    for hd in range(HA):
                        if hd == 0:
                            dve.wait_ge(qzero, 1)
                            dve.wait_ge(c_load[u], r * 48 + 48)
                        else:
                            dve.wait_ge(qcs_h, (c - 1) * HA + hd)
                        dve.tensor_copy(diag_blocks(qm), qc[:, u, hd, :].rearrange("p (b t) -> p b t", t=TS))\
                            .then_inc(qms, 1)
                if before:
                    gated(*before)
                if not first:
                    dve.wait_ge(ssq, c * HA)
                    dve.wait_ge(hns, c * HA)
                for hd in range(HA):
                    dve.wait_ge(pv, c * HA + hd + 1)
                    o = psum[0:n, 1 + hd % 2, 0:E1]
                    if first:
                        dve.tensor_copy(num[0:n, hd, :], o).then_inc(nums, 1)
                    else:
                        dve.wait_ge(ints, (c - 1) * HA + hd + 1)
                        dve.tensor_tensor(num[0:n, hd, :], inter[0:n, hd, :], o, ALU.add).then_inc(nums, 1)
                dve.wait_ge(nums, c * HA + HA)
                dve.scalar_tensor_tensor(small[0:n, 6, :], num[0:n, :, DV], -1.0, num[0:n, :, DV],
                                         ALU.mult, ALU.max).then_inc(aden, 1)
                dve.wait_ge(aden, c + 1)
                dve.tensor_tensor(small[0:n, 0, :], small[0:n, 6, :], cc[0:n, u, 64:64 + HA], ALU.max).then_inc(den, 1)
                dve.wait_ge(den, c + 1)
                dve.reciprocal(small[0:n, 1, :], small[0:n, 0, :]).then_inc(rden, 1)
                if not last:
                    dve.wait_ge(dcs, c + 1)
                    for hd in range(HA):
                        dve.wait_ge(upd, c * HA + hd + 1)
                        o = psum[:, 5 if hd % 2 else 0, 0:E1]
                        if first:
                            dve.tensor_copy(C[:, hd, :], o).then_inc(cup, 1)
                        else:
                            dve.scalar_tensor_tensor(C[:, hd, :], C[:, hd, :], dc[:, hd:hd + 1], o,
                                                     ALU.mult, ALU.add).then_inc(cup, 1)
                dve.wait_ge(ssq, c * HA + HA)
                dve.tensor_scalar(small[0:n, 3, :], small[0:n, 2, :], 1.0 / DV, EPS, ALU.mult, ALU.add)\
                    .then_inc(root, 1)
                dve.wait_ge(rinv, c + 1)
                dve.tensor_tensor(small[0:n, 5, :], small[0:n, 4, :], small[0:n, 1, :], ALU.mult).then_inc(fac, 1)
                dve.wait_ge(fac, c + 1)
                for hd in range(HA):
                    dve.tensor_scalar(hn[0:n, hd, :], num[0:n, hd, 0:DV], small[0:n, 5, hd:hd + 1], None, ALU.mult)\
                        .then_inc(hns, 1)
                if last:
                    for n2 in range(NB * HA):
                        hd, b = n2 // NB, n2 % NB
                        dve.wait_ge(cs_pe, n2 + 1)
                        dve.scalar_tensor_tensor(CS[:, b, hd, :], CS[:, b, hd, :], dec[:, hd, 1 + NMC + b:2 + NMC + b],
                                                 psum[:, SEQ_BANKS[n2 % 4], 0:E1], ALU.mult, ALU.add).then_inc(cs_up, 1)

            chunks(dve, step)
            gated(*LAST)


def attention(nc, a, s, following):
    at, sem, psum, ident = s["at"], s["sem"], s["psum"], s["ident"]
    k2_d, vt_d, qr_d, og_d = s["k2_d"], s["vt_d"], s["qr_d"], s["og_d"]
    place = [s["fixed_end"]]

    def sb(name, shape, dt=F32):
        t, place[0] = at("at_" + name, shape, dt, place[0])
        return t

    NU = 2 * KVH
    KW = META + WINDOW
    SK = META + CHUNK + TS
    CACHED = META + CHUNK
    NP = SEQ // CHUNK
    R = 2 * TS
    SB = P // R
    NSTEP = NP + NB // SB
    groups = [(0, META), (T_S - WINDOW, WINDOW), (T_S, NS)]
    kk, vv = sb("k_out", [P, 3, 2, P]), sb("v_out", [P, 3, 2, P])
    kv = sb("kv_rows", [P, 3, 2, 2 * P])
    q = sb("q", [P, 2, KD, CHUNK])
    qdl = sb("q_decode_loaded", [P, KD, NS])
    qd = sb("q_decode", [P, NB, KD, TS])
    k = sb("k", [P, 2, KVH, KW])
    v = sb("v", [P, 2, 2, WINDOW])
    vm = sb("v_meta", [P, NU, HD])
    pbm = sb("prob_meta", [P, 2, NU, META])
    vw = sb("v_window", [P, 2 * P])
    pb = sb("prob", [P, 2, NU, KW])
    pt = sb("prob_turned", [P, NU, P])
    pm = sb("prob_meta_turned", [P, P])
    ob = sb("out", [P, 2, KD, CHUNK])
    st = sb("stats", [P, 2, 8, NU])
    sink = sb("sink", [P, NU])
    sinks = sb("sink_decode", [P, NU])
    kct = sb("k_cached", [SK, NB, 2 * P])
    vct = sb("v_cached", [SK, NB, 2 * P])
    ks = sb("k_decode", [P, NB, KVH, SK])

    kvl, kvt, kve, kvo = (sem("at_kv_" + x) for x in ("loaded", "turned", "evac", "stored"))
    nx = s["Prefetch"]("at", following)
    cst, vml, vmz = sem("at_constants_loaded"), sem("at_v_meta_loaded"), sem("at_v_meta_zeroed")
    ld = [sem(f"at_chunk_loaded{u}") for u in range(2)]
    ldv = [sem(f"at_v_loaded{u}") for u in range(2)]
    st_o = [sem(f"at_out_stored{u}") for u in range(2)]
    dl = sem("at_decode_loaded")
    (sc, vt, ptd, pmd, pv) = (sem("at_pe_" + x) for x in ("scores", "v_turned", "p_turned", "p_meta_turned", "values"))
    (ex, es) = (sem("at_act_" + x) for x in ("exp", "sink"))
    obs = sem("at_act_out")
    (mx, mxs, neg, dsk, den, rdn, nrm, vws, pts, pms) = (sem("at_dve_" + x) for x in (
        "max", "max_sink", "neg_max", "sink_less_max", "den", "rden", "normal", "v_window", "p_turned", "p_meta"))
    dln = sem("at_decode_new_rows")
    snk = sem("at_decode_sinks")
    kml = sem("at_k_meta_loaded")
    qde = sem("at_pool_q_decode")
    kct_t = sem("at_pe_k_decode_turned")
    kse = [sem("at_dve_k_decode"), sem("at_act_k_decode")]

    def ahead(eng, first_part, second_part, middle=None, start=None):
        first_part(0, CHUNK, 0, 0)
        if start is not None:
            start(eng)
        for i in range(4):
            first_part(i + 1, WINDOW, (i + 1) % 2, (i + 1) // 2)
            if i == 3 and middle is not None:
                middle(eng)
            second_part(i, CHUNK if i == 0 else WINDOW, i % 2, i // 2)
        with eng.Fori(2, NP // 2 - 1) as i:
            for u in range(2):
                first_part(i * 2 + (u + 1), WINDOW, (u + 1) % 2, i + u)
                second_part(i * 2 + u, WINDOW, u, i)
        for i in range(NP - 2, NSTEP):
            if i + 1 < NSTEP:
                first_part(i + 1, WINDOW, (i + 1) % 2, (i + 1) // 2)
            second_part(i, WINDOW, i % 2, i // 2)

    def width(i):
        return SK if decode(i) else META + (CHUNK if isinstance(i, int) and i == 0 else WINDOW)

    CACHED_BANK = [[4, 5], [6, 5]]

    def decode(i):
        return isinstance(i, int) and i >= NP

    def later(i, than=0):
        return not isinstance(i, int) or i > than

    with nc.Block() as block:
        @block.sync
        def _(sp):
            def load(i, w, u):
                if decode(i):
                    return
                if later(i, 1):
                    sp.wait_ge(sc, i * 2 - 2)
                t = META + CHUNK * i if isinstance(i, int) else i * CHUNK + META
                w0 = t + CHUNK - w
                sp.dma_start(q[:, u], qr_d[:, :, ds(t, CHUNK)].rearrange("j p t -> p j t")).then_inc(ld[u], 16)
                sp.dma_start(k[:, u, :, META:META + w], k2_d[:, :, ds(w0, w)].rearrange("j p t -> p j t"))\
                    .then_inc(ld[u], 16)
                if later(i, 1):
                    sp.wait_ge(vt, i - 1)
                sp.dma_start(v[:, u, :, 0:w], vt_d[:, :, ds(w0, w)].rearrange("j p t -> p j t")).then_inc(ldv[u], 16)

            load(0, CHUNK, 0)
            for g, (t0, n) in enumerate(groups):
                for hh in range(2):
                    sp.dma_start(kk[HD * hh:HD * hh + HD, g, :, 0:n],
                                 k2_d.rearrange("(t hh) p n -> hh p t n", hh=2)[hh, 0:HD, :, t0:t0 + n]).then_inc(kvl, 16)
                sp.dma_start(vv[:, g, :, 0:n], vt_d[:, :, t0:t0 + n].rearrange("a p t -> p a t")).then_inc(kvl, 16)
            load(1, WINDOW, 1)
            sp.wait_ge(kve, 3)
            sp.wait_ge(vmz, 1)
            for un in range(NU):
                sp.dma_start(vm[META * un:META * un + META, un, :],
                             kv[0:META, 0, 1, (un % KVH) * HD:(un % KVH + 1) * HD]).then_inc(vml, 16)
            load(2, WINDOW, 0)
            nx.load(sp, 0)
            nx.load(sp, 1)
            with sp.Fori(1, NP // 2 - 1) as i:
                for u in range(2):
                    load(i * 2 + (u + 1), WINDOW, (u + 1) % 2)
            load(NP - 1, WINDOW, (NP - 1) % 2)
            for x, (m, w, d) in enumerate((("meta_k_p", "win_k_p", "win_k_s"), ("meta_v_p", "win_v_p", "win_v_s"))):
                sp.dma_start(a[m][0].rearrange("t h d -> t (h d)"), kv[0:META, 0, x, :]).then_inc(kvo, 16)
                sp.dma_start(a[w][0].rearrange("t h d -> t (h d)"), kv[:, 1, x, :]).then_inc(kvo, 16)
                for b in range(NB):
                    sp.dma_start(a[d][b, WINDOW - TS:WINDOW].rearrange("t h d -> t (h d)"),
                                 kv[TS * b:TS * b + TS, 2, x, :]).then_inc(kvo, 16)
            sp.wait_ge(kvo, 16 * 2 * (2 + NB))

        @block.gpsimd
        def _(pool):
            pool.memset(vm[:], 0.0).then_inc(vmz, 1)
            pool.wait_ge(kve, 3)
            for b in range(NB):
                for x, dst in enumerate((kct, vct)):
                    pool.dma_start(dst[CACHED:SK, b, :], kv[TS * b:TS * b + TS, 2, x, :]).then_inc(dln, 16)
            pool.wait_ge(cst, 64)
            for b in range(SB):
                for j in range(2):
                    pool.dma_start(sinks[R * b + j * TS:R * b + (j + 1) * TS], sink[j * CHUNK:j * CHUNK + TS])\
                        .then_inc(snk, 16)
            for u in range(2):
                nx.scale(pool, u)
                nx.split(pool, u)
            pool.wait_ge(dl, 16 * 5)
            pool.tensor_copy(qd[:].rearrange("p b j t -> p j b t"), qdl[:].rearrange("p j (b t) -> p j b t", t=TS))\
                .then_inc(qde, 1)

        @block.tensor
        def _(pe):
            def turn_new(pe):
                pe.wait_ge(kvl, 16 * 9)
                for g, (t0, n) in enumerate(groups):
                    for x, src in enumerate((kk, vv)):
                        for t in range(2):
                            y = pe.transpose(psum[0:n, 4 + g, (2 * x + t) * P:(2 * x + t + 1) * P], src[:, g, t, 0:n],
                                             ident[:])
                    y.then_inc(kvt, 1)
                pe.wait_ge(kve, 3)

            def scores(i, w, u, r):
                if later(i) and not decode(i - 1):
                    pe.wait_ge(ldv[1 - u], (r + u) * 16)
                    n = width(i - 1) - META
                    for t in range(2):
                        x = pe.transpose(psum[0:n, 6, (t + 1) * P:(t + 2) * P], v[:, 1 - u, t, 0:n], ident[:])
                    x.then_inc(vt, 1)
                if decode(i):
                    g = i - NP
                    if g == 0:
                        pe.wait_ge(qde, 1)
                        pe.wait_ge(ex, 2 * i)
                    for b in range(SB):
                        for un in range(NU):
                            kh, half = un % KVH, HD * (un // KVH)
                            x = pe.matmul(psum[R * b:R * b + R, 2 * g + un // 4, (un % 4) * SK:(un % 4 + 1) * SK],
                                          qd[half:half + HD, g * SB + b, 2 * kh:2 * kh + 2, :],
                                          ks[half:half + HD, g * SB + b, kh, :], start=True, stop=True)
                    x.then_inc(sc, 2)
                    return
                pe.wait_ge(ld[u], r * 32 + 32)
                if not later(i):
                    pe.wait_ge(kml, 32)
                for un in range(NU):
                    if later(i) and un % KVH == 0:
                        pe.wait_ge(ex, i * 2 + (un // KVH - 1) if un else i * 2 - 1)
                    kh, half = un % KVH, HD * (un // KVH)
                    ql = q[half:half + HD, u, 2 * kh:2 * kh + 2, :]
                    o = psum[:, un // 2, (un % 2) * (META + w):(un % 2 + 1) * (META + w)]
                    x = pe.matmul(o, ql, k[half:half + HD, u, kh, 0:META + w], start=True, stop=True)
                    if kh == KVH - 1:
                        x.then_inc(sc, 1)

            def values(i, w, u, r):
                dec = decode(i)
                pe.wait_ge(nrm, i + 1)
                if not dec:
                    pe.wait_ge(vws, i + 1)
                    pe.transpose(psum[:, 6, 0:P], pbm[:, u].rearrange("p u k -> p (u k)"), ident[:]).then_inc(pmd, 1)
                lo, n = (0, SK) if dec else (META, w)
                for un in range(NU):
                    x = pe.transpose(psum[0:n, 4 + un // 4, (un % 4) * P:(un % 4 + 1) * P],
                                     pb[:, u, un, lo:lo + n], ident[:])
                    if un % 4 == 3:
                        x.then_inc(ptd, 1)
                if not dec:
                    pe.wait_ge(pms, i + 1)
                if later(i):
                    pe.wait_ge(obs, i)
                else:
                    pe.wait_ge(vml, 16 * NU)
                for un in range(NU):
                    kh, half = un % KVH, HD * (un // KVH)
                    if kh == 0:
                        pe.wait_ge(pts, i * 2 + (1 + un // KVH))
                    if dec:
                        for b in range(SB):
                            x = pe.matmul(psum[half:half + HD, 7, kh * P + R * b:kh * P + R * b + R],
                                          vct[:, (i - NP) * SB + b, kh * HD:(kh + 1) * HD],
                                          pt[0:SK, un, R * b:R * b + R], start=True, stop=True)
                    else:
                        o = psum[half:half + HD, 7, kh * P:(kh + 1) * P]
                        pe.matmul(o, vw[0:w, kh * HD:(kh + 1) * HD], pt[0:w, un, :], start=True, stop=False)
                        x = pe.matmul(o, vm[:, un, :], pm[:], start=False, stop=True)
                x.then_inc(pv, 1)

            def turn_cached(pe):
                pe.wait_ge(dl, 16 * 5)
                pe.wait_ge(dln, 16 * 2 * NB)
                pe.wait_ge(vws, 4)
                for g in range(2):
                    for t in range(2):
                        if (g, t) == (1, 1):
                            pe.wait_ge(kse[1], 1)
                        for b in range(SB):
                            x = pe.transpose(psum[:, CACHED_BANK[g][t], b * SK:(b + 1) * SK],
                                             kct[:, g * SB + b, t * P:(t + 1) * P], ident[0:SK, 0:SK])
                    x.then_inc(kct_t, 1)
                for t in range(2):
                    pe.wait_ge(kse[t], 2)

            ahead(pe, scores, values, turn_cached, turn_new)

        def cached(eng, t, copy):
            for g in range(2):
                eng.wait_ge(kct_t, g + 1)
                for kh in (2 * t, 2 * t + 1):
                    for dup in range(2):
                        x = copy(ks[HD * dup:HD * dup + HD, g * SB:(g + 1) * SB, kh, :],
                                 psum[HD * (kh % 2):HD * (kh % 2) + HD, CACHED_BANK[g][t], 0:SB * SK]
                                 .rearrange("p (b k) -> p b k", k=SK))
                x.then_inc(kse[t], 1)

        def unit_scores(i, per):
            b = 0 if not decode(i) else 2 * (i - NP)
            return psum[:, b:b + NU // per, 0:per * width(i)].rearrange("p b (u k) -> p b u k", u=per)

        @block.scalar
        def _(act):
            for u in range(2):
                act.dma_start(k[:, u, :, 0:META], k2_d[:, :, 0:META].rearrange("h p t -> p h t")).then_inc(kml, 16)
            with nc.allow_non_contiguous_dma("sinks"):
                for j in range(2):
                    for half in range(2):
                        src = a["b_sinks"].rearrange("a (k j p) -> a k j p", j=2, p=2)[0:1, :, j, half]
                        u = slice(KVH * half, KVH * half + KVH)
                        act.dma_start(sink[j * CHUNK:(j + 1) * CHUNK, u], src.to_broadcast([CHUNK, KVH]))\
                            .then_inc(cst, 16)
            for dst, meta, win in ((kct, "cache_meta_k", "cache_win_k"), (vct, "cache_meta_v", "cache_win_v")):
                act.dma_start(dst[0:META], a[meta].rearrange("b t h d -> t b (h d)")).then_inc(dl, 16)
                act.dma_start(dst[META:CACHED], a[win][:, WINDOW - CHUNK:WINDOW].rearrange("b t h d -> t b (h d)"))\
                    .then_inc(dl, 16)
            act.dma_start(qdl[:], qr_d[:, :, T_S:T].rearrange("j p t -> p j t")).then_inc(dl, 16)

            def exponentials(i, w, u, r):
                act.wait_ge(neg, i + 1)
                if later(i, 1):
                    act.wait_ge(ptd, i * 2 - 2)
                    act.wait_ge(pmd, i - 1)
                per = 4 if decode(i) else 2
                src = unit_scores(i, per)
                for un in range(NU):
                    x = act.activation(pb[:, u, un, 0:width(i)], src[:, un // per, un % per, :], ACT.Exp,
                                       scale=SCORE_SCALE, bias=st[:, u, 2, un:un + 1], accum_out=st[:, u, 3, un:un + 1])
                    if un % KVH == KVH - 1:
                        x.then_inc(ex, 1)
                act.wait_ge(dsk, i + 1)
                act.activation(st[:, u, 5, :], st[:, u, 4, :], ACT.Exp).then_inc(es, 1)

            def store(i, w, u, r):
                act.wait_ge(pv, i + 1)
                if later(i, 1):
                    act.wait_ge(st_o[u], r * 16)
                if decode(i):
                    for kh in range(KVH):
                        x = act.activation(ob[:, u, 2 * kh:2 * kh + 2, :].rearrange("p j (s t) -> p s j t", s=SB),
                                           psum[:, 7, kh * P:(kh + 1) * P].rearrange("p (s j t) -> p s j t", s=SB, j=2),
                                           ACT.Copy)
                else:
                    x = act.activation(ob[:, u], psum[:, 7, :].rearrange("p (j t) -> p j t", j=KD), ACT.Copy)
                x.then_inc(obs, 1)
                act.wait_ge(obs, i + 1)
                if decode(i):
                    t, n = T_S + (i - NP) * CHUNK, SB * TS
                else:
                    t, n = (META + CHUNK * i if isinstance(i, int) else i * CHUNK + META), CHUNK
                act.dma_start(og_d[:, :, ds(t, n)].rearrange("j p t -> p j t"), ob[:, u]).then_inc(st_o[u], 16)

            ahead(act, exponentials, store,
                  lambda e: cached(e, 1, lambda o, x: e.activation(o, x, ACT.Copy)))
            for u in range(2):
                act.wait_ge(st_o[u], 16 * NSTEP // 2)

        @block.vector
        def _(dve):
            for g, (t0, n) in enumerate(groups):
                dve.wait_ge(kvt, g + 1)
                dve.tensor_copy(kv[0:n, g, :, :].rearrange("p x d -> p (x d)"), psum[0:n, 4 + g, :]).then_inc(kve, 1)
            dve.wait_ge(cst, 64)

            def maxima(i, u):
                sinks_row = sinks[:] if decode(i) else sink[:]
                if decode(i):
                    dve.wait_ge(snk, 16 * 2 * SB)
                per = 4 if decode(i) else 2
                out = st[:, u, 0, :].rearrange("p (b u) -> p b u", u=per)
                halves = 1 if decode(i) else 2
                m = NU // per // halves
                for x in range(halves):
                    dve.wait_ge(sc, i * 2 + (2 if decode(i) else x + 1))
                    y = dve.tensor_reduce(out[:, x * m:(x + 1) * m], unit_scores(i, per)[:, x * m:(x + 1) * m], AX_X,
                                          ALU.max)
                y.then_inc(mx, 1)
                dve.wait_ge(mx, i + 1)
                dve.scalar_tensor_tensor(st[:, u, 1, :], st[:, u, 0, :], SCORE_SCALE, sinks_row, ALU.mult, ALU.max)\
                    .then_inc(mxs, 1)
                dve.wait_ge(mxs, i + 1)
                dve.tensor_scalar(st[:, u, 2, :], st[:, u, 1, :], -1.0, None, ALU.mult).then_inc(neg, 1)
                dve.tensor_tensor(st[:, u, 4, :], sinks_row, st[:, u, 1, :], ALU.subtract).then_inc(dsk, 1)

            def normalise(i, u):
                dve.wait_ge(ex, i * 2 + 2)
                dve.wait_ge(es, i + 1)
                dve.tensor_tensor(st[:, u, 6, :], st[:, u, 3, :], st[:, u, 5, :], ALU.add).then_inc(den, 1)
                dve.wait_ge(den, i + 1)
                dve.reciprocal(st[:, u, 7, :], st[:, u, 6, :]).then_inc(rdn, 1)
                dve.wait_ge(rdn, i + 1)
                if later(i, 1) and not decode(i):
                    dve.wait_ge(pmd, i - 1)
                lo = 0 if decode(i) else META
                if not decode(i):
                    dve.tensor_tensor(pbm[:, u], pb[:, u, :, 0:META],
                                      st[:, u, 7, :].unsqueeze(2).to_broadcast([P, NU, META]), ALU.mult)
                p = pb[:, u, :, lo:width(i)]
                dve.tensor_tensor(p, p, st[:, u, 7, :].unsqueeze(2).to_broadcast([P, NU, width(i) - lo]), ALU.mult)\
                    .then_inc(nrm, 1)

            def first_part(i, w, u, r):
                if later(i):
                    normalise(i - 1, 1 - u)
                    if not decode(i - 1):
                        dve.wait_ge(vt, i)
                        if later(i, 1):
                            dve.wait_ge(pv, i - 1)
                        n = width(i - 1) - META
                        dve.tensor_copy(vw[0:n, :], psum[0:n, 6, P:3 * P]).then_inc(vws, 1)
                maxima(i, u)

            def second_part(i, w, u, r):
                n = SK if decode(i) else w
                if isinstance(i, int) and i == NSTEP - 1:
                    normalise(i, u)
                if later(i):
                    dve.wait_ge(pv, i)
                if not decode(i):
                    dve.wait_ge(pmd, i + 1)
                    dve.tensor_copy(pm[:], psum[:, 6, 0:P]).then_inc(pms, 1)
                for j in range(2):
                    dve.wait_ge(ptd, i * 2 + (j + 1))
                    dve.tensor_copy(pt[0:n, 4 * j:4 * j + 4, :],
                                    psum[0:n, 4 + j, :].rearrange("p (u r) -> p u r", u=4)).then_inc(pts, 1)

            ahead(dve, first_part, second_part, lambda e: cached(e, 0, e.tensor_copy))


def final(nc, a, s):
    at, sem, psum, ident, ones, h = s["at"], s["sem"], s["psum"], s["ident"], s["ones"], s["h"]
    gf, e = at("fi_gain", [P, D], F32, s["fixed_end"])
    y, e = at("fi_y", [P, 3, D], F32, e)
    junk, e = at("fi_junk", [P, 512], F32, e)
    ss, e = at("fi_sums", [P, 9, 5], F32, e)
    gl = sem("fi_gain_loaded")
    turned, sqr, tot, root, rs, ev = (sem("fi_" + x) for x in ("turned", "squares", "sum", "root", "rstd", "evac"))
    sto = [sem(f"fi_stored{i}") for i in range(3)]
    NT = (T - META) // P
    with nc.Block() as block:
        @block.sync
        def _(sp):
            sp.dma_start(gf[:], a["g_final"].rearrange("(a d) -> a d", a=1).to_broadcast([P, D])).then_inc(gl, 16)
            for i in range(NT):
                sp.wait_ge(ev, 2 * i + 2)
                dst = a["y_p"][0, i * P:(i + 1) * P, :] if i < NT - 1 else a["y_s"].rearrange("b t d -> (b t) d")
                sp.dma_start(dst, y[:, i % 3, :]).then_inc(sto[i % 3], 16)
            for b in range(3):
                sp.wait_ge(sto[b], 16 * (NT // 3))

        @block.tensor
        def _(pe):
            for i in range(NT):
                for half in range(2):
                    u = 2 * i + half
                    if i >= 4:
                        pe.wait_ge(ev, u - 7)
                    for k in range(4):
                        x = pe.transpose(psum[:, u % 8, k * P:(k + 1) * P],
                                         h[:, 4 * half + k, META + i * P:META + (i + 1) * P], ident[:])
                    x.then_inc(turned, 1)

        @block.scalar
        def _(act):
            for i in range(NT):
                for half in range(2):
                    u = 2 * i + half
                    act.wait_ge(turned, u + 1)
                    if u:
                        act.wait_ge(sqr, u)
                    act.activation(junk[:], psum[:, u % 8, :], ACT.Square, accum_out=ss[:, i, half:half + 1])\
                        .then_inc(sqr, 1)

        @block.gpsimd
        def _(pool):
            for i in range(NT):
                pool.wait_ge(root, i + 1)
                pool.tensor_tensor(ss[:, i, 4:5], ss[:, i, 3:4], s["powc"][:], ALU.pow).then_inc(rs, 1)

        @block.vector
        def _(dve):
            dve.wait_ge(gl, 16)

            def mean_square(i):
                dve.wait_ge(sqr, 2 * i + 2)
                dve.tensor_tensor(ss[:, i, 2:3], ss[:, i, 0:1], ss[:, i, 1:2], ALU.add).then_inc(tot, 1)
                dve.wait_ge(tot, i + 1)
                dve.tensor_scalar(ss[:, i, 3:4], ss[:, i, 2:3], 1.0 / D, EPS, ALU.mult, ALU.add).then_inc(root, 1)

            mean_square(0)
            for i in range(NT):
                if i + 1 < NT:
                    mean_square(i + 1)
                dve.wait_ge(rs, i + 1)
                if i >= 3:
                    dve.wait_ge(sto[i % 3], 16 * (i // 3))
                for half in range(2):
                    w = slice(512 * half, 512 * half + 512)
                    dve.scalar_tensor_tensor(y[:, i % 3, w], psum[:, (2 * i + half) % 8, :], ss[:, i, 4:5], gf[:, w],
                                             ALU.mult, ALU.mult).then_inc(ev, 1)


OUTS = [("y_p", (1, SEQ, D)), ("y_s", (NB, TS, D)),
        ("c_p", (1, 1, HA, DQK, DV)), ("n_p", (1, 1, HA, DQK)), ("m_p", (1, 1, HA)),
        ("meta_k_p", (1, META, KVH, HD)), ("meta_v_p", (1, META, KVH, HD)),
        ("win_k_p", (1, WINDOW, KVH, HD)), ("win_v_p", (1, WINDOW, KVH, HD)),
        ("c_s", (NB, 1, HA, DQK, DV)), ("n_s", (NB, 1, HA, DQK)), ("m_s", (NB, 1, HA)),
        ("win_k_s", (NB, WINDOW, KVH, HD)), ("win_v_s", (NB, WINDOW, KVH, HD))]


def rotary_tables():
    pos = np.concatenate([np.arange(T_S), np.tile(META + PAST + np.arange(TS), NB)]).astype(np.float32)
    half = HD // 2
    inv = (np.float32(10000.0) ** (-np.arange(half, dtype=np.float32) / np.float32(half))).astype(np.float32)
    ang = (pos[None, :] * inv[:, None]).astype(np.float32).astype(np.float64)
    cos, sin = np.cos(ang).astype(np.float32), np.sin(ang).astype(np.float32)
    return np.concatenate([cos] * 4), np.concatenate([-sin, sin] * 2)


def host_inputs(inputs):
    arrays = {n: np.ascontiguousarray(v) for n, v in inputs.items()}
    arrays["rope_cos"], arrays["rope_sin"] = rotary_tables()
    return arrays


def kernel(**inputs):
    import concourse.bacc as bacc
    from concourse.bass_utils import run_bass_kernel_spmd

    nc = bacc.Bacc("TRN2", target_bir_lowering=False, num_devices=1)
    arrays, aps = {}, {}
    for n, v in host_inputs(inputs).items():
        arrays["in_" + n] = v
        aps[n] = nc.dram_tensor("in_" + n, v.shape, mybir.dt.from_np(v.dtype), kind="ExternalInput").ap()
    for n, shape in OUTS:
        aps[n] = nc.dram_tensor(n, shape, F32, kind="ExternalOutput").ap()
    build(nc, aps)
    r = run_bass_kernel_spmd(nc, [arrays], core_ids=[0])
    return tuple(r.results[0][n] for n, _ in OUTS)
```
